# Optimizing a Trainium2 kernel written in Bass

```python
import math
import jax, jax.numpy as jnp
from jax import lax
import numpy as np

D_MODEL = 1024
BATCH = 1
SEQ = 256
DEPTH = 2

CTX_LEN = 256
GRID_W = 64
EPS = 1e-6
ROPE_BASE = 10000.0
Q_BLOCK = 128

MLA_HEADS = 4
MLA_Q_RANK = 256
MLA_KV_RANK = 128
MLA_NOPE_DIM = 128
MLA_ROPE_DIM = 64
MLA_V_DIM = 128

GLA_HEADS = 4
GLA_DK = 64
GLA_DV = 128
GLA_GATE_RANK = 16
GLA_TAU = 16.0
GLA_CHUNK = 64

DIFF_HEADS = 8
DIFF_DIM = 64

FFN_DIM = 2816
N_EXPERTS = 8
TOP_K = 2
EXPERT_DIM = 3584
MOE_BLOCK = 128

N_EVEN = (DEPTH + 1) // 2
N_ODD = DEPTH // 2

IN_A_SIZES = (MLA_Q_RANK, MLA_KV_RANK, MLA_ROPE_DIM,
              GLA_HEADS * GLA_DK, GLA_HEADS * GLA_DK, GLA_HEADS * GLA_DV, GLA_HEADS * GLA_DV,
              GLA_GATE_RANK, GLA_GATE_RANK)
IN_A_DIM = sum(IN_A_SIZES)
MIX_A_DIM = MLA_HEADS * MLA_V_DIM + GLA_HEADS * GLA_DV
MIX_C_DIM = DIFF_HEADS * 2 * DIFF_DIM

kernel_name = 'hybrid_mla_gla_diffattn_moe_dit'

def _rmsnorm(x, g):
    xf = x.astype(jnp.float32)
    y = xf * lax.rsqrt(jnp.mean(xf * xf, axis=-1, keepdims=True) + EPS)
    return (y * g.astype(jnp.float32)).astype(x.dtype)

def _axial_rope(n_tokens, rot_dim):
    rows = n_tokens // GRID_W
    row = jnp.repeat(jnp.arange(rows, dtype=jnp.float32), GRID_W)
    col = jnp.tile(jnp.arange(GRID_W, dtype=jnp.float32), rows)
    n_freq = rot_dim // 4
    freq = ROPE_BASE ** (-jnp.arange(n_freq, dtype=jnp.float32) / n_freq)
    ang = jnp.concatenate([row[:, None] * freq, col[:, None] * freq], axis=-1)
    return jnp.cos(ang), jnp.sin(ang)

def _apply_rope(x, cos, sin):
    half = x.shape[-1] // 2
    x1 = x[..., :half].astype(jnp.float32)
    x2 = x[..., half:].astype(jnp.float32)
    cs, sn = cos[None, :, None, :], sin[None, :, None, :]
    return jnp.concatenate([x1 * cs - x2 * sn, x2 * cs + x1 * sn], axis=-1).astype(x.dtype)

def _split_cols(p, sizes):
    return jnp.split(p, [int(o) for o in np.cumsum(sizes)[:-1]], axis=-1)

def _query_blocks(a):
    b, t = a.shape[:2]
    nb = t // Q_BLOCK
    return a.reshape((b, nb, Q_BLOCK) + a.shape[2:]).swapaxes(0, 1)

def _unblock(o):
    nb, b, qb = o.shape[:3]
    return o.swapaxes(0, 1).reshape((b, nb * qb) + o.shape[3:])

def _attend(q, k, v):
    scale = q.shape[-1] ** -0.5

    def one(qb):
        s = jnp.einsum('bqhd,bkhd->bhqk', qb, k, preferred_element_type=jnp.float32) * scale
        p = jax.nn.softmax(s, axis=-1)
        return jnp.einsum('bhqk,bkhd->bqhd', p.astype(v.dtype), v)

    return _unblock(lax.map(one, _query_blocks(q)))

def _diff_attend(q1, q2, k1, k2, v, lam):
    scale = q1.shape[-1] ** -0.5

    def one(args):
        a1, a2 = args
        s1 = jnp.einsum('bqhd,bkhd->bhqk', a1, k1, preferred_element_type=jnp.float32) * scale
        s2 = jnp.einsum('bqhd,bkhd->bhqk', a2, k2, preferred_element_type=jnp.float32) * scale
        p = jax.nn.softmax(s1, axis=-1) - lam * jax.nn.softmax(s2, axis=-1)
        return jnp.einsum('bhqk,bkhd->bqhd', p.astype(v.dtype), v)

    return _unblock(lax.map(one, (_query_blocks(q1), _query_blocks(q2))))

def _mla_qkv(c_q, c_kv, k_r, g_q, w_uq, g_kv, w_ukv, cos, sin):
    b, t, _ = c_q.shape
    q = (_rmsnorm(c_q, g_q) @ w_uq).reshape(b, t, MLA_HEADS, MLA_NOPE_DIM + MLA_ROPE_DIM)
    kv = (_rmsnorm(c_kv, g_kv) @ w_ukv).reshape(b, t, MLA_HEADS, MLA_NOPE_DIM + MLA_V_DIM)
    q_nope, q_rope = q[..., :MLA_NOPE_DIM], q[..., MLA_NOPE_DIM:]
    k_nope, v = kv[..., :MLA_NOPE_DIM], kv[..., MLA_NOPE_DIM:]
    k_rope = k_r[:, :, None, :]
    if cos is not None:
        q_rope = _apply_rope(q_rope, cos, sin)
        k_rope = _apply_rope(k_rope, cos, sin)
    q = jnp.concatenate([q_nope, q_rope], axis=-1)
    k = jnp.concatenate([k_nope, jnp.broadcast_to(k_rope, (b, t, MLA_HEADS, MLA_ROPE_DIM))], axis=-1)
    return q, k, v

def _gla_scan(q, k, v, log_a, s0):
    b, t, h, dk = q.shape
    dv = v.shape[-1]
    n = t // GLA_CHUNK

    def chunks(a):
        return a.astype(jnp.float32).reshape(b, n, GLA_CHUNK, h, a.shape[-1]).swapaxes(0, 1)

    mask = jnp.tril(jnp.ones((GLA_CHUNK, GLA_CHUNK), dtype=bool))[None, :, :, None, None]

    def step(state, inp):
        qc, kc, vc, lac = inp
        cum = jnp.cumsum(lac, axis=1)
        o_inter = jnp.einsum('bchk,bhkv->bchv', qc * jnp.exp(cum), state)
        rel = cum[:, :, None] - cum[:, None, :]
        decay = jnp.exp(jnp.where(mask, rel, -jnp.inf))
        att = jnp.einsum('bthk,btshk,bshk->bths', qc, decay, kc)
        o_intra = jnp.einsum('bths,bshv->bthv', att, vc)
        last = cum[:, -1]
        new_state = jnp.exp(last)[..., None] * state + jnp.einsum(
            'bshk,bshv->bhkv', kc * jnp.exp(last[:, None] - cum), vc)
        return new_state, o_inter + o_intra

    s_fin, o = lax.scan(step, s0.astype(jnp.float32), (chunks(q), chunks(k), chunks(v), chunks(log_a)))
    return o.swapaxes(0, 1).reshape(b, t, h, dv).astype(v.dtype), s_fin

def _gla_bidir(parts_l, parts_x, w_gf, b_gf, w_gb, b_gb, g_o, need_ctx):
    def prep(parts):
        q, k, v, r, af, ab = parts
        b, t, _ = q.shape
        q = q.reshape(b, t, GLA_HEADS, GLA_DK) * (GLA_DK ** -0.5)
        k = k.reshape(b, t, GLA_HEADS, GLA_DK)
        v = v.reshape(b, t, GLA_HEADS, GLA_DV)
        la_f = (jax.nn.log_sigmoid((af @ w_gf + b_gf).astype(jnp.float32)) / GLA_TAU).reshape(b, t, GLA_HEADS, GLA_DK)
        la_b = (jax.nn.log_sigmoid((ab @ w_gb + b_gb).astype(jnp.float32)) / GLA_TAU).reshape(b, t, GLA_HEADS, GLA_DK)
        return q, k, v, r, la_f, la_b

    ql, kl, vl, rl, lfl, lbl = prep(parts_l)
    qx, kx, vx, rx, lfx, lbx = prep(parts_x)
    flip = lambda a: jnp.flip(a, axis=1)
    s0 = jnp.zeros((ql.shape[0], GLA_HEADS, GLA_DK, GLA_DV), jnp.float32)
    ox_f, sx_f = _gla_scan(qx, kx, vx, lfx, s0)
    ox_b, sx_b = _gla_scan(flip(qx), flip(kx), flip(vx), flip(lbx), s0)
    ol_f, _ = _gla_scan(ql, kl, vl, lfl, sx_f)
    ol_b, _ = _gla_scan(flip(ql), flip(kl), flip(vl), flip(lbl), sx_b)

    def finish(o, r):
        b, t = o.shape[:2]
        gate = jax.nn.silu(r.reshape(b, t, GLA_HEADS, GLA_DV))
        return (_rmsnorm(o, g_o) * gate).reshape(b, t, GLA_HEADS * GLA_DV)

    out_l = finish(ol_f + flip(ol_b), rl)
    out_x = finish(ox_f + flip(ox_b), rx) if need_ctx else None
    return out_l, out_x

def _mixer_mla_gla(h, hx, w_in, g_q, w_uq, g_kv, w_ukv, w_gf, b_gf, w_gb, b_gb, g_o, w_out,
                   cos, sin, need_ctx):
    b, t, _ = h.shape
    parts = _split_cols(h @ w_in, IN_A_SIZES)
    parts_x = _split_cols(hx @ w_in, IN_A_SIZES)
    q_l, k_l, v_l = _mla_qkv(parts[0], parts[1], parts[2], g_q, w_uq, g_kv, w_ukv, cos, sin)
    q_x, k_x, v_x = _mla_qkv(parts_x[0], parts_x[1], parts_x[2], g_q, w_uq, g_kv, w_ukv, None, None)
    a_l = _attend(q_l, jnp.concatenate([k_x, k_l], axis=1), jnp.concatenate([v_x, v_l], axis=1))
    g_l, g_x = _gla_bidir(parts[3:], parts_x[3:], w_gf, b_gf, w_gb, b_gb, g_o, need_ctx)
    y = jnp.concatenate([a_l.reshape(b, t, MLA_HEADS * MLA_V_DIM), g_l], axis=-1) @ w_out
    yx = None
    if need_ctx:
        a_x = _attend(q_x, k_x, v_x)
        bx, tx = hx.shape[:2]
        yx = jnp.concatenate([a_x.reshape(bx, tx, MLA_HEADS * MLA_V_DIM), g_x], axis=-1) @ w_out
    return y, yx

def _diff_qkv(h, w_qkv, cos, sin):
    b, t, _ = h.shape
    q, k, v = jnp.split(h @ w_qkv, 3, axis=-1)
    q = q.reshape(b, t, 2 * DIFF_HEADS, DIFF_DIM)
    k = k.reshape(b, t, 2 * DIFF_HEADS, DIFF_DIM)
    if cos is not None:
        q = _apply_rope(q, cos, sin)
        k = _apply_rope(k, cos, sin)
    q = q.reshape(b, t, DIFF_HEADS, 2, DIFF_DIM)
    k = k.reshape(b, t, DIFF_HEADS, 2, DIFF_DIM)
    v = v.reshape(b, t, DIFF_HEADS, 2 * DIFF_DIM)
    return q[..., 0, :], q[..., 1, :], k[..., 0, :], k[..., 1, :], v

def _mixer_diff(h, hx, w_qkv, lq1, lk1, lq2, lk2, g_o, w_out, lam_init, cos, sin, need_ctx):
    f32 = jnp.float32
    lam = (jnp.exp(jnp.sum(lq1.astype(f32) * lk1.astype(f32)))
           - jnp.exp(jnp.sum(lq2.astype(f32) * lk2.astype(f32))) + lam_init)
    q1, q2, k1, k2, v = _diff_qkv(h, w_qkv, cos, sin)
    q1x, q2x, k1x, k2x, vx = _diff_qkv(hx, w_qkv, None, None)
    cat = lambda a, b_: jnp.concatenate([a, b_], axis=1)

    def finish(o):
        b, t = o.shape[:2]
        return (_rmsnorm(o, g_o) * (1.0 - lam_init)).reshape(b, t, MIX_C_DIM) @ w_out

    y = finish(_diff_attend(q1, q2, cat(k1x, k1), cat(k2x, k2), cat(vx, v), lam))
    yx = finish(_diff_attend(q1x, q2x, k1x, k2x, vx, lam)) if need_ctx else None
    return y, yx

def _swiglu(h, w_gate, w_up, w_down):
    return (jax.nn.silu(h @ w_gate) * (h @ w_up)) @ w_down

def _moe_swiglu(h, w_router, w_gate, w_up, w_down):
    n, d = h.shape
    logits = jnp.dot(h, w_router, preferred_element_type=jnp.float32)
    top_val, top_idx = lax.top_k(logits, TOP_K)
    gates = jax.nn.softmax(top_val, axis=-1)
    flat_e = top_idx.reshape(-1)
    flat_t = jnp.repeat(jnp.arange(n, dtype=jnp.int32), TOP_K)
    flat_g = gates.reshape(-1)
    order = jnp.argsort(flat_e, stable=True)
    e_s, t_s, g_s = flat_e[order], flat_t[order], flat_g[order]
    sizes = jnp.bincount(flat_e, length=N_EXPERTS)
    padded = (sizes + MOE_BLOCK - 1) // MOE_BLOCK * MOE_BLOCK
    start = jnp.cumsum(sizes) - sizes
    pend = jnp.cumsum(padded)
    pstart = pend - padded
    dest = pstart[e_s] + (jnp.arange(n * TOP_K) - start[e_s])
    cap = -(-(n * TOP_K) // MOE_BLOCK) * MOE_BLOCK + N_EXPERTS * MOE_BLOCK
    nb = cap // MOE_BLOCK
    buf_t = jnp.zeros((cap,), jnp.int32).at[dest].set(t_s)
    buf_g = jnp.zeros((cap,), jnp.float32).at[dest].set(g_s)
    blk_e = jnp.minimum(jnp.searchsorted(pend, jnp.arange(nb) * MOE_BLOCK, side='right'), N_EXPERTS - 1)
    xs = h[buf_t].reshape(nb, MOE_BLOCK, d)

    def expert_block(args):
        xb, e = args
        return (jax.nn.silu(xb @ w_gate[e]) * (xb @ w_up[e])) @ w_down[e]

    ys = lax.map(expert_block, (xs, blk_e)).reshape(cap, d)
    return jnp.zeros_like(h).at[buf_t].add(ys * buf_g[:, None].astype(h.dtype))

def setup_inputs(seed: int = 0) -> dict:
    key = jax.random.key(seed)
    ks = iter(jax.random.split(key, 48))
    D = D_MODEL

    def nrm(shape, scale):
        return scale * jax.random.normal(next(ks), shape, jnp.float32)

    def gain(shape):
        return 1.0 + nrm(shape, 0.05)

    return {
        'x': nrm((BATCH, SEQ, D), 1.0),
        'c': nrm((BATCH, D), 1.0),
        'ctx': nrm((BATCH, CTX_LEN, D), 1.0),
        'c_ctx': nrm((D,), 1.0),
        'w_mod': nrm((DEPTH, D, 6 * D), D ** -0.5),
        'b_mod': nrm((DEPTH, 6 * D), 0.02),
        'g_pre_mix': gain((DEPTH, D)),
        'g_post_mix': gain((DEPTH, D)),
        'g_pre_ffn': gain((DEPTH, D)),
        'g_post_ffn': gain((DEPTH, D)),
        'w_in_a': nrm((N_EVEN, D, IN_A_DIM), D ** -0.5),
        'mla_g_q': gain((N_EVEN, MLA_Q_RANK)),
        'mla_w_uq': nrm((N_EVEN, MLA_Q_RANK, MLA_HEADS * (MLA_NOPE_DIM + MLA_ROPE_DIM)), MLA_Q_RANK ** -0.5),
        'mla_g_kv': gain((N_EVEN, MLA_KV_RANK)),
        'mla_w_ukv': nrm((N_EVEN, MLA_KV_RANK, MLA_HEADS * (MLA_NOPE_DIM + MLA_V_DIM)), MLA_KV_RANK ** -0.5),
        'gla_w_gate_f': nrm((N_EVEN, GLA_GATE_RANK, GLA_HEADS * GLA_DK), GLA_GATE_RANK ** -0.5),
        'gla_b_gate_f': nrm((N_EVEN, GLA_HEADS * GLA_DK), 0.1),
        'gla_w_gate_b': nrm((N_EVEN, GLA_GATE_RANK, GLA_HEADS * GLA_DK), GLA_GATE_RANK ** -0.5),
        'gla_b_gate_b': nrm((N_EVEN, GLA_HEADS * GLA_DK), 0.1),
        'gla_g_out': gain((N_EVEN, GLA_DV)),
        'w_out_a': nrm((N_EVEN, MIX_A_DIM, D), MIX_A_DIM ** -0.5),
        'w_qkv_c': nrm((N_ODD, D, 3 * MIX_C_DIM), D ** -0.5),
        'diff_lq1': nrm((N_ODD, DIFF_DIM), 0.1),
        'diff_lk1': nrm((N_ODD, DIFF_DIM), 0.1),
        'diff_lq2': nrm((N_ODD, DIFF_DIM), 0.1),
        'diff_lk2': nrm((N_ODD, DIFF_DIM), 0.1),
        'diff_g_out': gain((N_ODD, 2 * DIFF_DIM)),
        'w_out_c': nrm((N_ODD, MIX_C_DIM, D), MIX_C_DIM ** -0.5),
        'ffn_w_gate': nrm((N_EVEN, D, FFN_DIM), D ** -0.5),
        'ffn_w_up': nrm((N_EVEN, D, FFN_DIM), D ** -0.5),
        'ffn_w_down': nrm((N_EVEN, FFN_DIM, D), FFN_DIM ** -0.5),
        'moe_w_router': nrm((N_ODD, D, N_EXPERTS), D ** -0.5),
        'moe_w_gate': nrm((N_ODD, N_EXPERTS, D, EXPERT_DIM), D ** -0.5),
        'moe_w_up': nrm((N_ODD, N_EXPERTS, D, EXPERT_DIM), D ** -0.5),
        'moe_w_down': nrm((N_ODD, N_EXPERTS, EXPERT_DIM, D), EXPERT_DIM ** -0.5),
    }

def reference(x, c, ctx, c_ctx, w_mod, b_mod, g_pre_mix, g_post_mix, g_pre_ffn, g_post_ffn,
              w_in_a, mla_g_q, mla_w_uq, mla_g_kv, mla_w_ukv,
              gla_w_gate_f, gla_b_gate_f, gla_w_gate_b, gla_b_gate_b, gla_g_out, w_out_a,
              w_qkv_c, diff_lq1, diff_lk1, diff_lq2, diff_lk2, diff_g_out, w_out_c,
              ffn_w_gate, ffn_w_up, ffn_w_down,
              moe_w_router, moe_w_gate, moe_w_up, moe_w_down):
    b, t, d = x.shape
    cos_a, sin_a = _axial_rope(t, MLA_ROPE_DIM)
    cos_c, sin_c = _axial_rope(t, DIFF_DIM)
    silu_c = jax.nn.silu(c)[:, None, :]
    silu_cx = jax.nn.silu(c_ctx)

    for i in range(DEPTH):
        last = i == DEPTH - 1
        j = i // 2
        mod = jnp.split(silu_c @ w_mod[i] + b_mod[i], 6, axis=-1)
        modx = jnp.split(silu_cx @ w_mod[i] + b_mod[i], 6, axis=-1)

        h = _rmsnorm(x, g_pre_mix[i]) * (1.0 + mod[1]) + mod[0]
        hx = _rmsnorm(ctx, g_pre_mix[i]) * (1.0 + modx[1]) + modx[0]
        if i % 2 == 0:
            y, yx = _mixer_mla_gla(h, hx, w_in_a[j], mla_g_q[j], mla_w_uq[j], mla_g_kv[j], mla_w_ukv[j],
                                   gla_w_gate_f[j], gla_b_gate_f[j], gla_w_gate_b[j], gla_b_gate_b[j],
                                   gla_g_out[j], w_out_a[j], cos_a, sin_a, not last)
        else:
            lam_init = 0.8 - 0.6 * math.exp(-0.3 * i)
            y, yx = _mixer_diff(h, hx, w_qkv_c[j], diff_lq1[j], diff_lk1[j], diff_lq2[j], diff_lk2[j],
                                diff_g_out[j], w_out_c[j], lam_init, cos_c, sin_c, not last)
        x = x + mod[2] * _rmsnorm(y, g_post_mix[i])
        if not last:
            ctx = ctx + modx[2] * _rmsnorm(yx, g_post_mix[i])

        h = _rmsnorm(x, g_pre_ffn[i]) * (1.0 + mod[4]) + mod[3]
        if i % 2 == 0:
            f = _swiglu(h, ffn_w_gate[j], ffn_w_up[j], ffn_w_down[j])
        else:
            f = _moe_swiglu(h.reshape(-1, d), moe_w_router[j], moe_w_gate[j], moe_w_up[j],
                            moe_w_down[j]).reshape(b, t, d)
        x = x + mod[5] * _rmsnorm(f, g_post_ffn[i])
        if not last:
            hx = _rmsnorm(ctx, g_pre_ffn[i]) * (1.0 + modx[4]) + modx[3]
            if i % 2 == 0:
                fx = _swiglu(hx, ffn_w_gate[j], ffn_w_up[j], ffn_w_down[j])
            else:
                fx = _moe_swiglu(hx.reshape(-1, d), moe_w_router[j], moe_w_gate[j], moe_w_up[j],
                                 moe_w_down[j]).reshape(ctx.shape)
            ctx = ctx + modx[5] * _rmsnorm(fx, g_post_ffn[i])
    return x


_drawn_inputs = setup_inputs


def setup_inputs(seed=0):
    import zlib

    import numpy as np

    out = dict(_drawn_inputs(seed))
    spreads = {}
    factors = {}
    for name, (base, spread) in spreads.items():
        noise = np.random.default_rng([zlib.crc32(name.encode()), seed]).standard_normal(out[name].shape)
        drawn = base * np.exp(spread * noise) if base else spread * noise
        out[name] = __import__('jax').numpy.asarray(drawn.astype(out[name].dtype))
    for name, factor in factors.items():
        out[name] = (out[name] * factor).astype(out[name].dtype)
    return out
```

```python
import math
from contextlib import ExitStack

import numpy as np
import concourse.bass as bass
from concourse import mybir

D, T_CTX, T_LAT = 1024, 256, 256
T = T_CTX + T_LAT
KT = D // 128
TT = T // 128
EPS = 1e-6
MLA_H, Q_RANK, KV_RANK, NOPE, ROPE, VD = 4, 256, 128, 128, 64, 128
MLA_SCALE = (NOPE + ROPE) ** -0.5
GLA_H, DK, DV, RANK, TAU, CHUNK = 4, 64, 128, 16, 16.0, 64
N_CHUNKS = T // CHUNK
LEVELS = [32, 16, 8, 4, 2, 1]
DIFF_H, DIFF_D = 8, 64
DIFF_SCALE = DIFF_D ** -0.5
LAM_INIT = 0.8 - 0.6 * math.exp(-0.3)
FFN = 2816
FT = FFN // 128
E, EF = 8, 3584
EC = EF // 512
GRID_W, ROPE_BASE = 64, 10000.0
COLS_A = dict(cq=0, ckv=256, kr=384, gq=448, gk=704, gv=960, gr=1472, af=1984, ab=2000)
IN_A = 2016

SLOTS, PIECE = 7, 2048
SPLITS = 3
BANKS = 8


def columns(*widths):
    at, out = 0, {}
    for name, width in widths:
        out[name] = (at, at + width)
        at += width
    return out, at


CONST, CONST_W = columns(
    ("ident", 128), ("ones", 128), ("tri_f", 128), ("tri_b", 128), ("before", 128), ("rot", 128),
    ("cos", 256), ("sin", 256), ("masks", 12 * 128), ("diag2", 128), ("iota", 128), ("lower8", 64))
PARAM, PARAM_W = columns(
    ("c", 16), ("g_pre_mix", 16), ("g_post_mix", 16), ("g_pre_ffn", 16), ("g_post_ffn", 16),
    ("b_mod", 96), ("g_q", 2), ("g_kv", 1), ("g_gla", 1), ("g_diff", 1),
    ("lq1", 64), ("lk1", 64), ("lq2", 64), ("lk2", 64), ("router", 64), ("w_gate", 512), ("b_gate", 512))


def plan():
    pieces, where, tiles = [], {}, []

    def linear(label, src, index, rows, c0, c1, last):
        kmax = PIECE // (c1 - c0)
        n = -(-rows // kmax)
        step = -(-rows // n)
        where[label] = []
        for k0 in range(0, rows, step):
            k1 = min(k0 + step, rows)
            where[label].append((len(pieces), k0, k1, c1 - c0))
            pieces.append((src, index, k0, k1, c0, c1, last))

    def mod(layer, chunks):
        for n in chunks:
            linear(("mod", layer, n), "w_mod", layer, KT, 512 * n, 512 * n + 512, ("mod", layer, n))
            tiles.append(("mod", layer, n))
            if n:
                tiles.append(("modT", layer, n - 1))
        if n == 11:
            tiles.append(("modT", layer, n))

    mod(0, range(12))
    tiles.append(("ss", 0))
    linear("in_a0", "w_in_a", 0, KT, 0, 448, "kr")
    linear("in_a1", "w_in_a", 0, KT, 448, 960, ("gk", 1))
    linear("gv", "w_in_a", 0, KT, 960, 1472, ("gv", 3))
    linear("gr", "w_in_a", 0, KT, 1472, 1984, ("gr", 3))
    linear("gaf", "w_in_a", 0, KT, 1984, 2016, "ab")
    tiles.extend([("cq", 0), ("cq", 1), "ckv", "kr", ("gq", 0), ("gq", 1), "ssq", "sskv", ("gk", 0), ("gk", 1)])
    tiles.extend(("gv", t) for t in range(TT))
    tiles.extend(("gr", m) for m in range(4))
    tiles.extend(["af", "ab"])
    linear("uq", "mla_w_uq", 0, 2, 0, 768, ("qr", 1))
    linear("ukv", "mla_w_ukv", 0, 1, 0, 1024, ("v", 3))
    tiles.extend(("qn", h) for h in range(4))
    tiles.extend(("qr", p) for p in range(2))
    tiles.extend(("kn", h) for h in range(4))
    tiles.extend(("v", t) for t in range(TT))
    tiles.extend([("rotq", 0), ("rotq", 1), "rotk"])
    tiles.extend(("gx", t) for t in range(TT))
    tiles.extend(x for x in mla_steps())
    tiles.extend(("cum", d, k) for d in range(2) for k in range(2))
    tiles.extend(("att", "diag", h) for h in range(4))
    tiles.extend(("kT", d, t) for d in range(2) for t in range(TT))
    tiles.extend(("att", (d, lv), h) for d in range(2) for lv in range(6) for h in range(4))
    tiles.extend(("U", d, p, r) for d in range(2) for p in range(2) for r in range(2))
    tiles.extend(("og", h) for h in range(4))
    tiles.extend(("ssg", h) for h in range(4))
    for n in range(2):
        linear(("out_a", n), "w_out_a", 0, KT, 512 * n, 512 * n + 512, ("ya", 4 * n + 3))
    tiles.extend(("ya", m) for m in range(8))
    mod(1, range(0, 4))
    tiles.append(("ss", 1))
    mod(1, range(4, 8))
    tiles.append(("ss", 2))
    for n in range(6):
        c1 = min(512 * n + 512, FFN)
        m1 = c1 // 128 - 1
        linear(("fg", n), "ffn_w_gate", 0, KT, 512 * n, c1, ("u", m1))
        linear(("fu", n), "ffn_w_up", 0, KT, 512 * n, c1, ("u", m1))
    for m in range(FT):
        tiles.extend([("g", m), ("u", m)])
    for m in range(8):
        linear(("fd", m), "ffn_w_down", 0, FT, 128 * m, 128 * m + 128, ("yf", m))
        tiles.append(("yf", m))
    mod(1, range(8, 12))
    tiles.append(("ss", 3))
    tiles.append(("ss", 4))
    for n in range(4):
        linear(("qk", n), "w_qkv_c", 0, KT, 512 * n, 512 * n + 512, ("qk", 4 * n + 3))
    for n in range(2):
        linear(("v1", n), "w_qkv_c", 0, KT, 2048 + 512 * n, 2560 + 512 * n, ("v1", 3, n))
    tiles.extend(("qk", m) for m in range(16))
    tiles.extend(("v1", t, n) for n in range(2) for t in range(TT))
    tiles.extend(("rot", m) for m in range(8))
    tiles.extend(x for x in diff_steps())
    for n in range(2):
        linear(("out_c", n), "w_out_c", 0, KT, 512 * n, 512 * n + 512, ("yc", 4 * n + 3))
    tiles.extend(("ssd", h) for h in range(8))
    tiles.extend(("yc", m) for m in range(8))
    tiles.extend([("ss", 5), ("ss", 6)])
    tiles.extend([("lg", 0), ("lg", 1)])
    tiles.extend(("ht", t, n) for t in range(2) for n in range(2))
    tiles.extend([("pos", 0), ("pos", 1), "cnt"])
    return pieces, where, {name: i for i, name in enumerate(tiles)}


def pipelined(scores, probs, outs, units):
    steps = []
    for u in range(2):
        steps += scores(u)
    for u in range(units):
        if u + 2 < units:
            steps += scores(u + 2)
        if u % 2 == 0 and u:
            steps.append(outs(u // 2 - 1))
        steps.append(probs(u))
    steps.append(outs(units // 2 - 1))
    return steps


def mla_steps():
    return pipelined(lambda u: [("s", u)], lambda u: ("pT", u), lambda g: ("o", g), MLA_H * TT)


def diff_steps():
    return pipelined(lambda u: [("s1", u), ("s2", u)], lambda u: ("dT", u), lambda g: ("do", g), DIFF_H * 2)


def expert_order():
    steps, at = [], 0
    for c in range(EC):
        for kind in "gu":
            steps.append((kind, c, at))
            at += 2
        if c:
            steps.append(("d", c - 1, at))
            at += 2
    steps.append(("d", EC - 1, at))
    return steps


PER_EXPERT = 6 * EC


def piece_of(kind, c):
    return next(j for k, cc, j in expert_order() if (k, cc) == (kind, c))

def vector_order():
    after = {}
    for c in range(EC):
        after.setdefault(min(piece_of("u", c) + 3, PER_EXPERT - 1), []).append(("hidden", c))
    for c in range(EC - 1):
        after.setdefault(piece_of("u", c + 1) + 1, []).insert(0, ("transposed", c))
    after.setdefault(PER_EXPERT - 1, []).append(("transposed", EC - 1))
    steps = []
    for q in range(PER_EXPERT):
        steps.append(("split", q))
        steps += after.get(q, [])
    return steps


def build(nc, stream, const_dram, param_dram, x_dram, out_dram):
    f32, f32r, i32, u32 = mybir.dt.float32, mybir.dt.float32r, mybir.dt.int32, mybir.dt.uint32
    ALU, ACT, AX = mybir.AluOpType, mybir.ActivationFunctionType, mybir.AxisListType
    pieces, where, tile_no = plan()
    n_pre = len(pieces)

    ctx = ExitStack()
    with ctx:
        def sb(name, width, dt=f32):
            return ctx.enter_context(nc.sbuf_tensor(name, [128, width], dt))

        A_ = sb("AREA", 9216 + 2 * SPLITS * PIECE)
        area_end = nc.sbuf_base
        X_ = sb("X", KT * T)
        H_ = sb("H", KT * T)
        RAW = sb("RAW", SLOTS * PIECE)
        C = sb("CONST", CONST_W)
        PR = sb("PARAM", PARAM_W)
        MOD_ = sb("MOD", 2 * 48 * 2)
        COEF_ = sb("COEF", 2 * 4 * 16)
        SC_ = sb("SC", 16)
        SMALL = sb("SMALL", 64)
        STAT = sb("STAT", 96)
        MROW = sb("MROW", 512)
        RST = sb("RST", T)
        TMP = sb("TMP", T)
        FLAG = sb("FLAG", 1, i32)
        XH, XL = sb("XH", KT * 128, f32r), sb("XL", KT * 128, f32r)
        HI = nc.alloc_sbuf_tensor_at("W_HI", [128, SPLITS * PIECE], f32r, offset=area_end - 8 * SPLITS * PIECE)
        LO = nc.alloc_sbuf_tensor_at("W_LO", [128, SPLITS * PIECE], f32r, offset=area_end - 4 * SPLITS * PIECE)
        HTH = nc.alloc_sbuf_tensor_at("HTH", [128, 512], f32r, offset=area_end - 8 * SPLITS * PIECE - 4096)
        HTL = nc.alloc_sbuf_tensor_at("HTL", [128, 512], f32r, offset=area_end - 8 * SPLITS * PIECE - 2048)
        PS = ctx.enter_context(nc.psum_tensor("PS", [128, BANKS, 512], f32))

        def view(t, start, *shape):
            n = int(np.prod(shape))
            v = t[:, start:start + n]
            if len(shape) == 2:
                v = v.rearrange("p (a b) -> p a b", b=shape[1])
            if len(shape) == 3:
                v = v.rearrange("p (a b c) -> p a b c", b=shape[1], c=shape[2])
            return v

        X, H = view(X_, 0, KT, T), view(H_, 0, KT, T)
        MOD = view(MOD_, 0, 2 * 48, 2)
        SC = view(SC_, 0, KT, 2)
        COEF = view(COEF_, 0, 8, 8, 2)

        def const(name):
            return C[:, CONST[name][0]:CONST[name][1]]

        def param(name, a=0, b=None):
            s, e = PARAM[name]
            return PR[:, s + a:(e if b is None else s + b)]

        IDENT, ONES, ROT = const("ident"), const("ones"), const("rot")

        GQ, GK = view(A_, 0, 2, T), view(A_, 1024, 2, T)
        GV, GR = view(A_, 2048, TT, 512), view(A_, 4096, 4, T)
        LX = view(A_, 6144, TT, 512)
        m0 = 8192
        CQ, CKV, KR = view(A_, m0, 2, T), A_[:, m0 + 1024:m0 + 1536], A_[:, m0 + 1536:m0 + 2048]
        QN, KN = view(A_, m0 + 2048, 4, T), view(A_, m0 + 4096, 4, T)
        QR, V = view(A_, m0 + 6144, 2, T), view(A_, m0 + 7168, TT, 512)
        PB = view(A_, m0 + 9216, 3, 512)
        PT = view(A_, m0 + 10752, 2, 4, 256)
        AF = view(A_, m0 + 10752, 2, T)
        LE = view(A_, m0 + 2048, TT, 512)
        SQ0 = view(A_, 0, KT, T)
        SQM = view(A_, m0 + 9216, 3, T)
        CUM = view(A_, m0, 4, T)
        EX, AA = view(A_, m0 + 2048, 2, 2 * T), view(A_, m0 + 4096, 2, 2 * T)
        ATT = view(A_, m0 + 6144, 4, T)
        KHT = view(A_, m0 + 8192, 8, 256)
        g0 = m0 + 10240
        STATES = (view(H_, 4 * T, 16, 128), view(A_, m0, 16, 128))
        QH = view(A_, g0, 4, T)
        YO = view(A_, 0, KT, T)
        SQY = view(A_, 4096, KT, T)
        FF = view(A_, 8192, FT, T)
        K1 = view(A_, 0, 8, T)
        Q1 = view(A_, 4096, 8, 256)
        V1 = view(A_, 6144, TT, D)
        E1 = view(A_, 10240, 3, 512)
        E2 = view(A_, 11776, 3, 512)
        PT1 = view(A_, 13312, 2, 4, 256)
        OD = view(A_, 15360, 8, 256)
        SQD = view(A_, 17408, 8, 256)
        YO1 = view(A_, 0, KT, 256)
        SQ1 = view(A_, 2048, KT, 256)
        HTOK = view(A_, 0, 2, D)
        PG = view(A_, 2048, 2, E, 128)
        GT = view(A_, 4096, E, 256)
        YS = A_[:, 6144:7168]
        HS = A_[:, 7168:7680]
        RT = A_[:, 7680:8192]
        PSEL = view(H_, 0, 2 * E, 128)
        ACC = view(H_, 2048, KT, 256)

        made = {}

        def sem(name):
            if name not in made:
                made[name] = ctx.enter_context(nc.semaphore(name))
            return made[name]

        loaded = [sem(f"weights_loaded_{s}") for s in range(SLOTS)]
        drained = [sem(f"bank_{b}_drained") for b in range(BANKS)]
        written = sem("tiles_written")

        def bank(name):
            return PS[:, tile_no[name] % BANKS, :]

        def wait_written(eng, name):
            eng.wait_ge(written, tile_no[name] + 1)

        def wait_drained(eng, name):
            eng.wait_ge(drained[tile_no[name] % BANKS], tile_no[name] // BANKS + 1)

        def drained_by(ins, name):
            ins.then_inc(drained[tile_no[name] % BANKS], 1)

        def slot(n):
            return RAW[:, n % SLOTS * PIECE:(n % SLOTS + 1) * PIECE]

        def wait_piece(eng, n):
            eng.wait_ge(loaded[n % SLOTS], 16 * (n // SLOTS + 1))

        def weight(label, kt):
            for n, k0, k1, cols in where[label]:
                if k0 <= kt < k1:
                    return slot(n)[:, (kt - k0) * cols:(kt - k0 + 1) * cols]

        def wait_weight(eng, label, kt):
            for n, k0, k1, cols in where[label]:
                if k0 == kt:
                    wait_piece(eng, n)

        has_state = {(0, c): c > 0 for c in range(8)} | {(1, c): c != 3 for c in range(8)}
        chunk_order = [list(range(8)), [3, 2, 1, 0, 7, 6, 5, 4]]

        def state(d, p, c):
            return STATES[d][:, p * 8 + c, :]

        block = ctx.enter_context(nc.Block())

        @block.sync
        def _(sp):
            sp.dma_start(PR[:], param_dram).then_inc(sem("param_loaded"), 16)
            for n, (_, _, k0, k1, c0, c1, _) in enumerate(pieces):
                if n >= SLOTS:
                    wait_written(sp, pieces[n - SLOTS][6])
                w = (k1 - k0) * (c1 - c0)
                sp.dma_start(slot(n)[:, 0:w], stream[n, :, 0:w]).then_inc(loaded[n % SLOTS], 16)

            def expert_pieces(k):
                def load(n, free):
                    for s in range(SLOTS):
                        free(s)
                        q = (n_pre + s) % SLOTS
                        sp.dma_start(slot(q), stream[n + s]).then_inc(loaded[q], 16)

                total = E * PER_EXPERT
                if k == 0:
                    load(n_pre, lambda s: wait_written(sp, pieces[n_pre - SLOTS + s][6]))
                with sp.Fori(1 if k == 0 else 0, total // SLOTS) as i:
                    def split(s):
                        sp.wait_ge(sem("hi_made"), SLOTS * i + (k * total + s - SLOTS + 1))
                        sp.wait_ge(sem("lo_made"), SLOTS * i + (k * total + s - SLOTS + 1))
                    load(n_pre + SLOTS * i, split)

            expert_pieces(0)
            sp.wait_ge(sem("flag_ready"), 1)
            flag = sp.value_load(FLAG[0:1, 0:1], min_val=0, max_val=1)
            with sp.If(flag > 0):
                expert_pieces(1)
            sp.wait_ge(sem("out_ready"), 8)
            sp.dma_start(out_dram.rearrange("(k p) t -> p k t", p=128), X[:, :, T_CTX:T]).then_inc(sem("out_stored"), 16)
            sp.wait_ge(sem("out_stored"), 16)

        @block.tensor
        def _(pe):
            def claim(name):
                n = tile_no[name]
                if n >= BANKS:
                    pe.wait_ge(drained[n % BANKS], n // BANKS)
                return PS[:, n % BANKS, :]

            def done(ins, name):
                written_so_far[0] += 1
                assert tile_no[name] + 1 == written_so_far[0], name
                ins.then_inc(written, 1)

            written_so_far = [0]

            def mm(out, lhsT, rhs, start, stop):
                return nc.tensor.matmul(out, lhsT, rhs, start=start, stop=stop)

            def linear(name, label, cols, rhs, n, first, rows=KT, ready=None):
                b = claim(name)
                for kt in range(rows):
                    if first:
                        wait_weight(pe, label, kt)
                    if ready is not None:
                        ready(kt)
                    w = weight(label, kt)[:, cols[0]:cols[1]]
                    i = mm(b[0:cols[1] - cols[0], 0:n], w, rhs(kt), kt == 0, kt == rows - 1)
                done(i, name)

            def mod(layer, chunks):
                def rows(n):
                    wait_drained(pe, ("mod", layer, n))
                    b = claim(("modT", layer, n))
                    for j in range(4):
                        i = nc.tensor.transpose(b[:, 2 * j:2 * j + 2], MROW[0:2, 128 * j:128 * j + 128],
                                                IDENT[0:2, 0:2])
                    done(i, ("modT", layer, n))

                for n in chunks:
                    b = claim(("mod", layer, n))
                    for kt in range(KT):
                        wait_weight(pe, ("mod", layer, n), kt)
                        i = mm(b[0:2, :], SC[:, kt, :], weight(("mod", layer, n), kt), kt == 0, kt == KT - 1)
                    done(i, ("mod", layer, n))
                    if n:
                        rows(n - 1)
                if n == 11:
                    rows(n)

            def sum_squares(name, sq, n, tiles, ready):
                b = claim(name)
                for k in range(tiles):
                    ready(k)
                    i = mm(b[:, 0:n], ONES, sq(k), k == 0, k == tiles - 1)
                done(i, name)

            def norm_sum(i, sq, n):
                sum_squares(("ss", i), sq, n, KT,
                            lambda k: pe.wait_ge(sem("squares"), 4 * i + k // 2 + 1) if k % 2 == 0 else None)

            pe.wait_ge(sem("silu_c"), 1)
            pe.wait_ge(sem("const_loaded"), 16)
            mod(0, range(12))
            norm_sum(0, lambda k: SQ0[:, k, :], T)

            def h_ready(stage):
                def ready(kt):
                    pe.wait_ge(sem("h_ready"), KT * stage + kt + 1)
                return ready

            hx = lambda kt: H[:, kt, :]
            hl = lambda kt: H[:, kt, T_CTX:T]
            linear(("cq", 0), "in_a0", (0, 128), hx, T, True, ready=h_ready(0))
            linear(("cq", 1), "in_a0", (128, 256), hx, T, False)
            linear("ckv", "in_a0", (256, 384), hx, T, False)
            linear("kr", "in_a0", (384, 448), hx, T, False)
            for m in range(2):
                linear(("gq", m), "in_a1", (128 * m, 128 * m + 128), hx, T, m == 0)
            sum_squares("ssq", lambda k: SQM[:, k, :], T, 2, lambda k: pe.wait_ge(sem("mla_squares"), k + 1))
            sum_squares("sskv", lambda k: SQM[:, 2, :], T, 1, lambda k: pe.wait_ge(sem("mla_squares"), 3))
            for m in range(2):
                linear(("gk", m), "in_a1", (256 + 128 * m, 384 + 128 * m), hx, T, False)

            def token_major(name, t, label, cols, src, first, rows=KT):
                b = claim(name)
                for kt in range(rows):
                    if first:
                        wait_weight(pe, label, kt)
                    i = mm(b[:, 0:cols[1] - cols[0]], src(kt)[:, 128 * t:128 * t + 128],
                           weight(label, kt)[:, cols[0]:cols[1]], kt == 0, kt == rows - 1)
                done(i, name)

            for t in range(TT):
                token_major(("gv", t), t, "gv", (0, 512), hx, t == 0)
            for m in range(4):
                linear(("gr", m), "gr", (128 * m, 128 * m + 128), hx, T, m == 0)
            linear("af", "gaf", (0, 16), hx, T, True)
            linear("ab", "gaf", (16, 32), hx, T, False)

            pe.wait_ge(sem("lora_normed"), 3)
            for h in range(MLA_H):
                linear(("qn", h), "uq", (128 * h, 128 * h + 128), lambda k: CQ[:, k, :], T, h == 0, rows=2)
            for p in range(2):
                linear(("qr", p), "uq", (512 + 128 * p, 640 + 128 * p), lambda k: CQ[:, k, :], T, False, rows=2)
            for h in range(MLA_H):
                linear(("kn", h), "ukv", (256 * h, 256 * h + 128), lambda k: CKV, T, h == 0, rows=1)
            for t in range(TT):
                b = claim(("v", t))
                w = weight("ukv", 0).rearrange("p (h c) -> p h c", c=256)[:, :, 128:256]
                done(mm(b, CKV[:, 128 * t:128 * t + 128], w, True, True), ("v", t))
            for p in range(2):
                wait_drained(pe, ("qr", p))
                b = claim(("rotq", p))
                done(mm(b[:, 0:256], ROT, QR[:, p, T_CTX:T], True, True), ("rotq", p))
            wait_drained(pe, "kr")
            b = claim("rotk")
            done(mm(b[:, 0:256], ROT, KR[:, T_CTX:T], True, True), "rotk")

            wait_drained(pe, "af")
            wait_drained(pe, "ab")
            for t in range(TT):
                b = claim(("gx", t))
                for d in range(2):
                    i = mm(b[:, 256 * d:256 * d + 256], AF[0:16, d, 128 * t:128 * t + 128],
                           param("w_gate", 256 * d, 256 * d + 256)[0:16, :], True, True)
                done(i, ("gx", t))

            for h in range(MLA_H):
                wait_drained(pe, ("kn", h))
                wait_drained(pe, ("qn", h))
            for t in range(TT):
                wait_drained(pe, ("v", t))
            pe.wait_ge(sem("mla_roped"), 3)
            for kind, u in mla_steps():
                if kind == "s":
                    h, q, keys = u // TT, u % TT, (2 if u % TT < 2 else 4) * 128
                    r = 64 * (h % 2)
                    b = claim(("s", u))
                    mm(b[:, 0:keys], QN[:, h, 128 * q:128 * q + 128], KN[:, h, 0:keys], True, False)
                    done(mm(b[:, 0:keys], QR[r:r + 64, h // 2, 128 * q:128 * q + 128], KR[r:r + 64, 0:keys],
                            False, True), ("s", u))
                elif kind == "pT":
                    pe.wait_ge(sem("probs"), u + 1)
                    b = claim(("pT", u))
                    for k in range(2 if u % TT < 2 else 4):
                        i = nc.tensor.transpose(b[:, 128 * k:128 * k + 128], PB[:, u % 3, 128 * k:128 * k + 128], IDENT)
                    done(i, ("pT", u))
                else:
                    wait_drained(pe, ("pT", 2 * u))
                    wait_drained(pe, ("pT", 2 * u + 1))
                    b = claim(("o", u))
                    kts = 2 if u % 2 == 0 else 4
                    for k in range(kts):
                        i = mm(b[:, 0:256], V[:, k, 128 * (u // 2):128 * (u // 2) + 128], PT[:, u % 2, k, :],
                               k == 0, k == kts - 1)
                    done(i, ("o", u))

            pe.wait_ge(sem("log_decays"), 1)
            for d in range(2):
                for k in range(2):
                    b = claim(("cum", d, k))
                    for t in range(TT):
                        i = mm(b[:, 128 * t:128 * t + 128], LX[:, t, 256 * d + 128 * k:256 * d + 128 * k + 128],
                               const(("tri_f", "tri_b")[d]), True, True)
                    done(i, ("cum", d, k))

            def pairs(name, lhs, rhs):
                h = name[2]
                r = 64 * (h % 2)
                b = claim(name)
                for t in range(TT):
                    c = slice(T * (h // 2) + 128 * t, T * (h // 2) + 128 * t + 128)
                    i = mm(b[:, 128 * t:128 * t + 128], lhs[r:r + 64, c], rhs[r:r + 64, c], True, True)
                done(i, name)

            gq, gk = A_[:, 0:1024], A_[:, 1024:2048]
            for m in range(2):
                wait_drained(pe, ("gq", m))
                wait_drained(pe, ("gk", m))
            for h in range(GLA_H):
                pairs(("att", "diag", h), gk, gq)
            for d in range(2):
                pe.wait_ge(sem("decayed_keys"), d + 1)
                for t in range(TT):
                    b = claim(("kT", d, t))
                    for k in range(2):
                        i = nc.tensor.transpose(b[:, 128 * k:128 * k + 128],
                                                AA[:, d, T * k + 128 * t:T * k + 128 * t + 128], IDENT)
                    done(i, ("kT", d, t))
            for d in range(2):
                for lv in range(6):
                    pe.wait_ge(sem("level_ready"), 6 * d + lv + 1)
                    for h in range(GLA_H):
                        a = AA[:, lv % 2, :]
                        pairs(("att", (d, lv), h), a, a)
            for d in range(2):
                for t in range(TT):
                    wait_drained(pe, ("kT", d, t))
            for d in range(2):
                for p in range(2):
                    for r in range(2):
                        b = claim(("U", d, p, r))
                        for t in range(TT):
                            for hh in range(2):
                                i = mm(b[64 * hh:64 * hh + 64, 128 * t:128 * t + 128],
                                       KHT[64 * r:64 * r + 64, TT * d + t, 128 * p + 64 * hh:128 * p + 64 * hh + 64],
                                       GV[64 * r:64 * r + 64, t, 128 * (2 * p + hh):128 * (2 * p + hh) + 128],
                                       True, True)
                        done(i, ("U", d, p, r))
            for h in range(GLA_H):
                wait_drained(pe, ("att", (1, 5), h))
            pe.wait_ge(sem("decayed_queries"), 2)
            for h in range(GLA_H):
                p, r = h // 2, 64 * (h % 2)
                b = claim(("og", h))
                for d in range(2):
                    for r2 in range(2):
                        wait_drained(pe, ("U", d, p, r2))
                for t in range(TT):
                    mms = [(slice(128 * t, 128 * t + 128), GV[:, t, 128 * h:128 * h + 128],
                            ATT[:, h, 128 * t:128 * t + 128])]
                    for c in (2 * t, 2 * t + 1):
                        for d in range(2):
                            if has_state[d, c]:
                                mms.append((slice(64 * c, 64 * c + 64), state(d, p, c)[r:r + 64, :],
                                            QH[r:r + 64, 2 * d + p, 64 * c:64 * c + 64]))
                    for j, (cols, a, w) in enumerate(mms):
                        i = nc.tensor.matmul(b[:, cols], a, w, start=j == 0, stop=j == len(mms) - 1,
                                             skip_group_check=True)
                done(i, ("og", h))
            for h in range(GLA_H):
                sum_squares(("ssg", h), lambda k: EX[:, h // 2, T * (h % 2):T * (h % 2) + T], T, 1,
                            lambda k: pe.wait_ge(sem("gla_squares"), h + 1))

            for m in range(8):
                def y_ready(kt):
                    if kt < 4:
                        wait_drained(pe, ("o", 2 * kt + 1))
                    else:
                        pe.wait_ge(sem("gla_out"), kt - 3)
                linear(("ya", m), ("out_a", m // 4), (128 * (m % 4), 128 * (m % 4) + 128), hx, T, m % 4 == 0,
                       ready=y_ready if m == 0 else None)
            mod(1, range(0, 4))
            norm_sum(1, lambda k: SQY[:, k, :], T)
            mod(1, range(4, 8))
            norm_sum(2, lambda k: SQY[:, k, :], T)
            for m in range(FT):
                c = (128 * (m % 4), 128 * (m % 4) + 128)
                linear(("g", m), ("fg", m // 4), c, hx, T, m % 4 == 0, ready=h_ready(1) if m == 0 else None)
                linear(("u", m), ("fu", m // 4), c, hx, T, m % 4 == 0)
            for m in range(8):
                linear(("yf", m), ("fd", m), (0, 128), lambda k: FF[:, k, :], T, True, rows=FT,
                       ready=(lambda k: wait_drained(pe, ("u", k))) if m == 0 else None)
            mod(1, range(8, 12))
            norm_sum(3, lambda k: SQY[:, k, :], T)

            norm_sum(4, lambda k: SQY[:, k, :], T)
            for m in range(16):
                c = (128 * (m % 4), 128 * (m % 4) + 128)
                linear(("qk", m), ("qk", m // 4), c, hl if m < 8 else hx, 256 if m < 8 else T, m % 4 == 0,
                       ready=h_ready(2) if m == 0 else None)
            for n in range(2):
                for t in range(TT):
                    token_major(("v1", t, n), t, ("v1", n), (0, 512), hx, t == 0)
            for m in range(8):
                wait_drained(pe, ("qk", m))
                wait_drained(pe, ("qk", 8 + m))
                b = claim(("rot", m))
                mm(b[:, 0:256], ROT, Q1[:, m, :], True, True)
                done(mm(b[:, 256:512], ROT, K1[:, m, T_CTX:T], True, True), ("rot", m))
            for n in range(2):
                for t in range(TT):
                    wait_drained(pe, ("v1", t, n))
            for kind, u in diff_steps():
                if kind in ("s1", "s2"):
                    h, q = u // 2, u % 2
                    r = 0 if kind == "s1" else 64
                    pe.wait_ge(sem("diff_roped"), h + 1)
                    b = claim((kind, u))
                    done(mm(b, Q1[r:r + 64, h, 128 * q:128 * q + 128], K1[r:r + 64, h, :], True, True), (kind, u))
                elif kind == "dT":
                    pe.wait_ge(sem("diff_probs"), u + 1)
                    b = claim(("dT", u))
                    for k in range(TT):
                        i = nc.tensor.transpose(b[:, 128 * k:128 * k + 128], E1[:, u % 3, 128 * k:128 * k + 128], IDENT)
                    done(i, ("dT", u))
                else:
                    wait_drained(pe, ("dT", 2 * u))
                    wait_drained(pe, ("dT", 2 * u + 1))
                    b = claim(("do", u))
                    for k in range(TT):
                        i = mm(b[:, 0:256], V1[:, k, 128 * u:128 * u + 128], PT1[:, u % 2, k, :], k == 0, k == 3)
                    done(i, ("do", u))
            for h in range(DIFF_H):
                sum_squares(("ssd", h), lambda k: SQD[:, h, :], 256, 1,
                            lambda k: pe.wait_ge(sem("diff_squares"), h + 1))
            for m in range(8):
                linear(("yc", m), ("out_c", m // 4), (128 * (m % 4), 128 * (m % 4) + 128), hl, 256, m % 4 == 0,
                       ready=(lambda k: pe.wait_ge(sem("diff_out"), k + 1)) if m == 0 else None)
            norm_sum(5, lambda k: SQ1[:, k, :], 256)
            norm_sum(6, lambda k: SQ1[:, k, :], 256)

            for t in range(2):
                b = claim(("lg", t))
                for kt in range(KT):
                    if t == 0:
                        h_ready(3)(kt)
                    i = mm(b[:, 0:E], H[:, kt, T_CTX + 128 * t:T_CTX + 128 * t + 128],
                           param("router", 8 * kt, 8 * kt + 8), kt == 0, kt == KT - 1)
                done(i, ("lg", t))
            for t in range(2):
                for n in range(2):
                    b = claim(("ht", t, n))
                    for j in range(4):
                        i = nc.tensor.transpose(b[:, 128 * j:128 * j + 128],
                                                H[:, 4 * n + j, T_CTX + 128 * t:T_CTX + 128 * t + 128], IDENT)
                    done(i, ("ht", t, n))
            pe.wait_ge(sem("selected"), 1)
            sel = lambda t: RT[:, 64 + 8 * t:72 + 8 * t]
            b = claim(("pos", 0))
            done(mm(b[:, 0:E], const("before"), sel(0), True, True), ("pos", 0))
            b = claim(("pos", 1))
            mm(b[:, 0:E], const("before"), sel(1), True, False)
            done(mm(b[:, 0:E], ONES, sel(0), False, True), ("pos", 1))
            b = claim("cnt")
            mm(b[:, 0:E], ONES, sel(0), True, False)
            done(mm(b[:, 0:E], ONES, sel(1), False, True), "cnt")
            for t in range(2):
                for n in range(2):
                    wait_drained(pe, ("ht", t, n))
            wait_drained(pe, ("pos", 1))
            wait_drained(pe, "cnt")

            def three(out, a, b, first, last):
                mm(out, a[0], b[0], first, False)
                mm(out, a[0], b[1], False, False)
                return mm(out, a[1], b[0], False, last)

            def expert_pass(k):
                pe.wait_ge(sem("acc_done"), 4 * E * k + 1)
                for j in range(4):
                    pe.wait_ge(sem("onehots"), 4 * k + j + 1)
                    for i2 in range(2):
                        for t in range(2):
                            at = 256 * i2 + 128 * t
                            i = nc.tensor.transpose(PS[:, j, at:at + 128], PG[:, t, 2 * j + i2, :], IDENT)
                    i.then_inc(sem("gt_written"), 1)
                pe.wait_ge(sem("gt_copied"), 4 * k + 4)
                with pe.Fori(0, E) as e:
                    E_ = e + E * k
                    for kt in range(KT):
                        for t in range(2):
                            i = mm(PS[:, 4 + kt // 4, 128 * (kt % 4):128 * (kt % 4) + 128],
                                   HTOK[:, t, 128 * kt:128 * kt + 128], PSEL[:, E * t + e, :], t == 0, t == 1)
                    i.then_inc(sem("gathered"), 1)
                    pe.wait_ge(sem("x_lo"), E_ + 1)
                    pe.wait_ge(sem("acc_done"), 4 * E_ + 1)
                    for kind, c, j in expert_order():
                        if kind == "u" and c:
                            transpose_hidden(E_, c - 1)
                        if kind == "d" and c == EC - 1:
                            transpose_hidden(E_, c)
                        if kind == "d":
                            pe.wait_ge(sem("ht_lo"), EC * E_ + c + 1)
                        for half in range(2):
                            q = j + half
                            s = slice(q % SPLITS * PIECE, (q % SPLITS + 1) * PIECE)
                            pe.wait_ge(sem("lo_made"), PER_EXPERT * E_ + q + 1)
                            if kind in "gu":
                                b = PS[:, 2 * (c % 2) + (kind == "u"), :]
                                for i in range(4):
                                    kt = 4 * half + i
                                    cols = slice(128 * kt, 128 * kt + 128)
                                    w = slice(s.start + 512 * i, s.start + 512 * i + 512)
                                    last = three(b, (XH[:, cols], XL[:, cols]), (HI[:, w], LO[:, w]),
                                                 kt == 0, kt == KT - 1)
                            else:
                                for i in range(2):
                                    ft = 2 * half + i
                                    cols = slice(128 * ft, 128 * ft + 128)
                                    for n in range(2):
                                        w = slice(s.start + 1024 * i + 512 * n, s.start + 1024 * i + 512 * n + 512)
                                        last = three(PS[:, 6 + n, :], (HTH[:, cols], HTL[:, cols]), (HI[:, w], LO[:, w]),
                                                     c == 0 and ft == 0, c == EC - 1 and ft == 3)
                            last.then_inc(sem("piece_used"), 1)
                    pe.wait_ge(sem("y_copied"), E_ + 1)
                    for kt in range(KT):
                        i = mm(PS[:, kt // 2, 256 * (kt % 2):256 * (kt % 2) + 256], YS[:, 128 * kt:128 * kt + 128],
                               GT[:, e, :], True, True)
                        if kt % 2:
                            i.then_inc(sem("scattered"), 1)

            def transpose_hidden(E_, c):
                pe.wait_ge(sem("hidden"), EC * E_ + c + 1)
                for j in range(4):
                    i = nc.tensor.transpose(PS[:, 4, 128 * j:128 * j + 128], HS[:, 128 * j:128 * j + 128], IDENT)
                i.then_inc(sem("hidden_T"), 1)

            expert_pass(0)
            pe.wait_ge(sem("flag_ready"), 1)
            flag = pe.value_load(FLAG[0:1, 0:1], min_val=0, max_val=1)
            with pe.If(flag > 0):
                expert_pass(1)
            pe.wait_ge(sem("moe_squares"), 1)
            for kt in range(KT):
                i = mm(PS[:, 5, 0:256], ONES, view(A_, 2048, KT, 256)[:, kt, :], kt == 0, kt == KT - 1)
            i.then_inc(sem("moe_sum"), 1)

        @block.scalar
        def _(act):
            count = {}

            def act_do(name, out, in_, func, **kw):
                count[name] = count.get(name, 0) + 1
                nc.scalar.activation(out, in_, func, **kw).then_inc(sem(name), 1)
                act.wait_ge(sem(name), count[name])

            act.dma_start(C[:], const_dram).then_inc(sem("const_loaded"), 16)
            act.dma_start(X, x_dram.rearrange("(k p) t -> p k t", p=128)).then_inc(sem("x_loaded"), 16)
            act.wait_ge(sem("param_loaded"), 16)
            nc.scalar.activation(SC_[:], param("c"), ACT.Silu).then_inc(sem("silu_c"), 1)

            def mod(layer, chunks):
                for n in chunks:
                    wait_written(act, ("mod", layer, n))
                    if n or layer:
                        wait_written(act, ("modT", layer, n - 1) if n else ("modT", 0, 11))
                    drained_by(nc.scalar.activation(MROW[0:2, :], bank(("mod", layer, n))[0:2, :], ACT.Copy),
                               ("mod", layer, n))

            def root(out, n):
                k = 5 + (D, Q_RANK, 2 * DIFF_D).index(n)
                nc.scalar.activation(out, out, ACT.Sqrt, bias=SMALL[:, k:k + 1]).then_inc(sem("rooted"), 1)

            def root_of(name, n, w):
                wait_written(act, name)
                root(bank(name)[:, 0:w], n)

            def squares(src, dst, lo, hi, ready=None):
                for j in range(4):
                    if ready is not None:
                        ready(j)
                    nc.scalar.activation(dst[:, 2 * j:2 * j + 2, :], src[:, 2 * j:2 * j + 2, lo:hi],
                                         ACT.Square).then_inc(sem("squares"), 1)

            def modulate(layer, which, stage, streams):
                act.wait_ge(sem("coefs"), layer + 1)
                seg = 0 if which == 0 else 3
                for kt in range(KT):
                    if kt % 2 == 0:
                        act.wait_ge(sem("x_scaled"), 4 * stage + kt // 2 + 1)
                    for s in streams:
                        h = H[:, kt, 256 * s:256 * s + 256]
                        i = nc.scalar.activation(h, h, ACT.Identity, scale=COEF[:, 4 * layer + which, kt, s:s + 1],
                                                 bias=MOD[:, 48 * layer + 8 * seg + kt, s:s + 1])
                    i.then_inc(sem("h_ready"), 1)

            def copy_out(name, dst, src=None, func=ACT.Copy, **kw):
                wait_written(act, name)
                drained_by(nc.scalar.activation(dst, bank(name) if src is None else src, func, **kw), name)

            act.wait_ge(sem("x_loaded"), 16)
            squares(X, SQ0, 0, T)
            mod(0, range(12))
            act.wait_ge(sem("eps_ready"), 3)
            root_of(("ss", 0), D, T)
            modulate(0, 0, 0, (0, 1))

            copy_out(("cq", 0), CQ[:, 0, :])
            copy_out(("cq", 1), CQ[:, 1, :])
            copy_out("ckv", CKV)
            wait_written(act, "kr")
            nc.scalar.activation(KR[0:64, :], bank("kr")[0:64, :], ACT.Copy)
            drained_by(nc.scalar.activation(KR[64:128, :], bank("kr")[0:64, :], ACT.Copy), "kr")
            for m, src in enumerate((CQ[:, 0, :], CQ[:, 1, :], CKV)):
                wait_drained(act, (("cq", 0), ("cq", 1), "ckv")[m])
                nc.scalar.activation(SQM[:, m, :], src, ACT.Square).then_inc(sem("mla_squares"), 1)
            for m in range(2):
                copy_out(("gq", m), GQ[:, m, :], scale=DK ** -0.5)
            root_of("ssq", Q_RANK, T)
            root_of("sskv", KV_RANK, T)
            for m in range(2):
                copy_out(("gk", m), GK[:, m, :])
            for t in range(TT):
                copy_out(("gv", t), GV[:, t, :])
            for m in range(4):
                copy_out(("gr", m), GR[:, m, :], func=ACT.Silu)
            for h in range(MLA_H):
                copy_out(("qn", h), QN[:, h, :])
            for h in range(MLA_H):
                copy_out(("kn", h), KN[:, h, :])

            def attend(steps):
                for kind, u in steps:
                    if kind == "s":
                        keys = (2 if u % TT < 2 else 4) * 128
                        act.wait_ge(sem("mla_max"), u + 1)
                        if u >= 3:
                            wait_written(act, ("pT", u - 3))
                        drained_by(nc.scalar.activation(PB[:, u % 3, 0:keys], bank(("s", u))[:, 0:keys], ACT.Exp,
                                                        bias=STAT[:, u:u + 1], scale=MLA_SCALE,
                                                        accum_out=STAT[:, 32 + u:33 + u]), ("s", u))
                    elif kind == "pT":
                        n = 2 if u % TT < 2 else 4
                        g, q = u // 2, u % 2
                        if g >= 2:
                            wait_written(act, ("o", g - 2))
                        copy_out(("pT", u), PT[:, g % 2, 0:n, 128 * q:128 * q + 128],
                                 bank(("pT", u))[:, 0:128 * n].rearrange("p (k q) -> p k q", q=128))
                    elif kind in ("s1", "s2"):
                        j = kind == "s2"
                        act.wait_ge(sem("diff_max"), 2 * u + j + 1)
                        if u >= 3:
                            wait_written(act, ("dT", u - 3))
                        drained_by(nc.scalar.activation((E2 if j else E1)[:, u % 3, :], bank((kind, u)), ACT.Exp,
                                                        bias=STAT[:, 16 * j + u:16 * j + u + 1], scale=DIFF_SCALE,
                                                        accum_out=STAT[:, 32 + 16 * j + u:33 + 16 * j + u]), (kind, u))
                    elif kind == "dT":
                        g, q = u // 2, u % 2
                        if g >= 2:
                            wait_written(act, ("do", g - 2))
                        copy_out(("dT", u), PT1[:, g % 2, :, 128 * q:128 * q + 128],
                                 bank(("dT", u)).rearrange("p (k q) -> p k q", q=128))
                    elif kind == "do":
                        wait_written(act, ("do", u))
                        nc.scalar.activation(SQD[:, u, :], bank(("do", u))[:, 0:256],
                                             ACT.Square).then_inc(sem("diff_squares"), 1)

            attend(mla_steps())

            act.wait_ge(sem("gate_abs"), 1)
            act_do("act_gate", LE, LE, ACT.Exp)
            act.wait_ge(sem("gate_plus"), 1)
            act_do("act_gate", LE, LE, ACT.Ln)
            for d in range(2):
                for k in range(2):
                    copy_out(("cum", d, k), CUM[:, 2 * d + k, :])
            for d in range(2):
                for k in range(2):
                    wait_drained(act, ("cum", d, k))
                nc.scalar.activation(QH[:, 2 * d:2 * d + 2, :], CUM[:, 2 * d:2 * d + 2, :],
                                     ACT.Exp).then_inc(sem("decay_exp"), 1)
                act.wait_ge(sem("key_exponents"), d + 1)
                nc.scalar.activation(EX[:, d, :], EX[:, d, :], ACT.Exp).then_inc(sem("key_exp"), 1)
                edge = 63 if d == 0 else 0
                nc.scalar.activation(STAT[:, 64 + 16 * d:80 + 16 * d].rearrange("p (k c) -> p k c", c=8),
                                     CUM[:, 2 * d:2 * d + 2, edge::CHUNK], ACT.Exp).then_inc(sem("chunk_decay"), 1)
            for t in range(2 * TT):
                name = ("kT", t // TT, t % TT)
                copy_out(name, KHT[:, t, :], bank(name)[:, 0:256])
            for n in range(12):
                act.wait_ge(sem("level_exponents"), n + 1)
                nc.scalar.activation(EX[:, n % 2, :], EX[:, n % 2, :], ACT.Exp).then_inc(sem("level_exp"), 1)
            for h in range(GLA_H):
                wait_written(act, ("og", h))
                nc.scalar.activation(EX[:, h // 2, T * (h % 2):T * (h % 2) + T], bank(("og", h)),
                                     ACT.Square).then_inc(sem("gla_squares"), 1)
            for h in range(GLA_H):
                root_of(("ssg", h), DV, T)

            for m in range(8):
                copy_out(("ya", m), YO[:, m, :])
            for m in range(8):
                wait_drained(act, ("ya", m))
            squares(YO, SQY, 0, T)
            mod(1, range(0, 4))
            root_of(("ss", 1), D, T)

            def x_ready(base):
                return lambda j: act.wait_ge(sem("x_ready"), base + 2 * j + 2)

            squares(X, SQY, 0, T, x_ready(0))
            mod(1, range(4, 8))
            root_of(("ss", 2), D, T)
            modulate(0, 2, 1, (0, 1))
            for m in range(FT):
                wait_written(act, ("g", m))
                drained_by(nc.scalar.activation(FF[:, m, :], bank(("g", m)), ACT.Silu), ("g", m))
            for m in range(8):
                copy_out(("yf", m), YO[:, m, :])
            for m in range(8):
                wait_drained(act, ("yf", m))
            squares(YO, SQY, 0, T)
            mod(1, range(8, 12))
            root_of(("ss", 3), D, T)
            squares(X, SQY, 0, T, x_ready(8))
            root_of(("ss", 4), D, T)
            modulate(1, 0, 2, (0, 1))
            for m in range(16):
                if m < 8:
                    copy_out(("qk", m), Q1[:, m, :], bank(("qk", m))[:, 0:256])
                else:
                    copy_out(("qk", m), K1[:, m - 8, :])
            act.wait_ge(sem("lam_logits"), 1)
            act_do("lam_exp", SMALL[:, 8:10], SMALL[:, 8:10], ACT.Exp)
            attend(diff_steps())
            for h in range(DIFF_H):
                root_of(("ssd", h), 2 * DIFF_D, 256)
            for m in range(8):
                copy_out(("yc", m), YO1[:, m, :], bank(("yc", m))[:, 0:256])
            for m in range(8):
                wait_drained(act, ("yc", m))
            squares(YO1, SQ1, 0, 256)
            root_of(("ss", 5), D, 256)
            squares(X, SQ1, T_CTX, T, x_ready(16))
            root_of(("ss", 6), D, 256)
            modulate(1, 2, 3, (1,))
            for t in range(2):
                for n in range(2):
                    copy_out(("ht", t, n), HTOK[:, t, 512 * n:512 * n + 512])
            act.wait_ge(sem("gate_logits"), 1)
            act_do("gate_exp", RT[:, 40:42], RT[:, 40:42], ACT.Exp)

            def expert_pass(k):
                for j in range(4):
                    act.wait_ge(sem("gt_written"), 4 * k + j + 1)
                    nc.scalar.activation(GT[:, 2 * j:2 * j + 2, :].rearrange("p e t -> p (e t)"), PS[:, j, :],
                                         ACT.Copy).then_inc(sem("gt_copied"), 1)
                with act.Fori(0, E) as e:
                    E_ = e + E * k

                    def split(q):
                        n = n_pre + q
                        act.wait_ge(loaded[n % SLOTS], 16 * (6 * E_ + (n // SLOTS + 1)))
                        if q >= SPLITS:
                            act.wait_ge(sem("piece_used"), PER_EXPERT * E_ + (q - SPLITS + 1))
                        nc.scalar.activation(HI[:, q % SPLITS * PIECE:(q % SPLITS + 1) * PIECE], slot(n),
                                             ACT.Copy).then_inc(sem("hi_made"), 1)

                    split(0)
                    split(1)
                    act.wait_ge(sem("gathered"), E_ + 1)
                    nc.scalar.activation(XH[:], PS[:, 4:6, :].rearrange("p a b -> p (a b)"),
                                         ACT.Copy).then_inc(sem("x_hi"), 1)
                    split(2)
                    for kind, c in vector_order():
                        if kind == "split":
                            if c > 2:
                                split(c)
                        elif kind == "hidden":
                            act.wait_ge(sem("piece_used"), PER_EXPERT * E_ + piece_of("u", c) + 2)
                            nc.scalar.activation(HS, PS[:, 2 * (c % 2), :], ACT.Silu).then_inc(sem("silu"), 1)
                        else:
                            act.wait_ge(sem("hidden_T"), EC * E_ + c + 1)
                            nc.scalar.activation(HTH[:], PS[:, 4, :], ACT.Copy).then_inc(sem("ht_hi"), 1)
                    act.wait_ge(sem("piece_used"), PER_EXPERT * E_ + PER_EXPERT)
                    nc.scalar.activation(YS, PS[:, 6:8, :].rearrange("p a b -> p (a b)"),
                                         ACT.Copy).then_inc(sem("y_copied"), 1)

            expert_pass(0)
            act.wait_ge(sem("flag_ready"), 1)
            flag = act.value_load(FLAG[0:1, 0:1], min_val=0, max_val=1)
            with act.If(flag > 0):
                expert_pass(1)
            act.wait_ge(sem("moe_sum"), 1)
            root(PS[:, 5, 0:256], D)

        @block.vector
        def _(dve):
            count = {}
            V_ = nc.vector

            def do(ins, name="dve_step"):
                count[name] = count.get(name, 0) + 1
                ins.then_inc(sem(name), 1)
                dve.wait_ge(sem(name), count[name])

            def drain(ins, name):
                drained_by(ins, name)
                wait_drained(dve, name)

            def mod(layer, chunks):
                for n in chunks:
                    wait_written(dve, ("modT", layer, n))
                    b = bank(("modT", layer, n))[:, 0:8].rearrange("p (m s) -> p m s", s=2)
                    bias = param("b_mod", 48 * layer + 4 * n, 48 * layer + 4 * n + 4).unsqueeze(2)
                    drain(V_.tensor_tensor(MOD[:, 48 * layer + 4 * n:48 * layer + 4 * n + 4, :], b,
                                           bias.to_broadcast([128, 4, 2]), ALU.add), ("modT", layer, n))

            def coefs(layer):
                for which, (seg, gain, one) in enumerate(((1, "g_pre_mix", 1.0), (2, "g_post_mix", 0.0),
                                                          (4, "g_pre_ffn", 1.0), (5, "g_post_ffn", 0.0))):
                    c = COEF[:, 4 * layer + which, :, :]
                    m = MOD[:, 48 * layer + 8 * seg:48 * layer + 8 * seg + 8, :]
                    g = param(gain, 8 * layer, 8 * layer + 8).unsqueeze(2).to_broadcast([128, 8, 2])
                    do(V_.tensor_scalar(c, m, one, math.sqrt(D), ALU.add, ALU.mult))
                    do(V_.tensor_tensor(c, c, g, ALU.mult), "dve_step" if which < 3 else "coefs")

            def rstd(name, out, n, width):
                count["rooted"] = count.get("rooted", 0) + 1
                dve.wait_ge(sem("rooted"), count["rooted"])
                drain(V_.reciprocal(out, bank(name)[:, 0:width]), name)

            def scaled(i, src, lo, hi):
                w = hi - lo
                rstd(("ss", i), RST[:, 0:w], D, w)
                for j in range(4):
                    V_.tensor_tensor(H[:, 2 * j:2 * j + 2, lo:hi], src[:, 2 * j:2 * j + 2, lo:hi],
                                     RST[:, 0:w].unsqueeze(1).to_broadcast([128, 2, w]),
                                     ALU.mult).then_inc(sem("x_scaled"), 1)

            def residual(i, y, layer, which, streams, ready="x_ready"):
                w = 256 * len(streams)
                if i is not None:
                    rstd(("ss", i), RST[:, 0:w], D, w)
                for j in range(4):
                    do(V_.tensor_tensor(y[:, 2 * j:2 * j + 2, 0:w], y[:, 2 * j:2 * j + 2, 0:w],
                                        RST[:, 0:w].unsqueeze(1).to_broadcast([128, 2, w]), ALU.mult))
                dve.wait_ge(sem("coefs"), layer + 1)
                for kt in range(KT):
                    for n, s in enumerate(streams):
                        x = X[:, kt, 256 * s:256 * s + 256]
                        ins = V_.scalar_tensor_tensor(x, y[:, kt, 256 * n:256 * n + 256],
                                                      COEF[:, 4 * layer + which, kt, s:s + 1], x, ALU.mult, ALU.add)
                    ins.then_inc(sem(ready), 1)
                    count[ready] = count.get(ready, 0) + 1
                dve.wait_ge(sem(ready), count[ready])

            for j, n in enumerate((D, Q_RANK, 2 * DIFF_D)):
                do(V_.memset(SMALL[:, 5 + j:6 + j], n * EPS), "eps_ready")
            dve.wait_ge(sem("param_loaded"), 16)
            for a, b, name, f in ((0, 2, "g_q", math.sqrt(Q_RANK)), (2, 3, "g_kv", math.sqrt(KV_RANK)),
                                  (3, 4, "g_gla", math.sqrt(DV)), (4, 5, "g_diff", math.sqrt(2 * DIFF_D) * (1.0 - LAM_INIT))):
                do(V_.tensor_scalar(SMALL[:, a:b], param(name), f, None, ALU.mult))
            for j, (a, b) in enumerate((("lq1", "lk1"), ("lq2", "lk2"))):
                do(V_.tensor_tensor(TMP[:, 0:64], param(a), param(b), ALU.mult))
                do(V_.reduce_sum(SMALL[:, 8 + j:9 + j], TMP[:, 0:64], axis=AX.X), ("dve_step", "lam_logits")[j])
            mod(0, range(12))
            coefs(0)
            scaled(0, X, 0, T)

            for name, parts in (("ssq", ((CQ[:, 0, :], 0), (CQ[:, 1, :], 1))), ("sskv", ((CKV, 2),))):
                rstd(name, RST[:], Q_RANK if name == "ssq" else KV_RANK, T)
                dve.wait_ge(sem("mla_squares"), 3)
                for part, g in parts:
                    do(V_.scalar_tensor_tensor(part, part, SMALL[:, g:g + 1], RST[:], ALU.mult, ALU.mult), "lora_normed")
            for d, name in enumerate(("af", "ab")):
                wait_written(dve, name)
                drain(V_.tensor_copy(AF[0:16, d, :], bank(name)[0:16, :]), name)
            for p in range(2):
                wait_written(dve, ("qr", p))
                drain(V_.tensor_copy(QR[:, p, :], bank(("qr", p))), ("qr", p))
            for t in range(TT):
                wait_written(dve, ("v", t))
                drain(V_.tensor_copy(V[:, t, :], bank(("v", t))), ("v", t))
            for name, x in ((("rotq", 0), QR[:, 0, T_CTX:T]), (("rotq", 1), QR[:, 1, T_CTX:T]), ("rotk", KR[:, T_CTX:T])):
                wait_written(dve, name)
                drain(V_.tensor_tensor(TMP[:, 0:256], bank(name)[:, 0:256], const("sin"), ALU.mult), name)
                do(V_.tensor_tensor(x, x, const("cos"), ALU.mult))
                do(V_.tensor_tensor(x, x, TMP[:, 0:256], ALU.add), "mla_roped")
            for t in range(TT):
                wait_written(dve, ("gx", t))
                drain(V_.tensor_tensor(LX[:, t, :], bank(("gx", t)), param("b_gate"), ALU.add), ("gx", t))

            def attend(steps):
                for kind, u in steps:
                    if kind == "s":
                        keys = (2 if u % TT < 2 else 4) * 128
                        wait_written(dve, ("s", u))
                        do(V_.reduce_max(STAT[:, u:u + 1], bank(("s", u))[:, 0:keys], axis=AX.X))
                        do(V_.tensor_scalar(STAT[:, u:u + 1], STAT[:, u:u + 1], -MLA_SCALE, None, ALU.mult), "mla_max")
                    elif kind == "pT":
                        keys = (2 if u % TT < 2 else 4) * 128
                        wait_drained(dve, ("s", u))
                        do(V_.reciprocal(STAT[:, 32 + u:33 + u], STAT[:, 32 + u:33 + u]))
                        do(V_.tensor_scalar(PB[:, u % 3, 0:keys], PB[:, u % 3, 0:keys], STAT[:, 32 + u:33 + u], None,
                                            ALU.mult), "probs")
                    elif kind == "o":
                        wait_written(dve, ("o", u))
                        drain(V_.tensor_copy(H[:, u // 2, 256 * (u % 2):256 * (u % 2) + 256], bank(("o", u))[:, 0:256]),
                              ("o", u))
                    elif kind in ("s1", "s2"):
                        j = kind == "s2"
                        c = 16 * j + u
                        wait_written(dve, (kind, u))
                        do(V_.reduce_max(STAT[:, c:c + 1], bank((kind, u)), axis=AX.X))
                        do(V_.tensor_scalar(STAT[:, c:c + 1], STAT[:, c:c + 1], -DIFF_SCALE, None, ALU.mult), "diff_max")
                    elif kind == "dT":
                        wait_drained(dve, ("s1", u))
                        wait_drained(dve, ("s2", u))
                        do(V_.reciprocal(STAT[:, 32 + u:33 + u], STAT[:, 32 + u:33 + u]))
                        do(V_.reciprocal(STAT[:, 48 + u:49 + u], STAT[:, 48 + u:49 + u]))
                        do(V_.tensor_scalar(E2[:, u % 3, :], E2[:, u % 3, :], STAT[:, 48 + u:49 + u], SMALL[:, 10:11],
                                            ALU.mult, ALU.mult))
                        do(V_.scalar_tensor_tensor(E1[:, u % 3, :], E1[:, u % 3, :], STAT[:, 32 + u:33 + u],
                                                   E2[:, u % 3, :], ALU.mult, ALU.subtract), "diff_probs")
                    elif kind == "do":
                        dve.wait_ge(sem("diff_squares"), u + 1)
                        drain(V_.tensor_copy(OD[:, u, :], bank(("do", u))[:, 0:256]), ("do", u))

            attend(mla_steps())

            do(V_.scalar_tensor_tensor(LE, LX, -1.0, LX, ALU.mult, ALU.min), "gate_abs")
            dve.wait_ge(sem("act_gate"), 1)
            do(V_.tensor_scalar(LE, LE, 1.0, None, ALU.add), "gate_plus")
            dve.wait_ge(sem("act_gate"), 2)
            do(V_.scalar_tensor_tensor(LX, LX, 0.0, LE, ALU.min, ALU.subtract), "log_decays")

            def cum_of(d, k):
                return CUM[:, 2 * d + k, :].rearrange("p (c i) -> p c i", i=CHUNK)

            for h in range(GLA_H):
                wait_written(dve, ("att", "diag", h))
                a = ATT[:, h, :].rearrange("p (c t) -> p c t", t=128)
                drained_by(V_.tensor_tensor(a, bank(("att", "diag", h)).rearrange("p (c t) -> p c t", t=128),
                                            const("diag2").unsqueeze(1).to_broadcast([128, TT, 128]), ALU.mult),
                           ("att", "diag", h))
            for h in range(GLA_H):
                wait_drained(dve, ("att", "diag", h))
            for d in range(2):
                for k in range(2):
                    wait_drained(dve, ("cum", d, k))
                    edge = 63 if d == 0 else 0
                    last = cum_of(d, k)[:, :, edge:edge + 1].to_broadcast([128, 8, CHUNK])
                    do(V_.tensor_tensor(EX[:, d, T * k:T * k + T].rearrange("p (c i) -> p c i", i=CHUNK), last,
                                        cum_of(d, k), ALU.subtract), ("dve_step", "key_exponents")[k])
                dve.wait_ge(sem("decay_exp"), d + 1)
                do(V_.tensor_tensor(QH[:, 2 * d:2 * d + 2, :], QH[:, 2 * d:2 * d + 2, :], GQ, ALU.mult), "decayed_queries")
                dve.wait_ge(sem("key_exp"), d + 1)
                do(V_.tensor_tensor(AA[:, d, :], EX[:, d, :], A_[:, 1024:2048], ALU.mult), "decayed_keys")

            def exponents(n):
                d, m = n // 6, LEVELS[n % 6]
                cum = A_[:, m0 + 1024 * d:m0 + 1024 * d + 1024].rearrange("p (b u m) -> p b u m", u=2, m=m)
                ex = EX[:, n % 2, :].rearrange("p (b u m) -> p b u m", u=2, m=m)
                nb = 2 * T // (2 * m)
                ref = (cum[:, :, 0, m - 1:m] if d == 0 else cum[:, :, 1, 0:1]).to_broadcast([128, nb, m])
                qh = 1 - d
                V_.tensor_tensor(ex[:, :, qh, :], cum[:, :, qh, :], ref, ALU.subtract)
                do(V_.tensor_tensor(ex[:, :, 1 - qh, :], ref, cum[:, :, 1 - qh, :], ALU.subtract), "level_exponents")

            def decayed(n):
                d, m = n // 6, LEVELS[n % 6]
                qh = 1 - d
                blocks = lambda a: a.rearrange("p (b u m) -> p b u m", u=2, m=m)
                dve.wait_ge(sem("level_exp"), n + 1)
                if n < 2:
                    for t in range(TT):
                        wait_written(dve, ("kT", n, t))
                else:
                    wait_written(dve, ("att", ((n - 2) // 6, (n - 2) % 6), 3))
                V_.tensor_tensor(blocks(AA[:, n % 2, :])[:, :, qh, :], blocks(EX[:, n % 2, :])[:, :, qh, :],
                                 blocks(A_[:, 0:1024])[:, :, qh, :], ALU.mult)
                do(V_.tensor_tensor(blocks(AA[:, n % 2, :])[:, :, 1 - qh, :], blocks(EX[:, n % 2, :])[:, :, 1 - qh, :],
                                    blocks(A_[:, 1024:2048])[:, :, 1 - qh, :], ALU.mult), "level_ready")

            def add_scores(n):
                mask = C[:, CONST["masks"][0] + 128 * n:CONST["masks"][0] + 128 * n + 128].bitcast(u32)
                for h in range(GLA_H):
                    name = ("att", (n // 6, n % 6), h)
                    wait_written(dve, name)
                    drained_by(V_.copy_predicated(ATT[:, h, :].rearrange("p (c t) -> p c t", t=128),
                                                  mask.unsqueeze(1).to_broadcast([128, TT, 128]),
                                                  bank(name).rearrange("p (c t) -> p c t", t=128)), name)
                for h in range(GLA_H):
                    wait_drained(dve, ("att", (n // 6, n % 6), h))

            exponents(0)
            exponents(1)
            for n in range(12):
                decayed(n)
                if n + 2 < 12:
                    exponents(n + 2)
                add_scores(n)
            for d in range(2):
                dve.wait_ge(sem("chunk_decay"), d + 1)
            for d in range(2):
                for p in range(2):
                    left = [c for c in chunk_order[d]][:-1]
                    lasts = {r: [c for c in left if c % 2 == r][-1] for r in range(2)}
                    for r in range(2):
                        wait_written(dve, ("U", d, p, r))
                    for j, c in enumerate(left):
                        nxt = chunk_order[d][j + 1]
                        name = ("U", d, p, c % 2)
                        u = bank(name)[:, 128 * (c // 2):128 * (c // 2) + 128]
                        if j == 0:
                            ins = V_.tensor_copy(state(d, p, nxt), u)
                        else:
                            k = 64 + 16 * d + 8 * p + c
                            ins = V_.scalar_tensor_tensor(state(d, p, nxt), state(d, p, c), STAT[:, k:k + 1], u,
                                                          ALU.mult, ALU.add)
                        if lasts[c % 2] == c:
                            drain(ins, name)
                        else:
                            do(ins, "states_step")
            for h in range(GLA_H):
                dve.wait_ge(sem("gla_squares"), h + 1)
                drain(V_.tensor_copy(AA[:, h // 2, T * (h % 2):T * (h % 2) + T], bank(("og", h))), ("og", h))
            for h in range(GLA_H):
                rstd(("ssg", h), RST[:], DV, T)
                y = H[:, 4 + h, :]
                do(V_.scalar_tensor_tensor(y, AA[:, h // 2, T * (h % 2):T * (h % 2) + T], SMALL[:, 3:4], RST[:],
                                           ALU.mult, ALU.mult))
                do(V_.tensor_tensor(y, y, GR[:, h, :], ALU.mult), "gla_out")

            def after_drained(names):
                for x in names:
                    wait_drained(dve, x)

            mod(1, range(0, 3))
            after_drained([("ya", m) for m in range(8)])
            residual(1, YO, 0, 1, (0, 1))
            mod(1, range(3, 7))
            scaled(2, X, 0, T)
            for m in range(FT):
                wait_written(dve, ("u", m))
                wait_drained(dve, ("g", m))
                ins = V_.tensor_tensor(FF[:, m, :], FF[:, m, :], bank(("u", m)), ALU.mult)
                drain(ins, ("u", m))
            mod(1, range(7, 12))
            coefs(1)
            after_drained([("yf", m) for m in range(8)])
            residual(3, YO, 0, 3, (0, 1))
            scaled(4, X, 0, T)
            dve.wait_ge(sem("lam_exp"), 1)
            do(V_.tensor_tensor(SMALL[:, 10:11], SMALL[:, 8:9], SMALL[:, 9:10], ALU.subtract))
            do(V_.tensor_scalar(SMALL[:, 10:11], SMALL[:, 10:11], LAM_INIT, None, ALU.add))
            for n in range(2):
                for t in range(TT):
                    wait_written(dve, ("v1", t, n))
                    drained_by(V_.tensor_copy(V1[:, t, 512 * n:512 * n + 512], bank(("v1", t, n))), ("v1", t, n))
            for m in range(8):
                wait_written(dve, ("rot", m))
                s2 = const("sin").unsqueeze(1).to_broadcast([128, 2, 256])
                drain(V_.tensor_tensor(TMP[:].rearrange("p (a b) -> p a b", b=256),
                                       bank(("rot", m)).rearrange("p (a b) -> p a b", b=256), s2, ALU.mult), ("rot", m))
                for j, x in enumerate((Q1[:, m, :], K1[:, m, T_CTX:T])):
                    do(V_.tensor_tensor(x, x, const("cos"), ALU.mult))
                    do(V_.tensor_tensor(x, x, TMP[:, 256 * j:256 * j + 256], ALU.add), ("dve_step", "diff_roped")[j])
            attend(diff_steps())
            for h in range(DIFF_H):
                rstd(("ssd", h), RST[:, 0:256], 2 * DIFF_D, 256)
                do(V_.scalar_tensor_tensor(H[:, h, T_CTX:T], OD[:, h, :], SMALL[:, 4:5], RST[:, 0:256], ALU.mult,
                                           ALU.mult), "diff_out")
            after_drained([("yc", m) for m in range(8)])
            residual(5, YO1, 1, 1, (1,))
            scaled(6, X, T_CTX, T)

            LG, RK, SEL = view(RT, 0, 2, E), view(RT, 48, 2, E), view(RT, 64, 2, E)
            GATE, SPOS, CMP = view(RT, 80, 2, E), view(RT, 96, 2, E), view(RT, 128, 8, 8)
            CMQ = view(RT, 192, 8, 8)
            for t in range(2):
                wait_written(dve, ("lg", t))
                drain(V_.tensor_copy(LG[:, t, :], bank(("lg", t))[:, 0:E]), ("lg", t))
                do(V_.max(RT[:, 16 + 8 * t:24 + 8 * t], LG[:, t, :]))
                do(V_.tensor_tensor(RT[:, 40 + t:41 + t], RT[:, 17 + 8 * t:18 + 8 * t], RT[:, 16 + 8 * t:17 + 8 * t],
                                    ALU.subtract), ("dve_step", "gate_logits")[t])
            for t in range(2):
                other = LG[:, t, :].unsqueeze(1).to_broadcast([128, 8, 8])
                own = LG[:, t, :].unsqueeze(2).to_broadcast([128, 8, 8])
                do(V_.tensor_tensor(CMP, other, own, ALU.is_gt))
                do(V_.tensor_tensor(CMQ, other, own, ALU.is_equal))
                do(V_.tensor_tensor(CMQ, CMQ, const("lower8").rearrange("p (a b) -> p a b", b=8), ALU.mult))
                do(V_.tensor_tensor(CMP, CMP, CMQ, ALU.add))
                do(V_.reduce_sum(RK[:, t, :], CMP, axis=AX.X))
            do(V_.tensor_scalar(SEL, RK, 2.0, None, ALU.is_lt), "selected")
            dve.wait_ge(sem("gate_exp"), 1)
            do(V_.tensor_scalar(RT[:, 42:44], RT[:, 40:42], 1.0, None, ALU.add))
            do(V_.reciprocal(RT[:, 42:44], RT[:, 42:44]))
            do(V_.tensor_tensor(RT[:, 44:46], RT[:, 42:44], RT[:, 40:42], ALU.mult))
            for t in range(2):
                do(V_.tensor_scalar(GATE[:, t, :], RK[:, t, :], 0.0, RT[:, 42 + t:43 + t], ALU.is_equal, ALU.mult))
                do(V_.tensor_scalar(CMQ[:, 0, :], RK[:, t, :], 1.0, RT[:, 44 + t:45 + t], ALU.is_equal, ALU.mult))
                do(V_.tensor_tensor(GATE[:, t, :], GATE[:, t, :], CMQ[:, 0, :], ALU.add))
            for t in range(2):
                wait_written(dve, ("pos", t))
                drain(V_.scalar_tensor_tensor(SPOS[:, t, :], bank(("pos", t))[:, 0:E], 1000.0, SEL[:, t, :], ALU.add,
                                              ALU.mult), ("pos", t))
            do(V_.tensor_scalar(SPOS, SPOS, -1000.0, None, ALU.add))
            wait_written(dve, "cnt")
            drain(V_.reduce_max(RT[:, 112:113], bank("cnt")[:, 0:E], axis=AX.X), "cnt")
            do(V_.tensor_scalar(FLAG[:], RT[:, 112:113], 128.0, None, ALU.is_gt), "flag_ready")
            for t in range(2):
                for n in range(2):
                    wait_written(dve, ("ht", t, n))
            do(V_.memset(ACC, 0.0), "acc_done")

            def expert_pass(k):
                if k:
                    do(V_.tensor_scalar(SPOS, SPOS, -128.0, None, ALU.add))
                for j in range(4):
                    for i2 in range(2):
                        for t in range(2):
                            e = 2 * j + i2
                            V_.tensor_scalar(PSEL[:, E * t + e, :], const("iota"), SPOS[:, t, e:e + 1], None, ALU.is_equal)
                            ins = V_.tensor_scalar(PG[:, t, e, :], const("iota"), SPOS[:, t, e:e + 1],
                                                   GATE[:, t, e:e + 1], ALU.is_equal, ALU.mult)
                    do(ins, "onehots")
                with dve.Fori(0, E) as e:
                    E_ = e + E * k

                    def split(q):
                        n = n_pre + q
                        dve.wait_ge(sem("hi_made"), PER_EXPERT * E_ + q + 1)
                        s = slice(q % SPLITS * PIECE, (q % SPLITS + 1) * PIECE)
                        V_.tensor_tensor(LO[:, s], slot(n), HI[:, s].bitcast(f32), ALU.subtract).then_inc(sem("lo_made"), 1)

                    split(0)
                    dve.wait_ge(sem("x_hi"), E_ + 1)
                    V_.tensor_tensor(XL[:], PS[:, 4:6, :].rearrange("p a b -> p (a b)"), XH[:].bitcast(f32),
                                     ALU.subtract).then_inc(sem("x_lo"), 1)
                    split(1)
                    for kind, c in vector_order():
                        if kind == "split":
                            if c > 1:
                                split(c)
                        elif kind == "hidden":
                            dve.wait_ge(sem("silu"), EC * E_ + c + 1)
                            V_.tensor_tensor(HS, HS, PS[:, 2 * (c % 2) + 1, :], ALU.mult).then_inc(sem("hidden"), 1)
                        else:
                            dve.wait_ge(sem("ht_hi"), EC * E_ + c + 1)
                            V_.tensor_tensor(HTL[:], PS[:, 4, :], HTH[:].bitcast(f32), ALU.subtract).then_inc(sem("ht_lo"), 1)
                    for j in range(4):
                        dve.wait_ge(sem("scattered"), 4 * E_ + j + 1)
                        a = ACC[:, 2 * j:2 * j + 2, :].rearrange("p a b -> p (a b)")
                        V_.tensor_tensor(a, a, PS[:, j, :], ALU.add).then_inc(sem("acc_done"), 1)
                dve.wait_ge(sem("acc_done"), 4 * E * (k + 1) + 1)

            expert_pass(0)
            dve.wait_ge(sem("flag_ready"), 1)
            flag = dve.value_load(FLAG[0:1, 0:1], min_val=0, max_val=1)
            with dve.If(flag > 0):
                expert_pass(1)
            do(V_.tensor_tensor(view(A_, 2048, KT, 256), ACC, ACC, ALU.mult), "moe_squares")
            dve.wait_ge(sem("rooted"), count["rooted"] + 1)
            do(V_.reciprocal(RST[:, 0:256], PS[:, 5, 0:256]))
            residual(None, ACC, 1, 3, (1,), ready="out_ready")


def constants():
    out = np.zeros((128, CONST_W), np.float32)

    def put(name, a):
        out[:, CONST[name][0]:CONST[name][1]] = a

    i, j = np.arange(128)[:, None], np.arange(128)[None, :]
    same = i // CHUNK == j // CHUNK
    put("ident", i == j)
    put("ones", 1.0)
    put("tri_f", (same & (i <= j)) / TAU)
    put("tri_b", (same & (i >= j)) / TAU)
    put("before", i < j)
    rot = np.zeros((128, 128), np.float32)
    for m in range(128):
        if m % 64 < 32:
            rot[m + 32, m] = -1.0
        else:
            rot[m - 32, m] = 1.0
    put("rot", rot)
    n_freq = ROPE // 4
    tok = np.arange(T_LAT)
    freq = (np.float32(ROPE_BASE) ** (-np.arange(n_freq, dtype=np.float32) / np.float32(n_freq))).astype(np.float32)
    row, col = (tok // GRID_W).astype(np.float32), (tok % GRID_W).astype(np.float32)
    ang = np.concatenate([row[:, None] * freq, col[:, None] * freq], axis=-1).T
    put("cos", np.tile(np.cos(ang), (4, 1)))
    put("sin", np.tile(np.sin(ang), (4, 1)))
    masks = []
    for d in range(2):
        for m in LEVELS:
            lo, hi = i % (2 * m) < m, j % (2 * m) >= m
            up, dn = i % (2 * m) >= m, j % (2 * m) < m
            block = i // (2 * m) == j // (2 * m)
            masks.append(block & (lo & hi if d == 0 else up & dn))
    put("masks", np.concatenate(masks, 1))
    put("diag2", 2.0 * (i == j))
    put("iota", np.broadcast_to(j, (128, 128)))
    put("lower8", np.broadcast_to((np.arange(8)[None, :] < np.arange(8)[:, None]).reshape(1, 64), (128, 64)))
    return out


def kernel(**inputs):
    import concourse.bacc as _bacc
    from concourse import mybir as _mybir
    from concourse.bass_utils import run_bass_kernel_spmd as _run

    a = {k: np.asarray(v) for k, v in inputs.items()}
    uq = a["mla_w_uq"].reshape(1, Q_RANK, MLA_H, NOPE + ROPE)
    a["mla_w_uq"] = np.concatenate([uq[..., :NOPE].reshape(1, Q_RANK, -1), uq[..., NOPE:].reshape(1, Q_RANK, -1)], 2)
    by_tile = lambda v: v.reshape(-1, 128).T

    pieces = list(plan()[0])
    for e in range(E):
        for kind, c, _ in expert_order():
            for half in range(2):
                if kind == "d":
                    pieces.append(("moe_w_down", (0, e), 4 * c + 2 * half, 4 * c + 2 * half + 2, 0, D, None))
                else:
                    pieces.append((("moe_w_gate" if kind == "g" else "moe_w_up"), (0, e), 4 * half, 4 * half + 4,
                                   512 * c, 512 * c + 512, None))
    stream = np.zeros((len(pieces), 128, PIECE), np.float32)
    for n, (src, index, k0, k1, c0, c1, _) in enumerate(pieces):
        w = a[src][index][128 * k0:128 * k1, c0:c1].reshape(k1 - k0, 128, c1 - c0)
        stream[n, :, 0:(k1 - k0) * (c1 - c0)] = w.transpose(1, 0, 2).reshape(128, -1)

    param = np.zeros((128, PARAM_W), np.float32)

    def put(name, v, rows=128):
        param[0:rows, PARAM[name][0]:PARAM[name][1]] = v

    put("c", np.stack([by_tile(a["c_ctx"]), by_tile(a["c"][0])], 2).reshape(128, 16))
    for name in ("g_pre_mix", "g_post_mix", "g_pre_ffn", "g_post_ffn", "b_mod"):
        put(name, np.concatenate([by_tile(a[name][i]) for i in range(2)], 1))
    put("g_q", by_tile(a["mla_g_q"][0]))
    put("g_kv", by_tile(a["mla_g_kv"][0]))
    put("g_gla", by_tile(a["gla_g_out"][0]))
    put("g_diff", by_tile(a["diff_g_out"][0]))
    for name in ("lq1", "lk1", "lq2", "lk2"):
        put(name, np.broadcast_to(a["diff_" + name][0], (128, DIFF_D)))
    put("router", a["moe_w_router"][0].reshape(KT, 128, E).transpose(1, 0, 2).reshape(128, KT * E))
    put("w_gate", np.concatenate([a["gla_w_gate_f"][0], a["gla_w_gate_b"][0]], 1), rows=RANK)
    put("b_gate", np.broadcast_to(np.concatenate([a["gla_b_gate_f"][0], a["gla_b_gate_b"][0]]), (128, 512)))

    arrays = {"stream_dram": stream, "const_dram": constants(), "param_dram": param,
              "x_dram": np.ascontiguousarray(np.concatenate([a["ctx"][0].T, a["x"][0].T], 1))}
    nc = _bacc.Bacc("TRN2", target_bir_lowering=False, num_devices=1)
    args = [nc.dram_tensor(n, v.shape, _mybir.dt.float32, kind="ExternalInput").ap() for n, v in arrays.items()]
    args.append(nc.dram_tensor("out_dram", (D, T_LAT), _mybir.dt.float32, kind="ExternalOutput").ap())
    build(nc, *args)
    r = _run(nc, [arrays], core_ids=[0])
    return np.ascontiguousarray(r.results[0]["out_dram"].T)[None]
```

```python
import math
from contextlib import ExitStack

import numpy as np
import concourse.bass as bass
from concourse import mybir

D, T_CTX, T_LAT = 1024, 256, 256
T = T_CTX + T_LAT
KT = D // 128
TT = T // 128
EPS = 1e-6
MLA_H, Q_RANK, KV_RANK, NOPE, ROPE, VD = 4, 256, 128, 128, 64, 128
MLA_SCALE = (NOPE + ROPE) ** -0.5
GLA_H, DK, DV, RANK, TAU, CHUNK = 4, 64, 128, 16, 16.0, 64
N_CHUNKS = T // CHUNK
LEVELS = [32, 16, 8, 4, 2, 1]
DIFF_H, DIFF_D = 8, 64
DIFF_SCALE = DIFF_D ** -0.5
LAM_INIT = 0.8 - 0.6 * math.exp(-0.3)
FFN = 2816
FT = FFN // 128
E, EF = 8, 3584
EC = EF // 512
GRID_W, ROPE_BASE = 64, 10000.0
COLS_A = dict(cq=0, ckv=256, kr=384, gq=448, gk=704, gv=960, gr=1472, af=1984, ab=2000)
IN_A = 2016

SLOTS, PIECE = 7, 2048
SPLITS = 3
BANKS = 8


def columns(*widths):
    at, out = 0, {}
    for name, width in widths:
        out[name] = (at, at + width)
        at += width
    return out, at


CONST, CONST_W = columns(
    ("ident", 128), ("ones", 128), ("tri_f", 128), ("tri_b", 128), ("before", 128), ("rot", 128),
    ("cos", 256), ("sin", 256), ("masks", 12 * 128), ("diag2", 128), ("iota", 256), ("lower8", 64))
PARAM, PARAM_W = columns(
    ("c", 16), ("g_pre_mix", 16), ("g_post_mix", 16), ("g_pre_ffn", 16), ("g_post_ffn", 16),
    ("b_mod", 96), ("g_q", 2), ("g_kv", 1), ("g_gla", 1), ("g_diff", 1),
    ("lq1", 64), ("lk1", 64), ("lq2", 64), ("lk2", 64), ("router", 64), ("w_gate", 512), ("b_gate", 512))


def plan():
    pieces, where, tiles = [], {}, []

    def linear(label, src, index, rows, c0, c1, last):
        kmax = PIECE // (c1 - c0)
        n = -(-rows // kmax)
        step = -(-rows // n)
        where[label] = []
        for k0 in range(0, rows, step):
            k1 = min(k0 + step, rows)
            where[label].append((len(pieces), k0, k1, c1 - c0))
            pieces.append((src, index, k0, k1, c0, c1, last))

    def mod(layer, chunks):
        for n in chunks:
            linear(("mod", layer, n), "w_mod", layer, KT, 512 * n, 512 * n + 512, ("mod", layer, n))
            tiles.append(("mod", layer, n))
            if n:
                tiles.append(("modT", layer, n - 1))
        if n == 11:
            tiles.append(("modT", layer, n))

    mod(0, range(12))
    tiles.append(("ss", 0))
    linear("in_a0", "w_in_a", 0, KT, 0, 448, "kr")
    linear("in_a1", "w_in_a", 0, KT, 448, 960, ("gk", 1))
    linear("gv", "w_in_a", 0, KT, 960, 1472, ("gv", 3))
    linear("gr", "w_in_a", 0, KT, 1472, 1984, ("gr", 3))
    linear("gaf", "w_in_a", 0, KT, 1984, 2016, "ab")
    tiles.extend([("cq", 0), ("cq", 1), "ckv", "kr", ("gq", 0), ("gq", 1), "ssq", "sskv", ("gk", 0), ("gk", 1)])
    tiles.extend(("gv", t) for t in range(TT))
    tiles.extend(("gr", m) for m in range(4))
    tiles.extend(["af", "ab"])
    linear("uq", "mla_w_uq", 0, 2, 0, 768, ("qr", 1))
    linear("ukv", "mla_w_ukv", 0, 1, 0, 1024, ("v", 3))
    tiles.extend(("qn", h) for h in range(4))
    tiles.extend(("qr", p) for p in range(2))
    tiles.extend(("kn", h) for h in range(4))
    tiles.extend(("v", t) for t in range(TT))
    tiles.extend([("rotq", 0), ("rotq", 1), "rotk"])
    tiles.extend(("gx", t) for t in range(TT))
    tiles.extend(x for x in mla_steps())
    tiles.extend(("cum", d, k) for d in range(2) for k in range(2))
    tiles.extend(("att", "diag", h) for h in range(4))
    tiles.extend(("kT", d, t) for d in range(2) for t in range(TT))
    tiles.extend(("att", (d, lv), h) for d in range(2) for lv in range(6) for h in range(4))
    tiles.extend(("U", d, p, r) for d in range(2) for p in range(2) for r in range(2))
    tiles.extend(("og", h) for h in range(4))
    tiles.extend(("ssg", h) for h in range(4))
    for n in range(2):
        linear(("out_a", n), "w_out_a", 0, KT, 512 * n, 512 * n + 512, ("ya", 4 * n + 3))
    tiles.extend(("ya", m) for m in range(8))
    mod(1, range(0, 4))
    tiles.append(("ss", 1))
    mod(1, range(4, 8))
    tiles.append(("ss", 2))
    for n in range(6):
        c1 = min(512 * n + 512, FFN)
        m1 = c1 // 128 - 1
        linear(("fg", n), "ffn_w_gate", 0, KT, 512 * n, c1, ("u", m1))
        linear(("fu", n), "ffn_w_up", 0, KT, 512 * n, c1, ("u", m1))
    for m in range(FT):
        tiles.extend([("g", m), ("u", m)])
    for m in range(8):
        linear(("fd", m), "ffn_w_down", 0, FT, 128 * m, 128 * m + 128, ("yf", m))
        tiles.append(("yf", m))
    mod(1, range(8, 12))
    tiles.append(("ss", 3))
    tiles.append(("ss", 4))
    for n in range(4):
        linear(("qk", n), "w_qkv_c", 0, KT, 512 * n, 512 * n + 512, ("qk", 4 * n + 3))
    for n in range(2):
        linear(("v1", n), "w_qkv_c", 0, KT, 2048 + 512 * n, 2560 + 512 * n, ("v1", 3, n))
    tiles.extend(("qk", m) for m in range(16))
    tiles.extend(("v1", t, n) for n in range(2) for t in range(TT))
    tiles.extend(("rot", m) for m in range(8))
    tiles.extend(x for x in diff_steps())
    for n in range(2):
        linear(("out_c", n), "w_out_c", 0, KT, 512 * n, 512 * n + 512, ("yc", 4 * n + 3))
    tiles.extend(("ssd", h) for h in range(8))
    tiles.extend(("yc", m) for m in range(8))
    tiles.extend([("ss", 5), ("ss", 6)])
    tiles.extend([("lg", 0), ("lg", 1)])
    tiles.extend(("ht", t, n) for t in range(2) for n in range(2))
    tiles.extend([("pos", 0), ("pos", 1), "cnt"])
    return pieces, where, {name: i for i, name in enumerate(tiles)}


def pipelined(scores, probs, outs, units):
    steps = []
    for u in range(2):
        steps += scores(u)
    for u in range(units):
        if u + 2 < units:
            steps += scores(u + 2)
        if u % 2 == 0 and u:
            steps.append(outs(u // 2 - 1))
        steps.append(probs(u))
    steps.append(outs(units // 2 - 1))
    return steps


def mla_steps():
    return pipelined(lambda u: [("s", u)], lambda u: ("pT", u), lambda g: ("o", g), MLA_H * TT)


def diff_steps():
    return pipelined(lambda u: [("s1", u), ("s2", u)], lambda u: ("dT", u), lambda g: ("do", g), DIFF_H * 2)


def expert_order():
    steps, at = [], 0
    for c in range(EC):
        for kind in "gu":
            steps.append((kind, c, at))
            at += 2
        if c:
            steps.append(("d", c - 1, at))
            at += 2
    steps.append(("d", EC - 1, at))
    return steps


PER_EXPERT = 6 * EC


def piece_of(kind, c):
    return next(j for k, cc, j in expert_order() if (k, cc) == (kind, c))

def vector_order():
    after = {}
    for c in range(EC):
        before = piece_of("d", c - 1) + 1 if c else piece_of("u", 0) + 1
        after.setdefault(min(piece_of("u", c) + 3, PER_EXPERT - 1), []).append(("hidden", c))
        after.setdefault(min(before + 2, PER_EXPERT - 1), []).append(("transposed", c))
    steps = []
    for q in range(PER_EXPERT):
        steps.append(("split", q))
        if q == piece_of("u", 0) + 3:
            steps.append(("scatter_matrix", 0))
        steps += sorted(after.get(q, []), key=lambda x: (x[0] != "hidden"))
    return steps


def build(nc, stream, const_dram, param_dram, x_dram, out_dram):
    f32, f32r, i32, u32 = mybir.dt.float32, mybir.dt.float32r, mybir.dt.int32, mybir.dt.uint32
    ALU, ACT, AX = mybir.AluOpType, mybir.ActivationFunctionType, mybir.AxisListType
    pieces, where, tile_no = plan()
    n_pre = len(pieces)

    ctx = ExitStack()
    with ctx:
        def sb(name, width, dt=f32):
            return ctx.enter_context(nc.sbuf_tensor(name, [128, width], dt))

        A_ = sb("AREA", 15360 + SPLITS * PIECE)
        area_end = nc.sbuf_base
        X_ = sb("X", KT * T)
        H_ = sb("H", KT * T)
        h_end = nc.sbuf_base
        RAW = sb("RAW", SLOTS * PIECE)
        raw_end = nc.sbuf_base
        C = sb("CONST", CONST_W)
        PR = sb("PARAM", PARAM_W)
        MOD_ = sb("MOD", 2 * 48 * 2)
        COEF_ = sb("COEF", 2 * 4 * 16)
        SC_ = sb("SC", 16)
        SMALL = sb("SMALL", 64)
        STAT = sb("STAT", 96)
        MROW = sb("MROW", 512)
        RST = sb("RST", T)
        TMP = sb("TMP", T)
        FLAGS = sb("FLAGS", E, i32)
        def over(name, width, offset):
            return nc.alloc_sbuf_tensor_at(name, [128, width], f32r, offset=offset)

        HI = over("W_HI", SPLITS * PIECE, area_end - 4 * SPLITS * PIECE)
        LO = over("W_LO", SLOTS * PIECE, raw_end - 4 * SLOTS * PIECE)
        XH = over("XH", KT * 256, h_end - 4 * KT * T)
        XL = over("XL", KT * 256, area_end - 4 * (SPLITS * PIECE + KT * 256))
        HTH = over("HTH", 1024, area_end - 4 * (SPLITS * PIECE + KT * 256 + 1024))
        HTL = over("HTL", 1024, area_end - 4 * (SPLITS * PIECE + KT * 256 + 2048))
        PS = ctx.enter_context(nc.psum_tensor("PS", [128, BANKS, 512], f32))

        def view(t, start, *shape):
            n = int(np.prod(shape))
            v = t[:, start:start + n]
            if len(shape) == 2:
                v = v.rearrange("p (a b) -> p a b", b=shape[1])
            if len(shape) == 3:
                v = v.rearrange("p (a b c) -> p a b c", b=shape[1], c=shape[2])
            return v

        X, H = view(X_, 0, KT, T), view(H_, 0, KT, T)
        MOD = view(MOD_, 0, 2 * 48, 2)
        SC = view(SC_, 0, KT, 2)
        COEF = view(COEF_, 0, 8, 8, 2)

        def const(name):
            return C[:, CONST[name][0]:CONST[name][1]]

        def param(name, a=0, b=None):
            s, e = PARAM[name]
            return PR[:, s + a:(e if b is None else s + b)]

        IDENT, ONES, ROT = const("ident"), const("ones"), const("rot")

        GQ, GK = view(A_, 0, 2, T), view(A_, 1024, 2, T)
        GV, GR = view(A_, 2048, TT, 512), view(A_, 4096, 4, T)
        LX = view(A_, 6144, TT, 512)
        m0 = 8192
        CQ, CKV, KR = view(A_, m0, 2, T), A_[:, m0 + 1024:m0 + 1536], A_[:, m0 + 1536:m0 + 2048]
        QN, KN = view(A_, m0 + 2048, 4, T), view(A_, m0 + 4096, 4, T)
        QR, V = view(A_, m0 + 6144, 2, T), view(A_, m0 + 7168, TT, 512)
        PB = view(A_, m0 + 9216, 3, 512)
        PT = view(A_, m0 + 10752, 2, 4, 256)
        AF = view(A_, m0 + 10752, 2, T)
        LE = view(A_, m0 + 2048, TT, 512)
        SQ0 = view(A_, 0, KT, T)
        SQM = view(A_, m0 + 9216, 3, T)
        CUM = view(A_, m0, 4, T)
        EX, AA = view(A_, m0 + 2048, 2, 2 * T), view(A_, m0 + 4096, 2, 2 * T)
        ATT = view(A_, m0 + 6144, 4, T)
        KHT = view(A_, m0 + 8192, 8, 256)
        g0 = m0 + 10240
        STATES = (view(H_, 4 * T, 16, 128), view(A_, m0, 16, 128))
        QH = view(A_, g0, 4, T)
        YO = view(A_, 0, KT, T)
        SQY = view(A_, 4096, KT, T)
        FF = view(A_, 8192, FT, T)
        K1 = view(A_, 0, 8, T)
        Q1 = view(A_, 4096, 8, 256)
        V1 = view(A_, 6144, TT, D)
        E1 = view(A_, 10240, 3, 512)
        E2 = view(A_, 11776, 3, 512)
        PT1 = view(A_, 13312, 2, 4, 256)
        OD = view(A_, 15360, 8, 256)
        SQD = view(A_, 17408, 8, 256)
        YO1 = view(A_, 0, KT, 256)
        SQ1 = view(A_, 2048, KT, 256)
        HTOK = view(A_, 0, 2, D)
        HS = A_[:, 2048:3072]
        YS = A_[:, 3072:5120]
        PSEL = view(A_, 5120, 2, 256)
        PG = view(A_, 5632, 2, 256)
        GT = view(A_, 6144, 2, 256)
        SQ7 = view(A_, 2048, KT, 256)
        RT = A_[:, 7680:8192]
        ACC = view(H_, 2048, KT, 256)

        made = {}

        def sem(name):
            if name not in made:
                made[name] = ctx.enter_context(nc.semaphore(name))
            return made[name]

        loaded = [sem(f"weights_loaded_{s}") for s in range(SLOTS)]
        drained = [sem(f"bank_{b}_drained") for b in range(BANKS)]
        written = sem("tiles_written")

        def bank(name):
            return PS[:, tile_no[name] % BANKS, :]

        def wait_written(eng, name):
            eng.wait_ge(written, tile_no[name] + 1)

        def wait_drained(eng, name):
            eng.wait_ge(drained[tile_no[name] % BANKS], tile_no[name] // BANKS + 1)

        def drained_by(ins, name):
            ins.then_inc(drained[tile_no[name] % BANKS], 1)

        def banks(first, n):
            return PS[:, first:first + n, :].rearrange("p a b -> p (a b)")

        def by_block(t, blocks):
            return t[:, 0:512 * blocks].rearrange("p (n f) -> p n f", f=512)

        def slot(n):
            return RAW[:, n % SLOTS * PIECE:(n % SLOTS + 1) * PIECE]

        def wait_piece(eng, n):
            eng.wait_ge(loaded[n % SLOTS], 16 * (n // SLOTS + 1))

        def weight(label, kt):
            for n, k0, k1, cols in where[label]:
                if k0 <= kt < k1:
                    return slot(n)[:, (kt - k0) * cols:(kt - k0 + 1) * cols]

        def wait_weight(eng, label, kt):
            for n, k0, k1, cols in where[label]:
                if k0 == kt:
                    wait_piece(eng, n)

        has_state = {(0, c): c > 0 for c in range(8)} | {(1, c): c != 3 for c in range(8)}
        chunk_order = [list(range(8)), [3, 2, 1, 0, 7, 6, 5, 4]]

        def state(d, p, c):
            return STATES[d][:, p * 8 + c, :]

        block = ctx.enter_context(nc.Block())

        @block.sync
        def _(sp):
            sp.dma_start(PR[:], param_dram).then_inc(sem("param_loaded"), 16)
            for n, (_, _, k0, k1, c0, c1, _) in enumerate(pieces):
                if n >= SLOTS:
                    wait_written(sp, pieces[n - SLOTS][6])
                w = (k1 - k0) * (c1 - c0)
                sp.dma_start(slot(n)[:, 0:w], stream[n, :, 0:w]).then_inc(loaded[n % SLOTS], 16)

            def expert_pieces(n, free):
                for s in range(SLOTS):
                    free(s)
                    q = (n_pre + s) % SLOTS
                    sp.dma_start(slot(q), stream[n + s]).then_inc(loaded[q], 16)

            expert_pieces(n_pre, lambda s: wait_written(sp, pieces[n_pre - SLOTS + s][6]))
            with sp.Fori(1, E * PER_EXPERT // SLOTS) as i:
                expert_pieces(n_pre + SLOTS * i, lambda s: sp.wait_ge(sem("piece_used"), SLOTS * i + (s - SLOTS + 1)))
            sp.wait_ge(sem("out_ready"), 8)
            sp.dma_start(out_dram.rearrange("(k p) t -> p k t", p=128), X[:, :, T_CTX:T]).then_inc(sem("out_stored"), 16)
            sp.wait_ge(sem("out_stored"), 16)

        @block.tensor
        def _(pe):
            def claim(name):
                n = tile_no[name]
                if n >= BANKS:
                    pe.wait_ge(drained[n % BANKS], n // BANKS)
                return PS[:, n % BANKS, :]

            def done(ins, name):
                written_so_far[0] += 1
                assert tile_no[name] + 1 == written_so_far[0], name
                ins.then_inc(written, 1)

            written_so_far = [0]

            def mm(out, lhsT, rhs, start, stop):
                return nc.tensor.matmul(out, lhsT, rhs, start=start, stop=stop)

            def linear(name, label, cols, rhs, n, first, rows=KT, ready=None):
                b = claim(name)
                for kt in range(rows):
                    if first:
                        wait_weight(pe, label, kt)
                    if ready is not None:
                        ready(kt)
                    w = weight(label, kt)[:, cols[0]:cols[1]]
                    i = mm(b[0:cols[1] - cols[0], 0:n], w, rhs(kt), kt == 0, kt == rows - 1)
                done(i, name)

            def mod(layer, chunks):
                def rows(n):
                    wait_drained(pe, ("mod", layer, n))
                    b = claim(("modT", layer, n))
                    for j in range(4):
                        i = nc.tensor.transpose(b[:, 2 * j:2 * j + 2], MROW[0:2, 128 * j:128 * j + 128],
                                                IDENT[0:2, 0:2])
                    done(i, ("modT", layer, n))

                for n in chunks:
                    b = claim(("mod", layer, n))
                    for kt in range(KT):
                        wait_weight(pe, ("mod", layer, n), kt)
                        i = mm(b[0:2, :], SC[:, kt, :], weight(("mod", layer, n), kt), kt == 0, kt == KT - 1)
                    done(i, ("mod", layer, n))
                    if n:
                        rows(n - 1)
                if n == 11:
                    rows(n)

            def sum_squares(name, sq, n, tiles, ready):
                b = claim(name)
                for k in range(tiles):
                    ready(k)
                    i = mm(b[:, 0:n], ONES, sq(k), k == 0, k == tiles - 1)
                done(i, name)

            def norm_sum(i, sq, n):
                sum_squares(("ss", i), sq, n, KT,
                            lambda k: pe.wait_ge(sem("squares"), 4 * i + k // 2 + 1) if k % 2 == 0 else None)

            pe.wait_ge(sem("silu_c"), 1)
            pe.wait_ge(sem("const_loaded"), 16)
            mod(0, range(12))
            norm_sum(0, lambda k: SQ0[:, k, :], T)

            def h_ready(stage):
                def ready(kt):
                    pe.wait_ge(sem("h_ready"), KT * stage + kt + 1)
                return ready

            hx = lambda kt: H[:, kt, :]
            hl = lambda kt: H[:, kt, T_CTX:T]
            linear(("cq", 0), "in_a0", (0, 128), hx, T, True, ready=h_ready(0))
            linear(("cq", 1), "in_a0", (128, 256), hx, T, False)
            linear("ckv", "in_a0", (256, 384), hx, T, False)
            linear("kr", "in_a0", (384, 448), hx, T, False)
            for m in range(2):
                linear(("gq", m), "in_a1", (128 * m, 128 * m + 128), hx, T, m == 0)
            sum_squares("ssq", lambda k: SQM[:, k, :], T, 2, lambda k: pe.wait_ge(sem("mla_squares"), k + 1))
            sum_squares("sskv", lambda k: SQM[:, 2, :], T, 1, lambda k: pe.wait_ge(sem("mla_squares"), 3))
            for m in range(2):
                linear(("gk", m), "in_a1", (256 + 128 * m, 384 + 128 * m), hx, T, False)

            def token_major(name, t, label, cols, src, first, rows=KT):
                b = claim(name)
                for kt in range(rows):
                    if first:
                        wait_weight(pe, label, kt)
                    i = mm(b[:, 0:cols[1] - cols[0]], src(kt)[:, 128 * t:128 * t + 128],
                           weight(label, kt)[:, cols[0]:cols[1]], kt == 0, kt == rows - 1)
                done(i, name)

            for t in range(TT):
                token_major(("gv", t), t, "gv", (0, 512), hx, t == 0)
            for m in range(4):
                linear(("gr", m), "gr", (128 * m, 128 * m + 128), hx, T, m == 0)
            linear("af", "gaf", (0, 16), hx, T, True)
            linear("ab", "gaf", (16, 32), hx, T, False)

            pe.wait_ge(sem("lora_normed"), 3)
            for h in range(MLA_H):
                linear(("qn", h), "uq", (128 * h, 128 * h + 128), lambda k: CQ[:, k, :], T, h == 0, rows=2)
            for p in range(2):
                linear(("qr", p), "uq", (512 + 128 * p, 640 + 128 * p), lambda k: CQ[:, k, :], T, False, rows=2)
            for h in range(MLA_H):
                linear(("kn", h), "ukv", (256 * h, 256 * h + 128), lambda k: CKV, T, h == 0, rows=1)
            for t in range(TT):
                b = claim(("v", t))
                w = weight("ukv", 0).rearrange("p (h c) -> p h c", c=256)[:, :, 128:256]
                done(mm(b, CKV[:, 128 * t:128 * t + 128], w, True, True), ("v", t))
            for p in range(2):
                wait_drained(pe, ("qr", p))
                b = claim(("rotq", p))
                done(mm(b[:, 0:256], ROT, QR[:, p, T_CTX:T], True, True), ("rotq", p))
            wait_drained(pe, "kr")
            b = claim("rotk")
            done(mm(b[:, 0:256], ROT, KR[:, T_CTX:T], True, True), "rotk")

            wait_drained(pe, "af")
            wait_drained(pe, "ab")
            for t in range(TT):
                b = claim(("gx", t))
                for d in range(2):
                    i = mm(b[:, 256 * d:256 * d + 256], AF[0:16, d, 128 * t:128 * t + 128],
                           param("w_gate", 256 * d, 256 * d + 256)[0:16, :], True, True)
                done(i, ("gx", t))

            for h in range(MLA_H):
                wait_drained(pe, ("kn", h))
                wait_drained(pe, ("qn", h))
            for t in range(TT):
                wait_drained(pe, ("v", t))
            pe.wait_ge(sem("mla_roped"), 3)
            for kind, u in mla_steps():
                if kind == "s":
                    h, q, keys = u // TT, u % TT, (2 if u % TT < 2 else 4) * 128
                    r = 64 * (h % 2)
                    b = claim(("s", u))
                    mm(b[:, 0:keys], QN[:, h, 128 * q:128 * q + 128], KN[:, h, 0:keys], True, False)
                    done(mm(b[:, 0:keys], QR[r:r + 64, h // 2, 128 * q:128 * q + 128], KR[r:r + 64, 0:keys],
                            False, True), ("s", u))
                elif kind == "pT":
                    pe.wait_ge(sem("probs"), u + 1)
                    b = claim(("pT", u))
                    for k in range(2 if u % TT < 2 else 4):
                        i = nc.tensor.transpose(b[:, 128 * k:128 * k + 128], PB[:, u % 3, 128 * k:128 * k + 128], IDENT)
                    done(i, ("pT", u))
                else:
                    wait_drained(pe, ("pT", 2 * u))
                    wait_drained(pe, ("pT", 2 * u + 1))
                    b = claim(("o", u))
                    kts = 2 if u % 2 == 0 else 4
                    for k in range(kts):
                        i = mm(b[:, 0:256], V[:, k, 128 * (u // 2):128 * (u // 2) + 128], PT[:, u % 2, k, :],
                               k == 0, k == kts - 1)
                    done(i, ("o", u))

            pe.wait_ge(sem("log_decays"), 1)
            for d in range(2):
                for k in range(2):
                    b = claim(("cum", d, k))
                    for t in range(TT):
                        i = mm(b[:, 128 * t:128 * t + 128], LX[:, t, 256 * d + 128 * k:256 * d + 128 * k + 128],
                               const(("tri_f", "tri_b")[d]), True, True)
                    done(i, ("cum", d, k))

            def pairs(name, lhs, rhs):
                h = name[2]
                r = 64 * (h % 2)
                b = claim(name)
                for t in range(TT):
                    c = slice(T * (h // 2) + 128 * t, T * (h // 2) + 128 * t + 128)
                    i = mm(b[:, 128 * t:128 * t + 128], lhs[r:r + 64, c], rhs[r:r + 64, c], True, True)
                done(i, name)

            gq, gk = A_[:, 0:1024], A_[:, 1024:2048]
            for m in range(2):
                wait_drained(pe, ("gq", m))
                wait_drained(pe, ("gk", m))
            for h in range(GLA_H):
                pairs(("att", "diag", h), gk, gq)
            for d in range(2):
                pe.wait_ge(sem("decayed_keys"), d + 1)
                for t in range(TT):
                    b = claim(("kT", d, t))
                    for k in range(2):
                        i = nc.tensor.transpose(b[:, 128 * k:128 * k + 128],
                                                AA[:, d, T * k + 128 * t:T * k + 128 * t + 128], IDENT)
                    done(i, ("kT", d, t))
            for d in range(2):
                for lv in range(6):
                    pe.wait_ge(sem("level_ready"), 6 * d + lv + 1)
                    for h in range(GLA_H):
                        a = AA[:, lv % 2, :]
                        pairs(("att", (d, lv), h), a, a)
            for d in range(2):
                for t in range(TT):
                    wait_drained(pe, ("kT", d, t))
            for d in range(2):
                for p in range(2):
                    for r in range(2):
                        b = claim(("U", d, p, r))
                        for t in range(TT):
                            for hh in range(2):
                                i = mm(b[64 * hh:64 * hh + 64, 128 * t:128 * t + 128],
                                       KHT[64 * r:64 * r + 64, TT * d + t, 128 * p + 64 * hh:128 * p + 64 * hh + 64],
                                       GV[64 * r:64 * r + 64, t, 128 * (2 * p + hh):128 * (2 * p + hh) + 128],
                                       True, True)
                        done(i, ("U", d, p, r))
            for h in range(GLA_H):
                wait_drained(pe, ("att", (1, 5), h))
            pe.wait_ge(sem("decayed_queries"), 2)
            for h in range(GLA_H):
                p, r = h // 2, 64 * (h % 2)
                b = claim(("og", h))
                for d in range(2):
                    for r2 in range(2):
                        wait_drained(pe, ("U", d, p, r2))
                for t in range(TT):
                    mms = [(slice(128 * t, 128 * t + 128), GV[:, t, 128 * h:128 * h + 128],
                            ATT[:, h, 128 * t:128 * t + 128])]
                    for c in (2 * t, 2 * t + 1):
                        for d in range(2):
                            if has_state[d, c]:
                                mms.append((slice(64 * c, 64 * c + 64), state(d, p, c)[r:r + 64, :],
                                            QH[r:r + 64, 2 * d + p, 64 * c:64 * c + 64]))
                    for j, (cols, a, w) in enumerate(mms):
                        i = nc.tensor.matmul(b[:, cols], a, w, start=j == 0, stop=j == len(mms) - 1,
                                             skip_group_check=True)
                done(i, ("og", h))
            for h in range(GLA_H):
                sum_squares(("ssg", h), lambda k: EX[:, h // 2, T * (h % 2):T * (h % 2) + T], T, 1,
                            lambda k: pe.wait_ge(sem("gla_squares"), h + 1))

            for m in range(8):
                def y_ready(kt):
                    if kt < 4:
                        wait_drained(pe, ("o", 2 * kt + 1))
                    else:
                        pe.wait_ge(sem("gla_out"), kt - 3)
                linear(("ya", m), ("out_a", m // 4), (128 * (m % 4), 128 * (m % 4) + 128), hx, T, m % 4 == 0,
                       ready=y_ready if m == 0 else None)
            mod(1, range(0, 4))
            norm_sum(1, lambda k: SQY[:, k, :], T)
            mod(1, range(4, 8))
            norm_sum(2, lambda k: SQY[:, k, :], T)
            for m in range(FT):
                c = (128 * (m % 4), 128 * (m % 4) + 128)
                linear(("g", m), ("fg", m // 4), c, hx, T, m % 4 == 0, ready=h_ready(1) if m == 0 else None)
                linear(("u", m), ("fu", m // 4), c, hx, T, m % 4 == 0)
            for m in range(8):
                linear(("yf", m), ("fd", m), (0, 128), lambda k: FF[:, k, :], T, True, rows=FT,
                       ready=(lambda k: wait_drained(pe, ("u", k))) if m == 0 else None)
            mod(1, range(8, 12))
            norm_sum(3, lambda k: SQY[:, k, :], T)

            norm_sum(4, lambda k: SQY[:, k, :], T)
            for m in range(16):
                c = (128 * (m % 4), 128 * (m % 4) + 128)
                linear(("qk", m), ("qk", m // 4), c, hl if m < 8 else hx, 256 if m < 8 else T, m % 4 == 0,
                       ready=h_ready(2) if m == 0 else None)
            for n in range(2):
                for t in range(TT):
                    token_major(("v1", t, n), t, ("v1", n), (0, 512), hx, t == 0)
            for m in range(8):
                wait_drained(pe, ("qk", m))
                wait_drained(pe, ("qk", 8 + m))
                b = claim(("rot", m))
                mm(b[:, 0:256], ROT, Q1[:, m, :], True, True)
                done(mm(b[:, 256:512], ROT, K1[:, m, T_CTX:T], True, True), ("rot", m))
            for n in range(2):
                for t in range(TT):
                    wait_drained(pe, ("v1", t, n))
            for kind, u in diff_steps():
                if kind in ("s1", "s2"):
                    h, q = u // 2, u % 2
                    r = 0 if kind == "s1" else 64
                    pe.wait_ge(sem("diff_roped"), h + 1)
                    b = claim((kind, u))
                    done(mm(b, Q1[r:r + 64, h, 128 * q:128 * q + 128], K1[r:r + 64, h, :], True, True), (kind, u))
                elif kind == "dT":
                    pe.wait_ge(sem("diff_probs"), u + 1)
                    b = claim(("dT", u))
                    for k in range(TT):
                        i = nc.tensor.transpose(b[:, 128 * k:128 * k + 128], E1[:, u % 3, 128 * k:128 * k + 128], IDENT)
                    done(i, ("dT", u))
                else:
                    wait_drained(pe, ("dT", 2 * u))
                    wait_drained(pe, ("dT", 2 * u + 1))
                    b = claim(("do", u))
                    for k in range(TT):
                        i = mm(b[:, 0:256], V1[:, k, 128 * u:128 * u + 128], PT1[:, u % 2, k, :], k == 0, k == 3)
                    done(i, ("do", u))
            for h in range(DIFF_H):
                sum_squares(("ssd", h), lambda k: SQD[:, h, :], 256, 1,
                            lambda k: pe.wait_ge(sem("diff_squares"), h + 1))
            for m in range(8):
                linear(("yc", m), ("out_c", m // 4), (128 * (m % 4), 128 * (m % 4) + 128), hl, 256, m % 4 == 0,
                       ready=(lambda k: pe.wait_ge(sem("diff_out"), k + 1)) if m == 0 else None)
            norm_sum(5, lambda k: SQ1[:, k, :], 256)
            norm_sum(6, lambda k: SQ1[:, k, :], 256)

            for t in range(2):
                b = claim(("lg", t))
                for kt in range(KT):
                    if t == 0:
                        h_ready(3)(kt)
                    i = mm(b[:, 0:E], H[:, kt, T_CTX + 128 * t:T_CTX + 128 * t + 128],
                           param("router", 8 * kt, 8 * kt + 8), kt == 0, kt == KT - 1)
                done(i, ("lg", t))
            for t in range(2):
                for n in range(2):
                    b = claim(("ht", t, n))
                    for j in range(4):
                        i = nc.tensor.transpose(b[:, 128 * j:128 * j + 128],
                                                H[:, 4 * n + j, T_CTX + 128 * t:T_CTX + 128 * t + 128], IDENT)
                    done(i, ("ht", t, n))
            pe.wait_ge(sem("selected"), 1)
            sel = lambda t: RT[:, 64 + 8 * t:72 + 8 * t]
            b = claim(("pos", 0))
            done(mm(b[:, 0:E], const("before"), sel(0), True, True), ("pos", 0))
            b = claim(("pos", 1))
            mm(b[:, 0:E], const("before"), sel(1), True, False)
            done(mm(b[:, 0:E], ONES, sel(0), False, True), ("pos", 1))
            b = claim("cnt")
            mm(b[:, 0:E], ONES, sel(0), True, False)
            done(mm(b[:, 0:E], ONES, sel(1), False, True), "cnt")
            for t in range(2):
                for n in range(2):
                    wait_drained(pe, ("ht", t, n))
            wait_drained(pe, ("pos", 1))
            wait_drained(pe, "cnt")

            def three(out, a, b, first, last):
                mm(out, a[0], b[0], first, False)
                mm(out, a[0], b[1], False, False)
                return mm(out, a[1], b[0], False, last)

            def transposed_hidden(e, c, blocks):
                pe.wait_ge(sem("hidden"), EC * e + c + 1)
                for n in range(blocks):
                    for j in range(4):
                        i = nc.tensor.transpose(PS[:, 2 + n, 128 * j:128 * j + 128],
                                                HS[:, 512 * n + 128 * j:512 * n + 128 * j + 128], IDENT)
                i.then_inc(sem("hidden_T"), 1)

            def expert(e, blocks):
                for kt in range(KT):
                    s = 128 * blocks * kt
                    for t in range(2):
                        i = mm(PS[:, s // 512, s % 512:s % 512 + 128 * blocks], HTOK[:, t, 128 * kt:128 * kt + 128],
                               PSEL[:, t, 0:128 * blocks], t == 0, t == 1)
                i.then_inc(sem("gathered"), 1)
                pe.wait_ge(sem("x_lo"), e + 1)
                for kind, c, j in expert_order():
                    if kind == "u" and c:
                        pe.wait_ge(sem("ht_lo"), EC * e + c)
                    if kind == "d" and c == EC - 1:
                        transposed_hidden(e, c, blocks)
                        pe.wait_ge(sem("ht_lo"), EC * e + c + 1)
                    for half in range(2):
                        q = j + half
                        h0 = q % SPLITS * PIECE
                        l0 = (n_pre + q) % SLOTS * PIECE
                        pe.wait_ge(sem("lo_made"), PER_EXPERT * e + q + 1)
                        for i in range(4):
                            for n in range(blocks):
                                if kind in "gu":
                                    kt, w = 4 * half + i, 512 * i
                                    out = PS[:, 2 * (kind == "u") + n, :]
                                    x = slice(128 * (blocks * kt + n), 128 * (blocks * kt + n) + 128)
                                    a, first, end = (XH[:, x], XL[:, x]), kt == 0, kt == KT - 1
                                else:
                                    ft, w = 2 * half + i // 2, 512 * i
                                    out = PS[:, 4 + 2 * n + i % 2, :]
                                    x = slice(512 * n + 128 * ft, 512 * n + 128 * ft + 128)
                                    a, first, end = (HTH[:, x], HTL[:, x]), c == 0 and ft == 0, c == EC - 1 and ft == 3
                                last = three(out, a, (HI[:, h0 + w:h0 + w + 512], LO[:, l0 + w:l0 + w + 512]), first, end)
                        last.then_inc(sem("piece_used"), 1)
                    if kind == "u" and c == 0:
                        pe.wait_ge(sem("acc_done"), 4 * e + 1)
                        pe.wait_ge(sem("onehots"), e + 1)
                        for n in range(blocks):
                            for t in range(2):
                                i = nc.tensor.transpose(PS[:, 7, 256 * n + 128 * t:256 * n + 128 * t + 128],
                                                        PG[:, t, 128 * n:128 * n + 128], IDENT)
                        i.then_inc(sem("gt_written"), 1)
                        transposed_hidden(e, 0, blocks)
                        pe.wait_ge(sem("gt_copied"), e + 1)
                    if kind == "d" and c < EC - 2:
                        transposed_hidden(e, c + 1, blocks)
                pe.wait_ge(sem("y_copied"), e + 1)
                for kt in range(KT):
                    for n in range(blocks):
                        i = mm(PS[:, 4 + kt // 2, 256 * (kt % 2):256 * (kt % 2) + 256],
                               YS[:, D * n + 128 * kt:D * n + 128 * kt + 128], GT[:, n, :], n == 0, n == blocks - 1)
                    if kt % 2:
                        i.then_inc(sem("scattered"), 1)

            pe.wait_ge(sem("flags_ready"), 1)
            pe.wait_ge(sem("selection"), 1)
            with pe.Fori(0, E) as e:
                flag = pe.value_load(FLAGS[0:1, bass.ds(e, 1)], min_val=0, max_val=1)
                pe.wait_ge(sem("selection"), e + 1)
                with pe.If(flag > 0):
                    expert(e, 2)
                with pe.Else():
                    expert(e, 1)
            pe.wait_ge(sem("moe_squares"), 1)
            for kt in range(KT):
                i = mm(PS[:, 0, 0:256], ONES, SQ7[:, kt, :], kt == 0, kt == KT - 1)
            i.then_inc(sem("moe_sum"), 1)

        @block.scalar
        def _(act):
            count = {}

            def act_do(name, out, in_, func, **kw):
                count[name] = count.get(name, 0) + 1
                nc.scalar.activation(out, in_, func, **kw).then_inc(sem(name), 1)
                act.wait_ge(sem(name), count[name])

            act.dma_start(C[:], const_dram).then_inc(sem("const_loaded"), 16)
            act.dma_start(X, x_dram.rearrange("(k p) t -> p k t", p=128)).then_inc(sem("x_loaded"), 16)
            act.wait_ge(sem("param_loaded"), 16)
            nc.scalar.activation(SC_[:], param("c"), ACT.Silu).then_inc(sem("silu_c"), 1)

            def mod(layer, chunks):
                for n in chunks:
                    wait_written(act, ("mod", layer, n))
                    if n or layer:
                        wait_written(act, ("modT", layer, n - 1) if n else ("modT", 0, 11))
                    drained_by(nc.scalar.activation(MROW[0:2, :], bank(("mod", layer, n))[0:2, :], ACT.Copy),
                               ("mod", layer, n))

            def root(out, n):
                k = 5 + (D, Q_RANK, 2 * DIFF_D).index(n)
                nc.scalar.activation(out, out, ACT.Sqrt, bias=SMALL[:, k:k + 1]).then_inc(sem("rooted"), 1)

            def root_of(name, n, w):
                wait_written(act, name)
                root(bank(name)[:, 0:w], n)

            def squares(src, dst, lo, hi, ready=None):
                for j in range(4):
                    if ready is not None:
                        ready(j)
                    nc.scalar.activation(dst[:, 2 * j:2 * j + 2, :], src[:, 2 * j:2 * j + 2, lo:hi],
                                         ACT.Square).then_inc(sem("squares"), 1)

            def modulate(layer, which, stage, streams):
                act.wait_ge(sem("coefs"), layer + 1)
                seg = 0 if which == 0 else 3
                for kt in range(KT):
                    if kt % 2 == 0:
                        act.wait_ge(sem("x_scaled"), 4 * stage + kt // 2 + 1)
                    for s in streams:
                        h = H[:, kt, 256 * s:256 * s + 256]
                        i = nc.scalar.activation(h, h, ACT.Identity, scale=COEF[:, 4 * layer + which, kt, s:s + 1],
                                                 bias=MOD[:, 48 * layer + 8 * seg + kt, s:s + 1])
                    i.then_inc(sem("h_ready"), 1)

            def copy_out(name, dst, src=None, func=ACT.Copy, **kw):
                wait_written(act, name)
                drained_by(nc.scalar.activation(dst, bank(name) if src is None else src, func, **kw), name)

            act.wait_ge(sem("x_loaded"), 16)
            squares(X, SQ0, 0, T)
            mod(0, range(12))
            act.wait_ge(sem("eps_ready"), 3)
            root_of(("ss", 0), D, T)
            modulate(0, 0, 0, (0, 1))

            copy_out(("cq", 0), CQ[:, 0, :])
            copy_out(("cq", 1), CQ[:, 1, :])
            copy_out("ckv", CKV)
            wait_written(act, "kr")
            nc.scalar.activation(KR[0:64, :], bank("kr")[0:64, :], ACT.Copy)
            drained_by(nc.scalar.activation(KR[64:128, :], bank("kr")[0:64, :], ACT.Copy), "kr")
            for m, src in enumerate((CQ[:, 0, :], CQ[:, 1, :], CKV)):
                wait_drained(act, (("cq", 0), ("cq", 1), "ckv")[m])
                nc.scalar.activation(SQM[:, m, :], src, ACT.Square).then_inc(sem("mla_squares"), 1)
            for m in range(2):
                copy_out(("gq", m), GQ[:, m, :], scale=DK ** -0.5)
            root_of("ssq", Q_RANK, T)
            root_of("sskv", KV_RANK, T)
            for m in range(2):
                copy_out(("gk", m), GK[:, m, :])
            for t in range(TT):
                copy_out(("gv", t), GV[:, t, :])
            for m in range(4):
                copy_out(("gr", m), GR[:, m, :], func=ACT.Silu)
            for h in range(MLA_H):
                copy_out(("qn", h), QN[:, h, :])
            for h in range(MLA_H):
                copy_out(("kn", h), KN[:, h, :])

            def attend(steps):
                for kind, u in steps:
                    if kind == "s":
                        keys = (2 if u % TT < 2 else 4) * 128
                        act.wait_ge(sem("mla_max"), u + 1)
                        if u >= 3:
                            wait_written(act, ("pT", u - 3))
                        drained_by(nc.scalar.activation(PB[:, u % 3, 0:keys], bank(("s", u))[:, 0:keys], ACT.Exp,
                                                        bias=STAT[:, u:u + 1], scale=MLA_SCALE,
                                                        accum_out=STAT[:, 32 + u:33 + u]), ("s", u))
                    elif kind == "pT":
                        n = 2 if u % TT < 2 else 4
                        g, q = u // 2, u % 2
                        if g >= 2:
                            wait_written(act, ("o", g - 2))
                        copy_out(("pT", u), PT[:, g % 2, 0:n, 128 * q:128 * q + 128],
                                 bank(("pT", u))[:, 0:128 * n].rearrange("p (k q) -> p k q", q=128))
                    elif kind in ("s1", "s2"):
                        j = kind == "s2"
                        act.wait_ge(sem("diff_max"), 2 * u + j + 1)
                        if u >= 3:
                            wait_written(act, ("dT", u - 3))
                        drained_by(nc.scalar.activation((E2 if j else E1)[:, u % 3, :], bank((kind, u)), ACT.Exp,
                                                        bias=STAT[:, 16 * j + u:16 * j + u + 1], scale=DIFF_SCALE,
                                                        accum_out=STAT[:, 32 + 16 * j + u:33 + 16 * j + u]), (kind, u))
                    elif kind == "dT":
                        g, q = u // 2, u % 2
                        if g >= 2:
                            wait_written(act, ("do", g - 2))
                        copy_out(("dT", u), PT1[:, g % 2, :, 128 * q:128 * q + 128],
                                 bank(("dT", u)).rearrange("p (k q) -> p k q", q=128))
                    elif kind == "do":
                        wait_written(act, ("do", u))
                        nc.scalar.activation(SQD[:, u, :], bank(("do", u))[:, 0:256],
                                             ACT.Square).then_inc(sem("diff_squares"), 1)

            attend(mla_steps())

            act.wait_ge(sem("gate_abs"), 1)
            act_do("act_gate", LE, LE, ACT.Exp)
            act.wait_ge(sem("gate_plus"), 1)
            act_do("act_gate", LE, LE, ACT.Ln)
            for d in range(2):
                for k in range(2):
                    copy_out(("cum", d, k), CUM[:, 2 * d + k, :])
            for d in range(2):
                for k in range(2):
                    wait_drained(act, ("cum", d, k))
                nc.scalar.activation(QH[:, 2 * d:2 * d + 2, :], CUM[:, 2 * d:2 * d + 2, :],
                                     ACT.Exp).then_inc(sem("decay_exp"), 1)
                act.wait_ge(sem("key_exponents"), d + 1)
                nc.scalar.activation(EX[:, d, :], EX[:, d, :], ACT.Exp).then_inc(sem("key_exp"), 1)
                edge = 63 if d == 0 else 0
                nc.scalar.activation(STAT[:, 64 + 16 * d:80 + 16 * d].rearrange("p (k c) -> p k c", c=8),
                                     CUM[:, 2 * d:2 * d + 2, edge::CHUNK], ACT.Exp).then_inc(sem("chunk_decay"), 1)
            for t in range(2 * TT):
                name = ("kT", t // TT, t % TT)
                copy_out(name, KHT[:, t, :], bank(name)[:, 0:256])
            for n in range(12):
                act.wait_ge(sem("level_exponents"), n + 1)
                nc.scalar.activation(EX[:, n % 2, :], EX[:, n % 2, :], ACT.Exp).then_inc(sem("level_exp"), 1)
            for h in range(GLA_H):
                wait_written(act, ("og", h))
                nc.scalar.activation(EX[:, h // 2, T * (h % 2):T * (h % 2) + T], bank(("og", h)),
                                     ACT.Square).then_inc(sem("gla_squares"), 1)
            for h in range(GLA_H):
                root_of(("ssg", h), DV, T)

            for m in range(8):
                copy_out(("ya", m), YO[:, m, :])
            for m in range(8):
                wait_drained(act, ("ya", m))
            squares(YO, SQY, 0, T)
            mod(1, range(0, 4))
            root_of(("ss", 1), D, T)

            def x_ready(base):
                return lambda j: act.wait_ge(sem("x_ready"), base + 2 * j + 2)

            squares(X, SQY, 0, T, x_ready(0))
            mod(1, range(4, 8))
            root_of(("ss", 2), D, T)
            modulate(0, 2, 1, (0, 1))
            for m in range(FT):
                wait_written(act, ("g", m))
                drained_by(nc.scalar.activation(FF[:, m, :], bank(("g", m)), ACT.Silu), ("g", m))
            for m in range(8):
                copy_out(("yf", m), YO[:, m, :])
            for m in range(8):
                wait_drained(act, ("yf", m))
            squares(YO, SQY, 0, T)
            mod(1, range(8, 12))
            root_of(("ss", 3), D, T)
            squares(X, SQY, 0, T, x_ready(8))
            root_of(("ss", 4), D, T)
            modulate(1, 0, 2, (0, 1))
            for m in range(16):
                if m < 8:
                    copy_out(("qk", m), Q1[:, m, :], bank(("qk", m))[:, 0:256])
                else:
                    copy_out(("qk", m), K1[:, m - 8, :])
            act.wait_ge(sem("lam_logits"), 1)
            act_do("lam_exp", SMALL[:, 8:10], SMALL[:, 8:10], ACT.Exp)
            attend(diff_steps())
            for h in range(DIFF_H):
                root_of(("ssd", h), 2 * DIFF_D, 256)
            for m in range(8):
                copy_out(("yc", m), YO1[:, m, :], bank(("yc", m))[:, 0:256])
            for m in range(8):
                wait_drained(act, ("yc", m))
            squares(YO1, SQ1, 0, 256)
            root_of(("ss", 5), D, 256)
            squares(X, SQ1, T_CTX, T, x_ready(16))
            root_of(("ss", 6), D, 256)
            modulate(1, 2, 3, (1,))
            for t in range(2):
                for n in range(2):
                    copy_out(("ht", t, n), HTOK[:, t, 512 * n:512 * n + 512])
            act.wait_ge(sem("gate_logits"), 1)
            act_do("gate_exp", RT[:, 40:42], RT[:, 40:42], ACT.Exp)

            def expert(e, blocks):
                def split(q):
                    n = n_pre + q
                    act.wait_ge(loaded[n % SLOTS], 16 * (6 * e + (n // SLOTS + 1)))
                    if q >= SPLITS:
                        act.wait_ge(sem("piece_used"), PER_EXPERT * e + (q - SPLITS + 1))
                    nc.scalar.activation(HI[:, q % SPLITS * PIECE:(q % SPLITS + 1) * PIECE], slot(n),
                                         ACT.Copy).then_inc(sem("hi_made"), 1)

                split(0)
                split(1)
                act.wait_ge(sem("gathered"), e + 1)
                nc.scalar.activation(XH[:, 0:1024 * blocks], banks(0, 2 * blocks), ACT.Copy).then_inc(sem("x_hi"), 1)
                for kind, c in vector_order():
                    if kind == "split" and c > 1:
                        split(c)
                    elif kind == "scatter_matrix":
                        act.wait_ge(sem("gt_written"), e + 1)
                        nc.scalar.activation(GT[:, 0:blocks, :].rearrange("p n t -> p (n t)"),
                                             PS[:, 7, 0:256 * blocks], ACT.Copy).then_inc(sem("gt_copied"), 1)
                    elif kind == "hidden":
                        act.wait_ge(sem("piece_used"), PER_EXPERT * e + piece_of("u", c) + 2)
                        nc.scalar.activation(by_block(HS, blocks), PS[:, 0:blocks, :],
                                             ACT.Silu).then_inc(sem("silu"), 1)
                    elif kind == "transposed":
                        act.wait_ge(sem("hidden_T"), EC * e + c + 1)
                        nc.scalar.activation(by_block(HTH, blocks), PS[:, 2:2 + blocks, :],
                                             ACT.Copy).then_inc(sem("ht_hi"), 1)
                act.wait_ge(sem("piece_used"), PER_EXPERT * e + PER_EXPERT)
                nc.scalar.activation(YS[:, 0:1024 * blocks], banks(4, 2 * blocks), ACT.Copy).then_inc(sem("y_copied"), 1)

            act.wait_ge(sem("flags_ready"), 1)
            with act.Fori(0, E) as e:
                flag = act.value_load(FLAGS[0:1, bass.ds(e, 1)], min_val=0, max_val=1)
                with act.If(flag > 0):
                    expert(e, 2)
                with act.Else():
                    expert(e, 1)
            act.wait_ge(sem("moe_sum"), 1)
            root(PS[:, 0, 0:256], D)

        @block.vector
        def _(dve):
            count = {}
            V_ = nc.vector

            def do(ins, name="dve_step"):
                count[name] = count.get(name, 0) + 1
                ins.then_inc(sem(name), 1)
                dve.wait_ge(sem(name), count[name])

            def drain(ins, name):
                drained_by(ins, name)
                wait_drained(dve, name)

            def mod(layer, chunks):
                for n in chunks:
                    wait_written(dve, ("modT", layer, n))
                    b = bank(("modT", layer, n))[:, 0:8].rearrange("p (m s) -> p m s", s=2)
                    bias = param("b_mod", 48 * layer + 4 * n, 48 * layer + 4 * n + 4).unsqueeze(2)
                    drain(V_.tensor_tensor(MOD[:, 48 * layer + 4 * n:48 * layer + 4 * n + 4, :], b,
                                           bias.to_broadcast([128, 4, 2]), ALU.add), ("modT", layer, n))

            def coefs(layer):
                for which, (seg, gain, one) in enumerate(((1, "g_pre_mix", 1.0), (2, "g_post_mix", 0.0),
                                                          (4, "g_pre_ffn", 1.0), (5, "g_post_ffn", 0.0))):
                    c = COEF[:, 4 * layer + which, :, :]
                    m = MOD[:, 48 * layer + 8 * seg:48 * layer + 8 * seg + 8, :]
                    g = param(gain, 8 * layer, 8 * layer + 8).unsqueeze(2).to_broadcast([128, 8, 2])
                    do(V_.tensor_scalar(c, m, one, math.sqrt(D), ALU.add, ALU.mult))
                    do(V_.tensor_tensor(c, c, g, ALU.mult), "dve_step" if which < 3 else "coefs")

            def rstd(name, out, n, width):
                count["rooted"] = count.get("rooted", 0) + 1
                dve.wait_ge(sem("rooted"), count["rooted"])
                drain(V_.reciprocal(out, bank(name)[:, 0:width]), name)

            def scaled(i, src, lo, hi):
                w = hi - lo
                rstd(("ss", i), RST[:, 0:w], D, w)
                for j in range(4):
                    V_.tensor_tensor(H[:, 2 * j:2 * j + 2, lo:hi], src[:, 2 * j:2 * j + 2, lo:hi],
                                     RST[:, 0:w].unsqueeze(1).to_broadcast([128, 2, w]),
                                     ALU.mult).then_inc(sem("x_scaled"), 1)

            def residual(i, y, layer, which, streams, ready="x_ready"):
                w = 256 * len(streams)
                if i is not None:
                    rstd(("ss", i), RST[:, 0:w], D, w)
                for j in range(4):
                    do(V_.tensor_tensor(y[:, 2 * j:2 * j + 2, 0:w], y[:, 2 * j:2 * j + 2, 0:w],
                                        RST[:, 0:w].unsqueeze(1).to_broadcast([128, 2, w]), ALU.mult))
                dve.wait_ge(sem("coefs"), layer + 1)
                for kt in range(KT):
                    for n, s in enumerate(streams):
                        x = X[:, kt, 256 * s:256 * s + 256]
                        ins = V_.scalar_tensor_tensor(x, y[:, kt, 256 * n:256 * n + 256],
                                                      COEF[:, 4 * layer + which, kt, s:s + 1], x, ALU.mult, ALU.add)
                    ins.then_inc(sem(ready), 1)
                    count[ready] = count.get(ready, 0) + 1
                dve.wait_ge(sem(ready), count[ready])

            for j, n in enumerate((D, Q_RANK, 2 * DIFF_D)):
                do(V_.memset(SMALL[:, 5 + j:6 + j], n * EPS), "eps_ready")
            dve.wait_ge(sem("param_loaded"), 16)
            for a, b, name, f in ((0, 2, "g_q", math.sqrt(Q_RANK)), (2, 3, "g_kv", math.sqrt(KV_RANK)),
                                  (3, 4, "g_gla", math.sqrt(DV)), (4, 5, "g_diff", math.sqrt(2 * DIFF_D) * (1.0 - LAM_INIT))):
                do(V_.tensor_scalar(SMALL[:, a:b], param(name), f, None, ALU.mult))
            for j, (a, b) in enumerate((("lq1", "lk1"), ("lq2", "lk2"))):
                do(V_.tensor_tensor(TMP[:, 0:64], param(a), param(b), ALU.mult))
                do(V_.reduce_sum(SMALL[:, 8 + j:9 + j], TMP[:, 0:64], axis=AX.X), ("dve_step", "lam_logits")[j])
            mod(0, range(12))
            coefs(0)
            scaled(0, X, 0, T)

            for name, parts in (("ssq", ((CQ[:, 0, :], 0), (CQ[:, 1, :], 1))), ("sskv", ((CKV, 2),))):
                rstd(name, RST[:], Q_RANK if name == "ssq" else KV_RANK, T)
                dve.wait_ge(sem("mla_squares"), 3)
                for part, g in parts:
                    do(V_.scalar_tensor_tensor(part, part, SMALL[:, g:g + 1], RST[:], ALU.mult, ALU.mult), "lora_normed")
            for d, name in enumerate(("af", "ab")):
                wait_written(dve, name)
                drain(V_.tensor_copy(AF[0:16, d, :], bank(name)[0:16, :]), name)
            for p in range(2):
                wait_written(dve, ("qr", p))
                drain(V_.tensor_copy(QR[:, p, :], bank(("qr", p))), ("qr", p))
            for t in range(TT):
                wait_written(dve, ("v", t))
                drain(V_.tensor_copy(V[:, t, :], bank(("v", t))), ("v", t))
            for name, x in ((("rotq", 0), QR[:, 0, T_CTX:T]), (("rotq", 1), QR[:, 1, T_CTX:T]), ("rotk", KR[:, T_CTX:T])):
                wait_written(dve, name)
                drain(V_.tensor_tensor(TMP[:, 0:256], bank(name)[:, 0:256], const("sin"), ALU.mult), name)
                do(V_.tensor_tensor(x, x, const("cos"), ALU.mult))
                do(V_.tensor_tensor(x, x, TMP[:, 0:256], ALU.add), "mla_roped")
            for t in range(TT):
                wait_written(dve, ("gx", t))
                drain(V_.tensor_tensor(LX[:, t, :], bank(("gx", t)), param("b_gate"), ALU.add), ("gx", t))

            def attend(steps):
                for kind, u in steps:
                    if kind == "s":
                        keys = (2 if u % TT < 2 else 4) * 128
                        wait_written(dve, ("s", u))
                        do(V_.reduce_max(STAT[:, u:u + 1], bank(("s", u))[:, 0:keys], axis=AX.X))
                        do(V_.tensor_scalar(STAT[:, u:u + 1], STAT[:, u:u + 1], -MLA_SCALE, None, ALU.mult), "mla_max")
                    elif kind == "pT":
                        keys = (2 if u % TT < 2 else 4) * 128
                        wait_drained(dve, ("s", u))
                        do(V_.reciprocal(STAT[:, 32 + u:33 + u], STAT[:, 32 + u:33 + u]))
                        do(V_.tensor_scalar(PB[:, u % 3, 0:keys], PB[:, u % 3, 0:keys], STAT[:, 32 + u:33 + u], None,
                                            ALU.mult), "probs")
                    elif kind == "o":
                        wait_written(dve, ("o", u))
                        drain(V_.tensor_copy(H[:, u // 2, 256 * (u % 2):256 * (u % 2) + 256], bank(("o", u))[:, 0:256]),
                              ("o", u))
                    elif kind in ("s1", "s2"):
                        j = kind == "s2"
                        c = 16 * j + u
                        wait_written(dve, (kind, u))
                        do(V_.reduce_max(STAT[:, c:c + 1], bank((kind, u)), axis=AX.X))
                        do(V_.tensor_scalar(STAT[:, c:c + 1], STAT[:, c:c + 1], -DIFF_SCALE, None, ALU.mult), "diff_max")
                    elif kind == "dT":
                        wait_drained(dve, ("s1", u))
                        wait_drained(dve, ("s2", u))
                        do(V_.reciprocal(STAT[:, 32 + u:33 + u], STAT[:, 32 + u:33 + u]))
                        do(V_.reciprocal(STAT[:, 48 + u:49 + u], STAT[:, 48 + u:49 + u]))
                        do(V_.tensor_scalar(E2[:, u % 3, :], E2[:, u % 3, :], STAT[:, 48 + u:49 + u], SMALL[:, 10:11],
                                            ALU.mult, ALU.mult))
                        do(V_.scalar_tensor_tensor(E1[:, u % 3, :], E1[:, u % 3, :], STAT[:, 32 + u:33 + u],
                                                   E2[:, u % 3, :], ALU.mult, ALU.subtract), "diff_probs")
                    elif kind == "do":
                        dve.wait_ge(sem("diff_squares"), u + 1)
                        drain(V_.tensor_copy(OD[:, u, :], bank(("do", u))[:, 0:256]), ("do", u))

            attend(mla_steps())

            do(V_.scalar_tensor_tensor(LE, LX, -1.0, LX, ALU.mult, ALU.min), "gate_abs")
            dve.wait_ge(sem("act_gate"), 1)
            do(V_.tensor_scalar(LE, LE, 1.0, None, ALU.add), "gate_plus")
            dve.wait_ge(sem("act_gate"), 2)
            do(V_.scalar_tensor_tensor(LX, LX, 0.0, LE, ALU.min, ALU.subtract), "log_decays")

            def cum_of(d, k):
                return CUM[:, 2 * d + k, :].rearrange("p (c i) -> p c i", i=CHUNK)

            for h in range(GLA_H):
                wait_written(dve, ("att", "diag", h))
                a = ATT[:, h, :].rearrange("p (c t) -> p c t", t=128)
                drained_by(V_.tensor_tensor(a, bank(("att", "diag", h)).rearrange("p (c t) -> p c t", t=128),
                                            const("diag2").unsqueeze(1).to_broadcast([128, TT, 128]), ALU.mult),
                           ("att", "diag", h))
            for h in range(GLA_H):
                wait_drained(dve, ("att", "diag", h))
            for d in range(2):
                for k in range(2):
                    wait_drained(dve, ("cum", d, k))
                    edge = 63 if d == 0 else 0
                    last = cum_of(d, k)[:, :, edge:edge + 1].to_broadcast([128, 8, CHUNK])
                    do(V_.tensor_tensor(EX[:, d, T * k:T * k + T].rearrange("p (c i) -> p c i", i=CHUNK), last,
                                        cum_of(d, k), ALU.subtract), ("dve_step", "key_exponents")[k])
                dve.wait_ge(sem("decay_exp"), d + 1)
                do(V_.tensor_tensor(QH[:, 2 * d:2 * d + 2, :], QH[:, 2 * d:2 * d + 2, :], GQ, ALU.mult), "decayed_queries")
                dve.wait_ge(sem("key_exp"), d + 1)
                do(V_.tensor_tensor(AA[:, d, :], EX[:, d, :], A_[:, 1024:2048], ALU.mult), "decayed_keys")

            def exponents(n):
                d, m = n // 6, LEVELS[n % 6]
                cum = A_[:, m0 + 1024 * d:m0 + 1024 * d + 1024].rearrange("p (b u m) -> p b u m", u=2, m=m)
                ex = EX[:, n % 2, :].rearrange("p (b u m) -> p b u m", u=2, m=m)
                nb = 2 * T // (2 * m)
                ref = (cum[:, :, 0, m - 1:m] if d == 0 else cum[:, :, 1, 0:1]).to_broadcast([128, nb, m])
                qh = 1 - d
                V_.tensor_tensor(ex[:, :, qh, :], cum[:, :, qh, :], ref, ALU.subtract)
                do(V_.tensor_tensor(ex[:, :, 1 - qh, :], ref, cum[:, :, 1 - qh, :], ALU.subtract), "level_exponents")

            def decayed(n):
                d, m = n // 6, LEVELS[n % 6]
                qh = 1 - d
                blocks = lambda a: a.rearrange("p (b u m) -> p b u m", u=2, m=m)
                dve.wait_ge(sem("level_exp"), n + 1)
                if n < 2:
                    for t in range(TT):
                        wait_written(dve, ("kT", n, t))
                else:
                    wait_written(dve, ("att", ((n - 2) // 6, (n - 2) % 6), 3))
                V_.tensor_tensor(blocks(AA[:, n % 2, :])[:, :, qh, :], blocks(EX[:, n % 2, :])[:, :, qh, :],
                                 blocks(A_[:, 0:1024])[:, :, qh, :], ALU.mult)
                do(V_.tensor_tensor(blocks(AA[:, n % 2, :])[:, :, 1 - qh, :], blocks(EX[:, n % 2, :])[:, :, 1 - qh, :],
                                    blocks(A_[:, 1024:2048])[:, :, 1 - qh, :], ALU.mult), "level_ready")

            def add_scores(n):
                mask = C[:, CONST["masks"][0] + 128 * n:CONST["masks"][0] + 128 * n + 128].bitcast(u32)
                for h in range(GLA_H):
                    name = ("att", (n // 6, n % 6), h)
                    wait_written(dve, name)
                    drained_by(V_.copy_predicated(ATT[:, h, :].rearrange("p (c t) -> p c t", t=128),
                                                  mask.unsqueeze(1).to_broadcast([128, TT, 128]),
                                                  bank(name).rearrange("p (c t) -> p c t", t=128)), name)
                for h in range(GLA_H):
                    wait_drained(dve, ("att", (n // 6, n % 6), h))

            exponents(0)
            exponents(1)
            for n in range(12):
                decayed(n)
                if n + 2 < 12:
                    exponents(n + 2)
                add_scores(n)
            for d in range(2):
                dve.wait_ge(sem("chunk_decay"), d + 1)
            for d in range(2):
                for p in range(2):
                    left = [c for c in chunk_order[d]][:-1]
                    lasts = {r: [c for c in left if c % 2 == r][-1] for r in range(2)}
                    for r in range(2):
                        wait_written(dve, ("U", d, p, r))
                    for j, c in enumerate(left):
                        nxt = chunk_order[d][j + 1]
                        name = ("U", d, p, c % 2)
                        u = bank(name)[:, 128 * (c // 2):128 * (c // 2) + 128]
                        if j == 0:
                            ins = V_.tensor_copy(state(d, p, nxt), u)
                        else:
                            k = 64 + 16 * d + 8 * p + c
                            ins = V_.scalar_tensor_tensor(state(d, p, nxt), state(d, p, c), STAT[:, k:k + 1], u,
                                                          ALU.mult, ALU.add)
                        if lasts[c % 2] == c:
                            drain(ins, name)
                        else:
                            do(ins, "states_step")
            for h in range(GLA_H):
                dve.wait_ge(sem("gla_squares"), h + 1)
                drain(V_.tensor_copy(AA[:, h // 2, T * (h % 2):T * (h % 2) + T], bank(("og", h))), ("og", h))
            for h in range(GLA_H):
                rstd(("ssg", h), RST[:], DV, T)
                y = H[:, 4 + h, :]
                do(V_.scalar_tensor_tensor(y, AA[:, h // 2, T * (h % 2):T * (h % 2) + T], SMALL[:, 3:4], RST[:],
                                           ALU.mult, ALU.mult))
                do(V_.tensor_tensor(y, y, GR[:, h, :], ALU.mult), "gla_out")

            def after_drained(names):
                for x in names:
                    wait_drained(dve, x)

            mod(1, range(0, 3))
            after_drained([("ya", m) for m in range(8)])
            residual(1, YO, 0, 1, (0, 1))
            mod(1, range(3, 7))
            scaled(2, X, 0, T)
            for m in range(FT):
                wait_written(dve, ("u", m))
                wait_drained(dve, ("g", m))
                ins = V_.tensor_tensor(FF[:, m, :], FF[:, m, :], bank(("u", m)), ALU.mult)
                drain(ins, ("u", m))
            mod(1, range(7, 12))
            coefs(1)
            after_drained([("yf", m) for m in range(8)])
            residual(3, YO, 0, 3, (0, 1))
            scaled(4, X, 0, T)
            dve.wait_ge(sem("lam_exp"), 1)
            do(V_.tensor_tensor(SMALL[:, 10:11], SMALL[:, 8:9], SMALL[:, 9:10], ALU.subtract))
            do(V_.tensor_scalar(SMALL[:, 10:11], SMALL[:, 10:11], LAM_INIT, None, ALU.add))
            for n in range(2):
                for t in range(TT):
                    wait_written(dve, ("v1", t, n))
                    drained_by(V_.tensor_copy(V1[:, t, 512 * n:512 * n + 512], bank(("v1", t, n))), ("v1", t, n))
            for m in range(8):
                wait_written(dve, ("rot", m))
                s2 = const("sin").unsqueeze(1).to_broadcast([128, 2, 256])
                drain(V_.tensor_tensor(TMP[:].rearrange("p (a b) -> p a b", b=256),
                                       bank(("rot", m)).rearrange("p (a b) -> p a b", b=256), s2, ALU.mult), ("rot", m))
                for j, x in enumerate((Q1[:, m, :], K1[:, m, T_CTX:T])):
                    do(V_.tensor_tensor(x, x, const("cos"), ALU.mult))
                    do(V_.tensor_tensor(x, x, TMP[:, 256 * j:256 * j + 256], ALU.add), ("dve_step", "diff_roped")[j])
            attend(diff_steps())
            for h in range(DIFF_H):
                rstd(("ssd", h), RST[:, 0:256], 2 * DIFF_D, 256)
                do(V_.scalar_tensor_tensor(H[:, h, T_CTX:T], OD[:, h, :], SMALL[:, 4:5], RST[:, 0:256], ALU.mult,
                                           ALU.mult), "diff_out")
            after_drained([("yc", m) for m in range(8)])
            residual(5, YO1, 1, 1, (1,))
            scaled(6, X, T_CTX, T)

            LG, RK, SEL = view(RT, 0, 2, E), view(RT, 48, 2, E), view(RT, 64, 2, E)
            GATE, SPOS, CMP = view(RT, 80, 2, E), view(RT, 96, 2, E + 1), view(RT, 128, 8, 8)
            CMQ = view(RT, 192, 8, 8)
            for t in range(2):
                wait_written(dve, ("lg", t))
                drain(V_.tensor_copy(LG[:, t, :], bank(("lg", t))[:, 0:E]), ("lg", t))
                do(V_.max(RT[:, 16 + 8 * t:24 + 8 * t], LG[:, t, :]))
                do(V_.tensor_tensor(RT[:, 40 + t:41 + t], RT[:, 17 + 8 * t:18 + 8 * t], RT[:, 16 + 8 * t:17 + 8 * t],
                                    ALU.subtract), ("dve_step", "gate_logits")[t])
            for t in range(2):
                other = LG[:, t, :].unsqueeze(1).to_broadcast([128, 8, 8])
                own = LG[:, t, :].unsqueeze(2).to_broadcast([128, 8, 8])
                do(V_.tensor_tensor(CMP, other, own, ALU.is_gt))
                do(V_.tensor_tensor(CMQ, other, own, ALU.is_equal))
                do(V_.tensor_tensor(CMQ, CMQ, const("lower8").rearrange("p (a b) -> p a b", b=8), ALU.mult))
                do(V_.tensor_tensor(CMP, CMP, CMQ, ALU.add))
                do(V_.reduce_sum(RK[:, t, :], CMP, axis=AX.X))
            do(V_.tensor_scalar(SEL, RK, 2.0, None, ALU.is_lt), "selected")
            dve.wait_ge(sem("gate_exp"), 1)
            do(V_.tensor_scalar(RT[:, 42:44], RT[:, 40:42], 1.0, None, ALU.add))
            do(V_.reciprocal(RT[:, 42:44], RT[:, 42:44]))
            do(V_.tensor_tensor(RT[:, 44:46], RT[:, 42:44], RT[:, 40:42], ALU.mult))
            for t in range(2):
                do(V_.tensor_scalar(GATE[:, t, :], RK[:, t, :], 0.0, RT[:, 42 + t:43 + t], ALU.is_equal, ALU.mult))
                do(V_.tensor_scalar(CMQ[:, 0, :], RK[:, t, :], 1.0, RT[:, 44 + t:45 + t], ALU.is_equal, ALU.mult))
                do(V_.tensor_tensor(GATE[:, t, :], GATE[:, t, :], CMQ[:, 0, :], ALU.add))
            for t in range(2):
                wait_written(dve, ("pos", t))
                drain(V_.scalar_tensor_tensor(SPOS[:, t, 0:E], bank(("pos", t))[:, 0:E], 1000.0, SEL[:, t, :], ALU.add,
                                              ALU.mult), ("pos", t))
            do(V_.memset(SPOS[:, :, E:E + 1], 0.0))
            do(V_.tensor_scalar(SPOS, SPOS, -1000.0, None, ALU.add))
            wait_written(dve, "cnt")
            drain(V_.tensor_scalar(FLAGS[:], bank("cnt")[:, 0:E], 128.0, None, ALU.is_gt), "cnt")
            do(V_.memset(RT[:, 120:121], 0.0), "flags_ready")
            for t in range(2):
                for n in range(2):
                    wait_written(dve, ("ht", t, n))
            do(V_.memset(ACC, 0.0), "acc_done")

            def selection(e, weighted):
                for t in range(2):
                    if weighted:
                        ins = V_.tensor_scalar(PG[:, t, :], const("iota"), SPOS[:, t, bass.ds(e, 1)], GATE[:, t, bass.ds(e, 1)],
                                               ALU.is_equal, ALU.mult)
                    else:
                        ins = V_.tensor_scalar(PSEL[:, t, :], const("iota"), SPOS[:, t, bass.ds(e, 1)], None, ALU.is_equal)
                ins.then_inc(sem("onehots" if weighted else "selection"), 1)

            def expert(e, blocks):
                def split(q):
                    n = n_pre + q
                    dve.wait_ge(sem("hi_made"), PER_EXPERT * e + q + 1)
                    l0 = n % SLOTS * PIECE
                    V_.tensor_tensor(LO[:, l0:l0 + PIECE], slot(n),
                                     HI[:, q % SPLITS * PIECE:(q % SPLITS + 1) * PIECE].bitcast(f32),
                                     ALU.subtract).then_inc(sem("lo_made"), 1)

                split(0)
                dve.wait_ge(sem("x_hi"), e + 1)
                w = 1024 * blocks
                V_.tensor_tensor(XL[:, 0:w], banks(0, 2 * blocks), XH[:, 0:w].bitcast(f32),
                                 ALU.subtract).then_inc(sem("x_lo"), 1)
                split(1)
                selection(e, True)
                selection(e + 1, False)
                for kind, c in vector_order():
                    if kind == "split" and c > 1:
                        split(c)
                    elif kind == "hidden":
                        dve.wait_ge(sem("silu"), EC * e + c + 1)
                        h = by_block(HS, blocks)
                        V_.tensor_tensor(h, h, PS[:, 2:2 + blocks, :], ALU.mult).then_inc(sem("hidden"), 1)
                    elif kind == "transposed":
                        dve.wait_ge(sem("ht_hi"), EC * e + c + 1)
                        V_.tensor_tensor(by_block(HTL, blocks), PS[:, 2:2 + blocks, :],
                                         by_block(HTH, blocks).bitcast(f32), ALU.subtract).then_inc(sem("ht_lo"), 1)
                for j in range(4):
                    dve.wait_ge(sem("scattered"), 4 * e + j + 1)
                    a = ACC[:, 2 * j:2 * j + 2, :].rearrange("p a b -> p (a b)")
                    V_.tensor_tensor(a, a, PS[:, 4 + j, :], ALU.add).then_inc(sem("acc_done"), 1)

            selection(0, False)
            with dve.Fori(0, E) as e:
                flag = dve.value_load(FLAGS[0:1, bass.ds(e, 1)], min_val=0, max_val=1)
                with dve.If(flag > 0):
                    expert(e, 2)
                with dve.Else():
                    expert(e, 1)
            dve.wait_ge(sem("acc_done"), 4 * E + 1)
            do(V_.tensor_tensor(SQ7, ACC, ACC, ALU.mult), "moe_squares")
            dve.wait_ge(sem("rooted"), count["rooted"] + 1)
            do(V_.reciprocal(RST[:, 0:256], PS[:, 0, 0:256]))
            residual(None, ACC, 1, 3, (1,), ready="out_ready")


def constants():
    out = np.zeros((128, CONST_W), np.float32)

    def put(name, a):
        out[:, CONST[name][0]:CONST[name][1]] = a

    i, j = np.arange(128)[:, None], np.arange(128)[None, :]
    same = i // CHUNK == j // CHUNK
    put("ident", i == j)
    put("ones", 1.0)
    put("tri_f", (same & (i <= j)) / TAU)
    put("tri_b", (same & (i >= j)) / TAU)
    put("before", i < j)
    rot = np.zeros((128, 128), np.float32)
    for m in range(128):
        if m % 64 < 32:
            rot[m + 32, m] = -1.0
        else:
            rot[m - 32, m] = 1.0
    put("rot", rot)
    n_freq = ROPE // 4
    tok = np.arange(T_LAT)
    freq = (np.float32(ROPE_BASE) ** (-np.arange(n_freq, dtype=np.float32) / np.float32(n_freq))).astype(np.float32)
    row, col = (tok // GRID_W).astype(np.float32), (tok % GRID_W).astype(np.float32)
    ang = np.concatenate([row[:, None] * freq, col[:, None] * freq], axis=-1).T
    put("cos", np.tile(np.cos(ang), (4, 1)))
    put("sin", np.tile(np.sin(ang), (4, 1)))
    masks = []
    for d in range(2):
        for m in LEVELS:
            lo, hi = i % (2 * m) < m, j % (2 * m) >= m
            up, dn = i % (2 * m) >= m, j % (2 * m) < m
            block = i // (2 * m) == j // (2 * m)
            masks.append(block & (lo & hi if d == 0 else up & dn))
    put("masks", np.concatenate(masks, 1))
    put("diag2", 2.0 * (i == j))
    put("iota", np.broadcast_to(np.arange(256)[None, :], (128, 256)))
    put("lower8", np.broadcast_to((np.arange(8)[None, :] < np.arange(8)[:, None]).reshape(1, 64), (128, 64)))
    return out


def kernel(**inputs):
    import concourse.bacc as _bacc
    from concourse import mybir as _mybir
    from concourse.bass_utils import run_bass_kernel_spmd as _run

    a = {k: np.asarray(v) for k, v in inputs.items()}
    uq = a["mla_w_uq"].reshape(1, Q_RANK, MLA_H, NOPE + ROPE)
    a["mla_w_uq"] = np.concatenate([uq[..., :NOPE].reshape(1, Q_RANK, -1), uq[..., NOPE:].reshape(1, Q_RANK, -1)], 2)
    by_tile = lambda v: v.reshape(-1, 128).T

    pieces = list(plan()[0])
    for e in range(E):
        for kind, c, _ in expert_order():
            for half in range(2):
                if kind == "d":
                    pieces.append(("moe_w_down", (0, e), 4 * c + 2 * half, 4 * c + 2 * half + 2, 0, D, None))
                else:
                    pieces.append((("moe_w_gate" if kind == "g" else "moe_w_up"), (0, e), 4 * half, 4 * half + 4,
                                   512 * c, 512 * c + 512, None))
    stream = np.zeros((len(pieces), 128, PIECE), np.float32)
    for n, (src, index, k0, k1, c0, c1, _) in enumerate(pieces):
        w = a[src][index][128 * k0:128 * k1, c0:c1].reshape(k1 - k0, 128, c1 - c0)
        stream[n, :, 0:(k1 - k0) * (c1 - c0)] = w.transpose(1, 0, 2).reshape(128, -1)

    param = np.zeros((128, PARAM_W), np.float32)

    def put(name, v, rows=128):
        param[0:rows, PARAM[name][0]:PARAM[name][1]] = v

    put("c", np.stack([by_tile(a["c_ctx"]), by_tile(a["c"][0])], 2).reshape(128, 16))
    for name in ("g_pre_mix", "g_post_mix", "g_pre_ffn", "g_post_ffn", "b_mod"):
        put(name, np.concatenate([by_tile(a[name][i]) for i in range(2)], 1))
    put("g_q", by_tile(a["mla_g_q"][0]))
    put("g_kv", by_tile(a["mla_g_kv"][0]))
    put("g_gla", by_tile(a["gla_g_out"][0]))
    put("g_diff", by_tile(a["diff_g_out"][0]))
    for name in ("lq1", "lk1", "lq2", "lk2"):
        put(name, np.broadcast_to(a["diff_" + name][0], (128, DIFF_D)))
    put("router", a["moe_w_router"][0].reshape(KT, 128, E).transpose(1, 0, 2).reshape(128, KT * E))
    put("w_gate", np.concatenate([a["gla_w_gate_f"][0], a["gla_w_gate_b"][0]], 1), rows=RANK)
    put("b_gate", np.broadcast_to(np.concatenate([a["gla_b_gate_f"][0], a["gla_b_gate_b"][0]]), (128, 512)))

    arrays = {"stream_dram": stream, "const_dram": constants(), "param_dram": param,
              "x_dram": np.ascontiguousarray(np.concatenate([a["ctx"][0].T, a["x"][0].T], 1))}
    nc = _bacc.Bacc("TRN2", target_bir_lowering=False, num_devices=1)
    args = [nc.dram_tensor(n, v.shape, _mybir.dt.float32, kind="ExternalInput").ap() for n, v in arrays.items()]
    args.append(nc.dram_tensor("out_dram", (D, T_LAT), _mybir.dt.float32, kind="ExternalOutput").ap())
    build(nc, *args)
    r = _run(nc, [arrays], core_ids=[0])
    return np.ascontiguousarray(r.results[0]["out_dram"].T)[None]
```

```python
import math
from contextlib import ExitStack

import numpy as np
import concourse.bass as bass
from concourse import mybir

D, T_CTX, T_LAT = 1024, 256, 256
T = T_CTX + T_LAT
KT = D // 128
TT = T // 128
EPS = 1e-6
MLA_H, Q_RANK, KV_RANK, NOPE, ROPE, VD = 4, 256, 128, 128, 64, 128
MLA_SCALE = (NOPE + ROPE) ** -0.5
GLA_H, DK, DV, RANK, TAU, CHUNK = 4, 64, 128, 16, 16.0, 64
N_CHUNKS = T // CHUNK
LEVELS = [32, 16, 8, 4, 2, 1]
DIFF_H, DIFF_D = 8, 64
DIFF_SCALE = DIFF_D ** -0.5
LAM_INIT = 0.8 - 0.6 * math.exp(-0.3)
FFN = 2816
FT = FFN // 128
FT_SPLIT = FT // 2
E, EF = 8, 3584
EC = EF // 512
GRID_W, ROPE_BASE = 64, 10000.0
COLS_A = dict(cq=0, ckv=256, kr=384, gq=448, gk=704, gv=960, gr=1472, af=1984, ab=2000)
IN_A = 2016

SLOTS, PIECE = 7, 2048
SPLITS = 3
BANKS = 8
QK_ORDER = (4, 5, 6, 7, 0, 1, 2, 3)


def columns(*widths):
    at, out = 0, {}
    for name, width in widths:
        out[name] = (at, at + width)
        at += width
    return out, at


CONST, CONST_W = columns(
    ("ident", 128), ("ones", 128), ("tri_f", 128), ("tri_b", 128), ("before", 128), ("rot", 128),
    ("cos", 256), ("sin", 256), ("masks", 12 * 128), ("diag2", 128), ("iota", 256), ("lower8", 64))
PARAM, PARAM_W = columns(
    ("c", 16), ("g_pre_mix", 16), ("g_post_mix", 16), ("g_pre_ffn", 16), ("g_post_ffn", 16),
    ("b_mod", 96), ("g_q", 2), ("g_kv", 1), ("g_gla", 1), ("g_diff", 1),
    ("lq1", 64), ("lk1", 64), ("lq2", 64), ("lk2", 64), ("router", 64), ("w_gate", 512), ("b_gate", 512))


MOD_LEVELS = {1: 8, 3: 9, 5: 10, 7: 11, 9: 12}


def mod_rows(g):
    return [x for x in (g - 1, g) if (x == g - 1 and g not in (0, 4)) or (x == g and g in (3, 23))]


def plan():
    pieces, where, tiles, split = [], {}, [], []

    def split_linear(label, src, index, c0, c1, last):
        split.append(len(pieces))
        linear(label, src, index, KT, c0, c1, last)

    def linear(label, src, index, rows, c0, c1, last):
        kmax = PIECE // (c1 - c0)
        n = -(-rows // kmax)
        step = -(-rows // n)
        where[label] = []
        for k0 in range(0, rows, step):
            k1 = min(k0 + step, rows)
            where[label].append((len(pieces), k0, k1, c1 - c0))
            pieces.append((src, index, k0, k1, c0, c1, last))

    def mod(*chunks):
        for g in chunks:
            linear(("mod", g), "w_mod", g // 12, KT, g % 12 * 512, g % 12 * 512 + 512, ("mod", g))
            tiles.append(("mod", g))
            tiles.extend(("modT", x) for x in mod_rows(g))

    mod(0, 1, 2, 3)
    tiles.append(("ss", 0))
    mod(4)
    split_linear("cq", "w_in_a", 0, COLS_A["cq"], COLS_A["ckv"], ("cq", 1))
    split_linear("ckv", "w_in_a", 0, COLS_A["ckv"], COLS_A["gq"], "kr")
    split_linear("gq", "w_in_a", 0, COLS_A["gq"], COLS_A["gk"], ("gq", 1))
    split_linear("gk", "w_in_a", 0, COLS_A["gk"], COLS_A["gv"], ("gk", 1))
    for n in range(2):
        split_linear(("gv", n), "w_in_a", 0, COLS_A["gv"] + 256 * n, COLS_A["gv"] + 256 * n + 256, ("gv", 3))
    for n in range(2):
        split_linear(("gr", n), "w_in_a", 0, COLS_A["gr"] + 256 * n, COLS_A["gr"] + 256 * n + 256, ("gr", 2 * n + 1))
    split_linear("gaf", "w_in_a", 0, COLS_A["af"], IN_A, "ab")
    tiles.extend([("cq", 0), ("cq", 1), "ckv", "kr", ("gq", 0), ("gq", 1), "ssq", "sskv", ("gk", 0), ("gk", 1)])
    tiles.extend(("gv", t) for t in range(TT))
    tiles.extend(("gr", m) for m in range(4))
    tiles.extend(["af", "ab"])
    linear("uq", "mla_w_uq", 0, 2, 0, 768, ("qr", 1))
    linear("ukv", "mla_w_ukv", 0, 1, 0, 1024, ("v", 3))
    tiles.extend(("qn", h) for h in range(4))
    tiles.extend(("qr", p) for p in range(2))
    tiles.extend(("kn", h) for h in range(4))
    tiles.extend(("v", t) for t in range(TT))
    tiles.extend([("rotq", 0), ("rotq", 1), "rotk"])
    tiles.extend(("gx", t) for t in range(TT))
    mod(5)
    tiles.extend(x for x in mla_steps())
    tiles.extend(("cum", d, k) for d in range(2) for k in range(2))
    tiles.extend(("att", "diag", h) for h in range(4))
    for d in range(2):
        mod(6 + d)
        tiles.extend(("kT", d, t) for t in range(TT))
    for n in range(12):
        tiles.extend(("att", (n // 6, n % 6), h) for h in range(4))
        if n in MOD_LEVELS:
            mod(MOD_LEVELS[n])
    tiles.extend(("U", d, p, r) for d in range(2) for p in range(2) for r in range(2))
    mod(13)
    tiles.extend(("og", h) for h in range(4))
    mod(14)
    tiles.extend(("ssg", h) for h in range(4))
    for n in range(2):
        linear(("out_a", n), "w_out_a", 0, KT, 512 * n, 512 * n + 512, ("ya", 4 * n + 3))
    tiles.extend(("ya", m) for m in range(8))
    mod(15)
    tiles.append(("ss", 1))
    mod(16, 17)
    tiles.append(("ss", 2))
    mod(18)
    for n in range(FT // 2):
        split_linear(("fg", n), "ffn_w_gate", 0, 256 * n, 256 * n + 256, ("g", 2 * n + 1))
        split_linear(("fu", n), "ffn_w_up", 0, 256 * n, 256 * n + 256, ("u", 2 * n + 1))
        tiles.extend([("g", 2 * n), ("g", 2 * n + 1), ("u", 2 * n), ("u", 2 * n + 1)])
    for m in range(8):
        split.append(len(pieces))
        linear(("fd", m), "ffn_w_down", 0, FT, 128 * m, 128 * m + 128, ("yf", m))
        tiles.append(("yf", m))
    mod(19)
    tiles.append(("ss", 3))
    mod(20)
    tiles.append(("ss", 4))
    mod(21)
    for n in QK_ORDER:
        split_linear(("qk", n), "w_qkv_c", 0, 256 * n, 256 * n + 256, ("qk", 2 * n + 1))
        tiles.extend([("qk", 2 * n), ("qk", 2 * n + 1)])
    for n in range(4):
        split_linear(("v1", n), "w_qkv_c", 0, 2048 + 256 * n, 2304 + 256 * n, ("v1", 3, n // 2))
    tiles.extend(("v1", t, n) for n in range(2) for t in range(TT))
    tiles.extend(("rot", m) for m in range(8))
    for x in diff_steps():
        if x == ("dT", 0):
            mod(22)
        tiles.append(x)
    mod(23)
    for n in range(2):
        linear(("out_c", n), "w_out_c", 0, KT, 512 * n, 512 * n + 512, ("yc", 4 * n + 3))
    tiles.extend(("ssd", h) for h in range(8))
    tiles.extend(("yc", m) for m in range(8))
    tiles.extend([("ss", 5), ("ss", 6)])
    tiles.extend([("lg", 0), ("lg", 1)])
    tiles.extend(("ht", t, n) for t in range(2) for n in range(2))
    tiles.extend([("pos", 0), ("pos", 1), "cnt"])
    return pieces, where, {name: i for i, name in enumerate(tiles)}, split


def pipelined(scores, probs, outs, units):
    steps = []
    for u in range(2):
        steps += scores(u)
    for u in range(units):
        if u + 2 < units:
            steps += scores(u + 2)
        if u % 2 == 0 and u:
            steps.append(outs(u // 2 - 1))
        steps.append(probs(u))
    steps.append(outs(units // 2 - 1))
    return steps


def vector_steps(steps):
    late, out = [], []
    for kind, u in steps:
        if kind in ("pT", "dT") or (kind in ("s", "s1", "s2") and u < 2):
            out += [(kind, u)] + late
            late = []
        else:
            late.append((kind, u))
    return out + late


def mla_steps():
    return pipelined(lambda u: [("s", u)], lambda u: ("pT", u), lambda g: ("o", g), MLA_H * TT)


def diff_steps():
    return pipelined(lambda u: [("s1", u), ("s2", u)], lambda u: ("dT", u), lambda g: ("do", g), DIFF_H * 2)


def expert_order():
    steps, at = [], 0
    for c in range(EC):
        for kind in "gu":
            steps.append((kind, c, at))
            at += 2
        if c:
            steps.append(("d", c - 1, at))
            at += 2
    steps.append(("d", EC - 1, at))
    return steps


PER_EXPERT = 6 * EC


def piece_of(kind, c):
    return next(j for k, cc, j in expert_order() if (k, cc) == (kind, c))



def vector_order(blocks):
    after = {}
    for c in range(EC):
        before = piece_of("d", c - 1) + 1 if c else piece_of("g", 1) + 1 if blocks == 1 else piece_of("u", 0) + 1
        after.setdefault(min(piece_of("u", c) + 3, PER_EXPERT - 1), []).append(("hidden", c))
        after.setdefault(min(before + 2, PER_EXPERT - 1), []).append(("transposed", c))
    steps = []
    for q in range(PER_EXPERT):
        steps.append(("split", q))
        if q == piece_of("u", 0) + 3:
            steps.append(("scatter_matrix", 0))
        steps += sorted(after.get(q, []), key=lambda x: (x[0] != "hidden"))
    return steps


def build(nc, stream, const_dram, param_dram, x_dram, out_dram):
    f32, f32r, i32, u32 = mybir.dt.float32, mybir.dt.float32r, mybir.dt.int32, mybir.dt.uint32
    ALU, ACT, AX = mybir.AluOpType, mybir.ActivationFunctionType, mybir.AxisListType
    pieces, where, tile_no, split_pieces = plan()
    n_pre = len(pieces)

    ctx = ExitStack()
    with ctx:
        def sb(name, width, dt=f32):
            return ctx.enter_context(nc.sbuf_tensor(name, [128, width], dt))

        A_ = sb("AREA", 15360 + SPLITS * PIECE)
        area_end = nc.sbuf_base
        X_ = sb("X", KT * T)
        H_ = sb("H", KT * T)
        h_end = nc.sbuf_base
        RAW = sb("RAW", SLOTS * PIECE)
        raw_end = nc.sbuf_base
        C = sb("CONST", CONST_W)
        PR = sb("PARAM", PARAM_W)
        MOD_ = sb("MOD", 2 * 48 * 2)
        COEF_ = sb("COEF", 2 * 4 * 16)
        SC_ = sb("SC", 16)
        SMALL = sb("SMALL", 64)
        STAT = sb("STAT", 96)
        MROW = sb("MROW", 512)
        RST = sb("RST", T)
        TMP = sb("TMP", T)
        FLAGS = sb("FLAGS", E, i32)
        def over(name, width, offset):
            return nc.alloc_sbuf_tensor_at(name, [128, width], f32r, offset=offset)

        A_R = over("AREA_R", 15360 + SPLITS * PIECE, area_end - 4 * (15360 + SPLITS * PIECE))
        H_R = over("H_R", KT * T, h_end - 4 * KT * T)
        HI = over("W_HI", SPLITS * PIECE, area_end - 4 * SPLITS * PIECE)
        LO = over("W_LO", SLOTS * PIECE, raw_end - 4 * SLOTS * PIECE)
        XH = over("XH", KT * 256, h_end - 4 * KT * T)
        XL = over("XL", KT * 256, area_end - 4 * (SPLITS * PIECE + KT * 256))
        HTH = over("HTH", 1024, area_end - 4 * (SPLITS * PIECE + KT * 256 + 1024))
        HTL = over("HTL", 1024, area_end - 4 * (SPLITS * PIECE + KT * 256 + 2048))
        PS = ctx.enter_context(nc.psum_tensor("PS", [128, BANKS, 512], f32))

        def view(t, start, *shape):
            n = int(np.prod(shape))
            v = t[:, start:start + n]
            if len(shape) == 2:
                v = v.rearrange("p (a b) -> p a b", b=shape[1])
            if len(shape) == 3:
                v = v.rearrange("p (a b c) -> p a b c", b=shape[1], c=shape[2])
            return v

        X, H = view(X_, 0, KT, T), view(H_, 0, KT, T)
        MOD = view(MOD_, 0, 2 * 48, 2)
        SC = view(SC_, 0, KT, 2)
        COEF = view(COEF_, 0, 8, 8, 2)

        def const(name):
            return C[:, CONST[name][0]:CONST[name][1]]

        def param(name, a=0, b=None):
            s, e = PARAM[name]
            return PR[:, s + a:(e if b is None else s + b)]

        IDENT, ONES, ROT = const("ident"), const("ones"), const("rot")

        GQ, GK = view(A_, 0, 2, T), view(A_, 1024, 2, T)
        GV, GR = view(A_, 2048, TT, 512), view(A_, 4096, 4, T)
        LX = view(A_, 6144, TT, 512)
        m0 = 8192
        CQ, CKV, KR = view(A_, m0, 2, T), A_[:, m0 + 1024:m0 + 1536], A_[:, m0 + 1536:m0 + 2048]
        QN, KN = view(A_, m0 + 2048, 4, T), view(A_, m0 + 4096, 4, T)
        QR, V = view(A_, m0 + 6144, 2, T), view(A_, m0 + 7168, TT, 512)
        PB = view(A_, m0 + 9216, 3, 512)
        PT = view(A_, m0 + 10752, 2, 4, 256)
        AF = view(A_, m0 + 10752, 2, T)
        LE = view(H_, 4 * T, TT, 512)
        SQ0 = view(A_, 0, KT, T)
        SQM = view(A_, 19968, 3, T)
        CUM = view(A_, m0, 4, T)
        EX, AA = view(A_, m0 + 2048, 2, 2 * T), view(A_, m0 + 4096, 2, 2 * T)
        ATT = view(A_, m0 + 6144, 4, T)
        KHT = view(A_, m0 + 8192, 8, 256)
        g0 = m0 + 10240
        STATES = (view(H_, 4 * T, 16, 128), view(A_, m0, 16, 128))
        QH = view(A_, g0, 4, T)
        YO = view(A_, 0, KT, T)
        SQY = view(A_, 4096, KT, T)
        FF = view(A_, 8192, FT, T)
        K1 = view(A_, 0, 8, T)
        Q1 = view(A_, 4096, 8, 256)
        V1 = view(A_, 6144, TT, D)
        E1 = view(A_, 10240, 3, 512)
        E2 = view(A_, 11776, 3, 512)
        PT1 = view(A_, 13312, 2, 4, 256)
        OD = view(A_, 15360, 8, 256)
        SQD = view(A_, 17408, 8, 256)
        YO1 = view(A_, 0, KT, 256)
        SQ1 = view(A_, 2048, KT, 256)
        HTOK = view(A_, 0, 2, D)
        HS = A_[:, 2048:3072]
        YS = A_[:, 3072:5120]
        MERGE = YS[0:64, 1024:2048].rearrange("p (a b) -> p a b", b=512)
        PSEL = view(A_, 5120, 2, 256)
        PG = view(A_, 5632, 2, 256)
        GT = view(A_, 6144, 2, 256)
        SQ7 = view(A_, 2048, KT, 256)
        RT = A_[:, 7680:8192]
        HL = view(H_R, 0, KT, T)
        HH = [view(A_R, at, KT, T) for at in (10240, 0, 10240)]
        FF_HIGH = ((0, 4, H_R[:, 0:2048]), (4, 8, H_R[:, 2048:4096]), (8, FT_SPLIT, A_R[:, 4096:4096 + 512 * (FT_SPLIT - 8)]))
        FF_LOW = A_R[:, 8192:8192 + T * FT_SPLIT]
        STAGE_PIECES = [range(0, 9), range(9, 9 + FT), range(9 + FT, 17 + FT), range(17 + FT, 29 + FT)]
        W_AT = [(6144, 14336, 16384), (19456, 4096, 6144), (5632, 19456), (14336, 16384, 18432)]
        ACC = view(H_, 2048, KT, 256)

        made = {}

        def sem(name):
            if name not in made:
                made[name] = ctx.enter_context(nc.semaphore(name))
            return made[name]

        loaded = [sem(f"weights_loaded_{s}") for s in range(SLOTS)]
        drained = [sem(f"bank_{b}_drained") for b in range(BANKS)]
        written = sem("tiles_written")

        def bank(name):
            return PS[:, tile_no[name] % BANKS, :]

        def wait_written(eng, name):
            eng.wait_ge(written, tile_no[name] + 1)

        def wait_drained(eng, name):
            eng.wait_ge(drained[tile_no[name] % BANKS], tile_no[name] // BANKS + 1)

        def drained_by(ins, name):
            ins.then_inc(drained[tile_no[name] % BANKS], 1)

        def banks(first, n):
            return PS[:, first:first + n, :].rearrange("p a b -> p (a b)")

        def halves(t, start, lo):
            w = 1024 if t is XH else 512
            v = t[:, start:start + w].rearrange("p (n s) -> p n s", s=128)
            return v[:, :, 64 * lo:64 * lo + 64]

        def narrow_tokens():
            return PS[:, 2:4, :].rearrange("p a (n s) -> p (a n) s", s=128)[:, :, 0:64]

        def narrow_hidden(b):
            return PS[:, b, :].rearrange("p (n s) -> p n s", s=128)[:, :, 0:64]

        def hidden_bank(blocks):
            return 6 if blocks == 1 else 2

        def turn(blocks, c):
            return c % 2 if blocks == 1 else 0

        def by_block(t, blocks):
            return t[:, 0:512 * blocks].rearrange("p (n f) -> p n f", f=512)

        def slot(n):
            return RAW[:, n % SLOTS * PIECE:(n % SLOTS + 1) * PIECE]

        def wait_piece(eng, n):
            eng.wait_ge(loaded[n % SLOTS], 16 * (n // SLOTS + 1))

        def weight(label, kt):
            for n, k0, k1, cols in where[label]:
                if k0 <= kt < k1:
                    return slot(n)[:, (kt - k0) * cols:(kt - k0 + 1) * cols]

        def wait_weight(eng, label, kt):
            for n, k0, k1, cols in where[label]:
                if k0 == kt:
                    wait_piece(eng, n)

        def high(k):
            stage = next(i for i, x in enumerate(STAGE_PIECES) if k in x)
            at = W_AT[stage][(k - STAGE_PIECES[stage][0]) % len(W_AT[stage])]
            return A_R[:, at:at + PIECE]

        def low(k):
            n = split_pieces[k] % SLOTS
            return LO[:, n * PIECE:(n + 1) * PIECE]

        def wait_high_free(eng, k):
            stage = next(i for i, x in enumerate(STAGE_PIECES) if k in x)
            last = k - len(W_AT[stage])
            if last in STAGE_PIECES[stage]:
                wait_written(eng, pieces[split_pieces[last]][6])

        def piece_width(k):
            _, _, k0, k1, c0, c1, _ = pieces[split_pieces[k]]
            return (k1 - k0) * (c1 - c0)

        has_state = {(0, c): c > 0 for c in range(8)} | {(1, c): c != 3 for c in range(8)}
        chunk_order = [list(range(8)), [3, 2, 1, 0, 7, 6, 5, 4]]

        def state(d, p, c):
            return STATES[d][:, p * 8 + c, :]

        block = ctx.enter_context(nc.Block())

        @block.sync
        def _(sp):
            sp.dma_start(PR[:], param_dram).then_inc(sem("param_loaded"), 16)
            for n, (_, _, k0, k1, c0, c1, _) in enumerate(pieces):
                if n >= SLOTS:
                    wait_written(sp, pieces[n - SLOTS][6])
                if n == 2:
                    sp.dma_start(C[:], const_dram).then_inc(sem("const_loaded"), 16)
                w = (k1 - k0) * (c1 - c0)
                sp.dma_start(slot(n)[:, 0:w], stream[n, :, 0:w]).then_inc(loaded[n % SLOTS], 16)

            def expert_pieces(n, free):
                for s in range(SLOTS):
                    free(s)
                    q = (n_pre + s) % SLOTS
                    sp.dma_start(slot(q), stream[n + s]).then_inc(loaded[q], 16)

            expert_pieces(n_pre, lambda s: wait_written(sp, pieces[n_pre - SLOTS + s][6]))
            with sp.Fori(1, E * PER_EXPERT // SLOTS) as i:
                expert_pieces(n_pre + SLOTS * i, lambda s: sp.wait_ge(sem("piece_used"), SLOTS * i + (s - SLOTS + 1)))
            sp.wait_ge(sem("out_ready"), 8)
            sp.dma_start(out_dram.rearrange("(k p) t -> p k t", p=128), X[:, :, T_CTX:T]).then_inc(sem("out_stored"), 16)
            sp.wait_ge(sem("out_stored"), 16)

        @block.tensor
        def _(pe):
            def claim(name):
                n = tile_no[name]
                if n >= BANKS:
                    pe.wait_ge(drained[n % BANKS], n // BANKS)
                return PS[:, n % BANKS, :]

            def done(ins, name):
                written_so_far[0] += 1
                assert tile_no[name] + 1 == written_so_far[0], name
                ins.then_inc(written, 1)

            written_so_far = [0]

            def mm(out, lhsT, rhs, start, stop):
                return nc.tensor.matmul(out, lhsT, rhs, start=start, stop=stop)

            def linear(name, label, cols, rhs, n, first, rows=KT, ready=None):
                b = claim(name)
                for kt in range(rows):
                    if first:
                        wait_weight(pe, label, kt)
                    if ready is not None:
                        ready(kt)
                    w = weight(label, kt)[:, cols[0]:cols[1]]
                    i = mm(b[0:cols[1] - cols[0], 0:n], w, rhs(kt), kt == 0, kt == rows - 1)
                done(i, name)

            def linears(label, tiles, rhs, n, ready):
                bs = [claim(name) for name, _ in tiles]
                for kt in range(KT):
                    wait_weight(pe, label, kt)
                    ready(kt)
                    ins = [mm(b[0:c1 - c0, 0:n], weight(label, kt)[:, c0:c1], rhs(kt), kt == 0, kt == KT - 1)
                           for b, (_, (c0, c1)) in zip(bs, tiles)]
                for i, (name, _) in zip(ins, tiles):
                    done(i, name)

            def three(out, a, b, first, last):
                mm(out, a[0], b[0], first, False)
                mm(out, a[0], b[1], False, False)
                return mm(out, a[1], b[0], False, last)

            def split_weight(label, kt, c0, c1):
                n, _, _, cols = where[label][0]
                k = split_pieces.index(n)
                return [t[:, cols * kt + c0:cols * kt + c1] for t in (high(k), low(k))]

            def wait_split(label):
                pe.wait_ge(sem("low_made"), split_pieces.index(where[label][0][0]) + 1)

            def split_x(stage, kt, t0, t1):
                return [t[:, kt, t0:t1] for t in (HH[stage], HL)]

            def split_linear(stage, label, tiles, t0=0, first=False):
                wait_split(label)
                bs = [claim(name) for name, _ in tiles]
                for kt in range(KT):
                    if first:
                        pe.wait_ge(sem("h_lo"), KT * stage + kt + 1)
                    ins = [three(b[0:c1 - c0, 0:T - t0], split_weight(label, kt, c0, c1),
                                 split_x(stage, kt, t0, T), kt == 0, kt == KT - 1)
                           for b, (_, (c0, c1)) in zip(bs, tiles)]
                for i, (name, _) in zip(ins, tiles):
                    done(i, name)

            def split_token_major(stage, names, labels):
                bs = [claim(name) for name in names]
                for half, label in enumerate(labels):
                    wait_split(label)
                    for t, name in enumerate(names):
                        for kt in range(KT):
                            i = three(bs[t][:, 256 * half:256 * half + 256],
                                      split_x(stage, kt, 128 * t, 128 * t + 128), split_weight(label, kt, 0, 256),
                                      kt == 0, kt == KT - 1)
                        if half:
                            done(i, name)

            def mod(*chunks):
                for g in chunks:
                    b = claim(("mod", g))
                    for kt in range(KT):
                        wait_weight(pe, ("mod", g), kt)
                        i = mm(b[0:2, :], SC[:, kt, :], weight(("mod", g), kt), kt == 0, kt == KT - 1)
                    done(i, ("mod", g))
                    if g == 1:
                        pe.wait_ge(sem("const_loaded"), 16)
                    for x in mod_rows(g):
                        wait_drained(pe, ("mod", x))
                        b = claim(("modT", x))
                        for j in range(4):
                            i = nc.tensor.transpose(b[:, 2 * j:2 * j + 2], MROW[0:2, 128 * j:128 * j + 128],
                                                    IDENT[0:2, 0:2])
                        done(i, ("modT", x))

            def sum_squares(name, sq, n, tiles, ready):
                b = claim(name)
                for k in range(tiles):
                    ready(k)
                    i = mm(b[:, 0:n], ONES, sq(k), k == 0, k == tiles - 1)
                done(i, name)

            def norm_sum(i, sq, n):
                sum_squares(("ss", i), sq, n, KT,
                            lambda k: pe.wait_ge(sem("squares"), 4 * i + k // 2 + 1) if k % 2 == 0 else None)

            pe.wait_ge(sem("silu_c"), 1)
            mod(0, 1, 2, 3)
            norm_sum(0, lambda k: SQ0[:, k, :], T)
            mod(4)

            def h_ready(stage):
                def ready(kt):
                    pe.wait_ge(sem("h_ready"), KT * stage + kt + 1)
                return ready

            hx = lambda kt: H[:, kt, :]
            hl = lambda kt: H[:, kt, T_CTX:T]
            pair = ((0, 128), (128, 256))
            split_linear(0, "cq", [(("cq", m), pair[m]) for m in range(2)], first=True)
            split_linear(0, "ckv", [("ckv", (0, 128)), ("kr", (128, 192))])
            split_linear(0, "gq", [(("gq", m), pair[m]) for m in range(2)])
            sum_squares("ssq", lambda k: SQM[:, k, :], T, 2, lambda k: pe.wait_ge(sem("mla_squares"), k + 1))
            sum_squares("sskv", lambda k: SQM[:, 2, :], T, 1, lambda k: pe.wait_ge(sem("mla_squares"), 3))
            split_linear(0, "gk", [(("gk", m), pair[m]) for m in range(2)])
            split_token_major(0, [("gv", t) for t in range(TT)], [("gv", 0), ("gv", 1)])
            for n in range(2):
                split_linear(0, ("gr", n), [(("gr", 2 * n + j), pair[j]) for j in range(2)])
            split_linear(0, "gaf", [("af", (0, 16)), ("ab", (16, 32))])

            pe.wait_ge(sem("lora_normed"), 3)
            for h in range(MLA_H):
                linear(("qn", h), "uq", (128 * h, 128 * h + 128), lambda k: CQ[:, k, :], T, h == 0, rows=2)
            for p in range(2):
                linear(("qr", p), "uq", (512 + 128 * p, 640 + 128 * p), lambda k: CQ[:, k, :], T, False, rows=2)
            for h in range(MLA_H):
                linear(("kn", h), "ukv", (256 * h, 256 * h + 128), lambda k: CKV, T, h == 0, rows=1)
            for t in range(TT):
                b = claim(("v", t))
                w = weight("ukv", 0).rearrange("p (h c) -> p h c", c=256)[:, :, 128:256]
                done(mm(b, CKV[:, 128 * t:128 * t + 128], w, True, True), ("v", t))
            for p in range(2):
                wait_drained(pe, ("qr", p))
                b = claim(("rotq", p))
                done(mm(b[:, 0:256], ROT, QR[:, p, T_CTX:T], True, True), ("rotq", p))
            wait_drained(pe, "kr")
            b = claim("rotk")
            done(mm(b[:, 0:256], ROT, KR[:, T_CTX:T], True, True), "rotk")

            wait_drained(pe, "af")
            wait_drained(pe, "ab")
            for t in range(TT):
                b = claim(("gx", t))
                for d in range(2):
                    i = mm(b[:, 256 * d:256 * d + 256], AF[0:16, d, 128 * t:128 * t + 128],
                           param("w_gate", 256 * d, 256 * d + 256)[0:16, :], True, True)
                done(i, ("gx", t))
            mod(5)

            for h in range(MLA_H):
                wait_drained(pe, ("kn", h))
                wait_drained(pe, ("qn", h))
            for t in range(TT):
                wait_drained(pe, ("v", t))
            pe.wait_ge(sem("mla_roped"), 3)
            for kind, u in mla_steps():
                if kind == "s":
                    h, q, keys = u // TT, u % TT, (2 if u % TT < 2 else 4) * 128
                    r = 64 * (h % 2)
                    b = claim(("s", u))
                    mm(b[:, 0:keys], QN[:, h, 128 * q:128 * q + 128], KN[:, h, 0:keys], True, False)
                    done(mm(b[:, 0:keys], QR[r:r + 64, h // 2, 128 * q:128 * q + 128], KR[r:r + 64, 0:keys],
                            False, True), ("s", u))
                elif kind == "pT":
                    pe.wait_ge(sem("probs"), u + 1)
                    b = claim(("pT", u))
                    for k in range(2 if u % TT < 2 else 4):
                        i = nc.tensor.transpose(b[:, 128 * k:128 * k + 128], PB[:, u % 3, 128 * k:128 * k + 128], IDENT)
                    done(i, ("pT", u))
                else:
                    wait_drained(pe, ("pT", 2 * u))
                    wait_drained(pe, ("pT", 2 * u + 1))
                    b = claim(("o", u))
                    kts = 2 if u % 2 == 0 else 4
                    for k in range(kts):
                        i = mm(b[:, 0:256], V[:, k, 128 * (u // 2):128 * (u // 2) + 128], PT[:, u % 2, k, :],
                               k == 0, k == kts - 1)
                    done(i, ("o", u))

            pe.wait_ge(sem("log_decays"), 1)
            for d in range(2):
                for k in range(2):
                    b = claim(("cum", d, k))
                    for t in range(TT):
                        i = mm(b[:, 128 * t:128 * t + 128], LX[:, t, 256 * d + 128 * k:256 * d + 128 * k + 128],
                               const(("tri_f", "tri_b")[d]), True, True)
                    done(i, ("cum", d, k))

            def pairs(name, lhs, rhs):
                h = name[2]
                r = 64 * (h % 2)
                b = claim(name)
                for t in range(TT):
                    c = slice(T * (h // 2) + 128 * t, T * (h // 2) + 128 * t + 128)
                    i = mm(b[:, 128 * t:128 * t + 128], lhs[r:r + 64, c], rhs[r:r + 64, c], True, True)
                done(i, name)

            gq, gk = A_[:, 0:1024], A_[:, 1024:2048]
            for m in range(2):
                wait_drained(pe, ("gq", m))
                wait_drained(pe, ("gk", m))
            for h in range(GLA_H):
                pairs(("att", "diag", h), gk, gq)
            for d in range(2):
                mod(6 + d)
                pe.wait_ge(sem("decayed_keys"), d + 1)
                for t in range(TT):
                    b = claim(("kT", d, t))
                    for k in range(2):
                        i = nc.tensor.transpose(b[:, 128 * k:128 * k + 128],
                                                AA[:, d, T * k + 128 * t:T * k + 128 * t + 128], IDENT)
                    done(i, ("kT", d, t))
            for d in range(2):
                for lv in range(6):
                    pe.wait_ge(sem("level_ready"), 6 * d + lv + 1)
                    for h in range(GLA_H):
                        a = AA[:, lv % 2, :]
                        pairs(("att", (d, lv), h), a, a)
                    if 6 * d + lv in MOD_LEVELS:
                        mod(MOD_LEVELS[6 * d + lv])
            for d in range(2):
                for t in range(TT):
                    wait_drained(pe, ("kT", d, t))
            for d in range(2):
                for p in range(2):
                    for r in range(2):
                        b = claim(("U", d, p, r))
                        for t in range(TT):
                            for hh in range(2):
                                i = mm(b[64 * hh:64 * hh + 64, 128 * t:128 * t + 128],
                                       KHT[64 * r:64 * r + 64, TT * d + t, 128 * p + 64 * hh:128 * p + 64 * hh + 64],
                                       GV[64 * r:64 * r + 64, t, 128 * (2 * p + hh):128 * (2 * p + hh) + 128],
                                       True, True)
                        done(i, ("U", d, p, r))
            mod(13)
            for h in range(GLA_H):
                wait_drained(pe, ("att", (1, 5), h))
            pe.wait_ge(sem("decayed_queries"), 2)
            for h in range(GLA_H):
                p, r = h // 2, 64 * (h % 2)
                b = claim(("og", h))
                for d in range(2):
                    for r2 in range(2):
                        wait_drained(pe, ("U", d, p, r2))
                for t in range(TT):
                    mms = [(slice(128 * t, 128 * t + 128), GV[:, t, 128 * h:128 * h + 128],
                            ATT[:, h, 128 * t:128 * t + 128])]
                    for c in (2 * t, 2 * t + 1):
                        for d in range(2):
                            if has_state[d, c]:
                                mms.append((slice(64 * c, 64 * c + 64), state(d, p, c)[r:r + 64, :],
                                            QH[r:r + 64, 2 * d + p, 64 * c:64 * c + 64]))
                    for j, (cols, a, w) in enumerate(mms):
                        i = nc.tensor.matmul(b[:, cols], a, w, start=j == 0, stop=j == len(mms) - 1,
                                             skip_group_check=True)
                done(i, ("og", h))
            mod(14)
            for h in range(GLA_H):
                sum_squares(("ssg", h), lambda k: EX[:, h // 2, T * (h % 2):T * (h % 2) + T], T, 1,
                            lambda k: pe.wait_ge(sem("gla_squares"), h + 1))

            def y_ready(kt):
                if kt < 4:
                    wait_drained(pe, ("o", 2 * kt + 1))
                else:
                    pe.wait_ge(sem("gla_out"), kt - 3)

            quarters = [(128 * j, 128 * j + 128) for j in range(4)]
            linears(("out_a", 0), [(("ya", m), quarters[m]) for m in range(4)], hx, T, y_ready)
            for m in range(4, 8):
                linear(("ya", m), ("out_a", 1), quarters[m % 4], hx, T, m == 4)
            mod(15)
            norm_sum(1, lambda k: SQY[:, k, :], T)
            mod(16, 17)
            norm_sum(2, lambda k: SQY[:, k, :], T)
            mod(18)
            for n in range(FT // 2):
                for x in "gu":
                    split_linear(1, ("f" + x, n), [((x, 2 * n + j), pair[j]) for j in range(2)], first=(x, n) == ("g", 0))
            for m in range(8):
                b = claim(("yf", m))
                for kt in range(FT_SPLIT, FT):
                    wait_weight(pe, ("fd", m), kt)
                    if m == 0:
                        wait_drained(pe, ("u", kt))
                    mm(b, weight(("fd", m), kt), FF[:, kt, :], kt == FT_SPLIT, False)
                wait_split(("fd", m))
                for i, (k0, k1, hi) in enumerate(FF_HIGH):
                    if m == 0:
                        pe.wait_ge(sem("ff_low"), i + 1)
                    for kt in range(k0, k1):
                        x = [hi[:, T * (kt - k0):T * (kt - k0) + T], FF_LOW[:, T * kt:T * kt + T]]
                        ins = three(b, split_weight(("fd", m), kt, 0, 128), x, False, kt == FT_SPLIT - 1)
                done(ins, ("yf", m))
            mod(19)
            norm_sum(3, lambda k: SQY[:, k, :], T)
            mod(20)

            norm_sum(4, lambda k: SQY[:, k, :], T)
            mod(21)
            for n in QK_ORDER:
                split_linear(2, ("qk", n), [(("qk", 2 * n + j), pair[j]) for j in range(2)], 0 if n >= 4 else T_CTX,
                             first=n == QK_ORDER[0])
            for n in range(2):
                split_token_major(2, [("v1", t, n) for t in range(TT)], [("v1", 2 * n), ("v1", 2 * n + 1)])
            for m in range(8):
                wait_drained(pe, ("qk", m))
                wait_drained(pe, ("qk", 8 + m))
                b = claim(("rot", m))
                mm(b[:, 0:256], ROT, Q1[:, m, :], True, True)
                done(mm(b[:, 256:512], ROT, K1[:, m, T_CTX:T], True, True), ("rot", m))
            for n in range(2):
                for t in range(TT):
                    wait_drained(pe, ("v1", t, n))
            for kind, u in diff_steps():
                if kind in ("s1", "s2"):
                    h, q = u // 2, u % 2
                    r = 0 if kind == "s1" else 64
                    pe.wait_ge(sem("diff_roped"), h + 1)
                    b = claim((kind, u))
                    done(mm(b, Q1[r:r + 64, h, 128 * q:128 * q + 128], K1[r:r + 64, h, :], True, True), (kind, u))
                elif kind == "dT":
                    if u == 0:
                        mod(22)
                    pe.wait_ge(sem("diff_probs"), u + 1)
                    b = claim(("dT", u))
                    for k in range(TT):
                        i = nc.tensor.transpose(b[:, 128 * k:128 * k + 128], E1[:, u % 3, 128 * k:128 * k + 128], IDENT)
                    done(i, ("dT", u))
                else:
                    wait_drained(pe, ("dT", 2 * u))
                    wait_drained(pe, ("dT", 2 * u + 1))
                    b = claim(("do", u))
                    for k in range(TT):
                        i = mm(b[:, 0:256], V1[:, k, 128 * u:128 * u + 128], PT1[:, u % 2, k, :], k == 0, k == 3)
                    done(i, ("do", u))
            mod(23)
            for h in range(DIFF_H):
                sum_squares(("ssd", h), lambda k: SQD[:, h, :], 256, 1,
                            lambda k: pe.wait_ge(sem("diff_squares"), h + 1))
            linears(("out_c", 0), [(("yc", m), quarters[m]) for m in range(4)], hl, 256,
                    lambda k: pe.wait_ge(sem("diff_out"), k + 1))
            for m in range(4, 8):
                linear(("yc", m), ("out_c", 1), quarters[m % 4], hl, 256, m == 4)
            norm_sum(5, lambda k: SQ1[:, k, :], 256)
            norm_sum(6, lambda k: SQ1[:, k, :], 256)

            for t in range(2):
                b = claim(("lg", t))
                for kt in range(KT):
                    if t == 0:
                        h_ready(3)(kt)
                    i = mm(b[:, 0:E], H[:, kt, T_CTX + 128 * t:T_CTX + 128 * t + 128],
                           param("router", 8 * kt, 8 * kt + 8), kt == 0, kt == KT - 1)
                done(i, ("lg", t))
            for t in range(2):
                for n in range(2):
                    b = claim(("ht", t, n))
                    for j in range(4):
                        i = nc.tensor.transpose(b[:, 128 * j:128 * j + 128],
                                                H[:, 4 * n + j, T_CTX + 128 * t:T_CTX + 128 * t + 128], IDENT)
                    done(i, ("ht", t, n))
            pe.wait_ge(sem("selected"), 1)
            sel = lambda t: RT[:, 64 + 8 * t:72 + 8 * t]
            b = claim(("pos", 0))
            done(mm(b[:, 0:E], const("before"), sel(0), True, True), ("pos", 0))
            b = claim(("pos", 1))
            mm(b[:, 0:E], const("before"), sel(1), True, False)
            done(mm(b[:, 0:E], ONES, sel(0), False, True), ("pos", 1))
            b = claim("cnt")
            mm(b[:, 0:E], ONES, sel(0), True, False)
            done(mm(b[:, 0:E], ONES, sel(1), False, True), "cnt")
            for t in range(2):
                for n in range(2):
                    wait_drained(pe, ("ht", t, n))
            wait_drained(pe, ("pos", 1))
            wait_drained(pe, "cnt")

            def transposed_hidden(e, c, blocks, rows):
                pe.wait_ge(sem("hidden"), EC * e + c + 1)
                for n in range(blocks):
                    for j in range(4):
                        i = nc.tensor.transpose(PS[:, hidden_bank(blocks) + n, 128 * j:128 * j + rows[n]],
                                                HS[0:rows[n], 512 * n + 128 * j:512 * n + 128 * j + 128],
                                                IDENT[0:rows[n], 0:rows[n]])
                i.then_inc(sem("hidden_T"), 1)

            def gather(n, slots=128):
                for kt in range(KT):
                    for t in range(2):
                        i = mm(PS[:, 2 * n + kt // 4, kt % 4 * 128:kt % 4 * 128 + slots],
                               HTOK[:, t, 128 * kt:128 * kt + 128], PSEL[:, t, 128 * n:128 * n + slots], t == 0, t == 1)
                i.then_inc(sem(f"gathered_{n}"), 1)

            def two(out, a, b, first, last):
                mm(out, a[0], b[0], first, False)
                return mm(out, a[0], b[1], False, last)

            def expert(e, blocks, narrow=False, last=False):
                rows = (128, 64 if narrow else 128)
                if blocks == 2:
                    gather(1, rows[1])
                    pe.wait_ge(sem("x_lo_1"), e + 1)
                pe.wait_ge(sem("x_lo_0"), e + 1)
                for kind, c, j in expert_order():
                    if kind == "u" and c and blocks == 2:
                        pe.wait_ge(sem("ht_lo"), EC * e + c)
                    if kind == "d" and c == EC - 1:
                        transposed_hidden(e, c, blocks, rows)
                        if not last:
                            pe.wait_ge(sem("selection"), e + 2)
                            gather(0)
                    if kind == "d":
                        pe.wait_ge(sem("ht_lo"), EC * e + c + 1)
                        if c == 0:
                            pe.wait_ge(sem("gt_copied"), e + 1)
                    for half in range(2):
                        q = j + half
                        h0 = q % SPLITS * PIECE
                        l0 = (n_pre + q) % SLOTS * PIECE
                        pe.wait_ge(sem("lo_made"), PER_EXPERT * e + q + 1)
                        for i in range(4):
                            for n in range(blocks):
                                if kind in "gu":
                                    kt, w = 4 * half + i, 512 * i
                                    out = PS[:, 2 * (kind == "u") + n + turn(blocks, c), :]
                                    x = slice(128 * (KT * n + kt), 128 * (KT * n + kt) + 128)
                                    a, first, end = (XH[:, x], XL[:, x]), kt == 0, kt == KT - 1
                                else:
                                    ft, w = 2 * half + i // 2, 512 * i
                                    out = PS[:, 4 + 2 * n + i % 2, :]
                                    x = slice(512 * n + 128 * ft, 512 * n + 128 * ft + 128)
                                    a, first, end = (HTH[:, x], HTL[:, x]), c == 0 and ft == 0, c == EC - 1 and ft == 3
                                ins = (two if narrow and n else three)(
                                    out, a, (HI[:, h0 + w:h0 + w + 512], LO[:, l0 + w:l0 + w + 512]), first, end)
                        ins.then_inc(sem("piece_used"), 1)
                    if kind == "u" and c == 0:
                        pe.wait_ge(sem("acc_done"), 4 * e + 1)
                        pe.wait_ge(sem("onehots"), e + 1)
                        for n in range(blocks):
                            for t in range(2):
                                i = nc.tensor.transpose(PS[:, 7, 256 * n + 128 * t:256 * n + 128 * t + 128],
                                                        PG[:, t, 128 * n:128 * n + 128], IDENT)
                        i.then_inc(sem("gt_written"), 1)
                        if blocks == 1:
                            nc.tensor.transpose(PS[:, 6, 0:128], IDENT, IDENT).then_inc(sem("gathered_1"), 1)
                    if (kind, c) == (("u", 0) if blocks == 2 else ("g", 1)):
                        transposed_hidden(e, 0, blocks, rows)
                    if kind == "d" and c < EC - 2:
                        transposed_hidden(e, c + 1, blocks, rows)
                pe.wait_ge(sem("y_copied"), e + 1)
                for kt in range(KT):
                    for n in range(blocks):
                        i = mm(PS[:, 4 + kt // 2, 256 * (kt % 2):256 * (kt % 2) + 256],
                               YS[:, D * n + 128 * kt:D * n + 128 * kt + 128], GT[:, n, :], n == 0, n == blocks - 1)
                    if kt % 2:
                        i.then_inc(sem("scattered"), 1)

            pe.wait_ge(sem("flags_ready"), 1)
            pe.wait_ge(sem("selection"), 1)
            gather(0)
            with pe.Fori(0, E - 1) as e:
                kind = pe.value_load(FLAGS[0:1, bass.ds(e, 1)], min_val=0, max_val=2)
                with pe.If(kind < 1):
                    expert(e, 1)
                with pe.If(kind == 1):
                    expert(e, 2, narrow=True)
                with pe.If(kind > 1):
                    expert(e, 2)
            kind = pe.value_load(FLAGS[0:1, E - 1:E], min_val=0, max_val=2)
            with pe.If(kind < 1):
                expert(E - 1, 1, last=True)
            with pe.If(kind == 1):
                expert(E - 1, 2, narrow=True, last=True)
            with pe.If(kind > 1):
                expert(E - 1, 2, last=True)
            pe.wait_ge(sem("moe_squares"), 1)
            for kt in range(KT):
                i = mm(PS[:, 0, 0:256], ONES, SQ7[:, kt, :], kt == 0, kt == KT - 1)
            i.then_inc(sem("moe_sum"), 1)

        @block.scalar
        def _(act):
            count = {}

            def act_do(name, out, in_, func, **kw):
                count[name] = count.get(name, 0) + 1
                nc.scalar.activation(out, in_, func, **kw).then_inc(sem(name), 1)
                act.wait_ge(sem(name), count[name])

            act.wait_ge(sem("param_loaded"), 16)
            nc.scalar.activation(SC_[:], param("c"), ACT.Silu).then_inc(sem("silu_c"), 1)
            wait_piece(act, 0)
            act.dma_start(X, x_dram.rearrange("(k p) t -> p k t", p=128)).then_inc(sem("x_loaded"), 16)

            def mod(*chunks):
                for g in chunks:
                    wait_written(act, ("mod", g))
                    if g:
                        wait_written(act, ("modT", g - 1))
                    drained_by(nc.scalar.activation(MROW[0:2, :], bank(("mod", g))[0:2, :], ACT.Copy), ("mod", g))

            def root(out, n):
                k = 5 + (D, Q_RANK, 2 * DIFF_D).index(n)
                nc.scalar.activation(out, out, ACT.Sqrt, bias=SMALL[:, k:k + 1]).then_inc(sem("rooted"), 1)

            def root_of(name, n, w):
                wait_written(act, name)
                root(bank(name)[:, 0:w], n)

            def squares(src, dst, lo, hi, ready=None):
                for j in range(4):
                    if ready is not None:
                        ready(j)
                    nc.scalar.activation(dst[:, 2 * j:2 * j + 2, :], src[:, 2 * j:2 * j + 2, lo:hi],
                                         ACT.Square).then_inc(sem("squares"), 1)

            def modulate(layer, which, stage, streams):
                act.wait_ge(sem("coefs"), {(0, 0): 1, (0, 2): 2, (1, 0): 3, (1, 2): 5}[layer, which])
                seg = 0 if which == 0 else 3
                for kt in range(KT):
                    if kt % 2 == 0:
                        act.wait_ge(sem("x_scaled"), 4 * stage + kt // 2 + 1)
                    for s in streams:
                        h = H[:, kt, 256 * s:256 * s + 256]
                        i = nc.scalar.activation(h, h, ACT.Identity, scale=COEF[:, 4 * layer + which, kt, s:s + 1],
                                                 bias=MOD[:, 48 * layer + 8 * seg + kt, s:s + 1])
                    i.then_inc(sem("h_ready"), 1)
                    if stage < 3 and kt:
                        input_high(stage, kt - 1)
                if stage < 3:
                    input_high(stage, KT - 1)

            def input_high(stage, kt):
                act.wait_ge(sem("h_ready"), KT * stage + kt + 1)
                nc.scalar.activation(HH[stage][:, kt, :], H[:, kt, :], ACT.Copy).then_inc(sem("h_hi"), 1)

            def split(k):
                wait_piece(act, split_pieces[k])
                wait_high_free(act, k)
                w = piece_width(k)
                nc.scalar.activation(high(k)[:, 0:w], slot(split_pieces[k])[:, 0:w],
                                     ACT.Copy).then_inc(sem("high_made"), 1)

            def copy_out(name, dst, src=None, func=ACT.Copy, **kw):
                wait_written(act, name)
                drained_by(nc.scalar.activation(dst, bank(name) if src is None else src, func, **kw), name)

            mod(0, 1)
            act.wait_ge(sem("x_loaded"), 16)
            squares(X, SQ0, 0, T)
            mod(2, 3)
            act.wait_ge(sem("eps_ready"), 3)
            split(0)
            root_of(("ss", 0), D, T)
            modulate(0, 0, 0, (0, 1))
            split(1)
            split(2)
            mod(4)

            copy_out(("cq", 0), CQ[:, 0, :])
            copy_out(("cq", 1), CQ[:, 1, :])
            split(3)
            copy_out("ckv", CKV)
            wait_written(act, "kr")
            nc.scalar.activation(KR[0:64, :], bank("kr")[0:64, :], ACT.Copy)
            drained_by(nc.scalar.activation(KR[64:128, :], bank("kr")[0:64, :], ACT.Copy), "kr")
            split(4)
            for m, src in enumerate((CQ[:, 0, :], CQ[:, 1, :], CKV)):
                wait_drained(act, (("cq", 0), ("cq", 1), "ckv")[m])
                nc.scalar.activation(SQM[:, m, :], src, ACT.Square).then_inc(sem("mla_squares"), 1)
            for m in range(2):
                copy_out(("gq", m), GQ[:, m, :], scale=DK ** -0.5)
            split(5)
            root_of("ssq", Q_RANK, T)
            root_of("sskv", KV_RANK, T)
            for m in range(2):
                copy_out(("gk", m), GK[:, m, :])
            split(6)
            for t in range(TT):
                copy_out(("gv", t), GV[:, t, :])
            split(7)
            split(8)
            for m in range(4):
                copy_out(("gr", m), GR[:, m, :], func=ACT.Silu)
            for h in range(MLA_H):
                copy_out(("qn", h), QN[:, h, :])
            for h in range(MLA_H):
                copy_out(("kn", h), KN[:, h, :])

            def attend(steps):
                for kind, u in steps:
                    if kind == "s":
                        keys = (2 if u % TT < 2 else 4) * 128
                        act.wait_ge(sem("mla_max"), u + 1)
                        if u >= 3:
                            wait_written(act, ("pT", u - 3))
                        drained_by(nc.scalar.activation(PB[:, u % 3, 0:keys], bank(("s", u))[:, 0:keys], ACT.Exp,
                                                        bias=STAT[:, u:u + 1], scale=MLA_SCALE,
                                                        accum_out=STAT[:, 32 + u:33 + u]), ("s", u))
                    elif kind == "pT":
                        n = 2 if u % TT < 2 else 4
                        g, q = u // 2, u % 2
                        if g >= 2:
                            wait_written(act, ("o", g - 2))
                        copy_out(("pT", u), PT[:, g % 2, 0:n, 128 * q:128 * q + 128],
                                 bank(("pT", u))[:, 0:128 * n].rearrange("p (k q) -> p k q", q=128))
                    elif kind in ("s1", "s2"):
                        j = kind == "s2"
                        act.wait_ge(sem("diff_max"), 2 * u + j + 1)
                        if u >= 3:
                            wait_written(act, ("dT", u - 3))
                        drained_by(nc.scalar.activation((E2 if j else E1)[:, u % 3, :], bank((kind, u)), ACT.Exp,
                                                        bias=STAT[:, 16 * j + u:16 * j + u + 1], scale=DIFF_SCALE,
                                                        accum_out=STAT[:, 32 + 16 * j + u:33 + 16 * j + u]), (kind, u))
                    elif kind == "dT":
                        g, q = u // 2, u % 2
                        if u == 0:
                            mod(22)
                        if g >= 2:
                            wait_written(act, ("do", g - 2))
                        copy_out(("dT", u), PT1[:, g % 2, :, 128 * q:128 * q + 128],
                                 bank(("dT", u)).rearrange("p (k q) -> p k q", q=128))
                    elif kind == "do":
                        wait_written(act, ("do", u))
                        nc.scalar.activation(SQD[:, u, :], bank(("do", u))[:, 0:256],
                                             ACT.Square).then_inc(sem("diff_squares"), 1)

            act.wait_ge(sem("gate_abs"), 1)
            act_do("act_gate", LE, LE, ACT.Exp)
            act.wait_ge(sem("gate_plus"), 1)
            act_do("act_gate", LE, LE, ACT.Ln)
            mod(5)

            attend(mla_steps())

            for d in range(2):
                for k in range(2):
                    copy_out(("cum", d, k), CUM[:, 2 * d + k, :])
            for d in range(2):
                for k in range(2):
                    wait_drained(act, ("cum", d, k))
                nc.scalar.activation(QH[:, 2 * d:2 * d + 2, :], CUM[:, 2 * d:2 * d + 2, :],
                                     ACT.Exp).then_inc(sem("decay_exp"), 1)
                act.wait_ge(sem("key_exponents"), d + 1)
                nc.scalar.activation(EX[:, d, :], EX[:, d, :], ACT.Exp).then_inc(sem("key_exp"), 1)
                edge = 63 if d == 0 else 0
                nc.scalar.activation(STAT[:, 64 + 16 * d:80 + 16 * d].rearrange("p (k c) -> p k c", c=8),
                                     CUM[:, 2 * d:2 * d + 2, edge::CHUNK], ACT.Exp).then_inc(sem("chunk_decay"), 1)
            mod(6)
            for t in range(2 * TT):
                if t == TT:
                    mod(7)
                name = ("kT", t // TT, t % TT)
                copy_out(name, KHT[:, t, :], bank(name)[:, 0:256])
            for n in range(12):
                act.wait_ge(sem("level_exponents"), n + 1)
                nc.scalar.activation(EX[:, n % 2, :], EX[:, n % 2, :], ACT.Exp).then_inc(sem("level_exp"), 1)
                if n - 2 in MOD_LEVELS:
                    mod(MOD_LEVELS[n - 2])
            mod(13)
            for h in range(GLA_H):
                wait_written(act, ("og", h))
                nc.scalar.activation(EX[:, h // 2, T * (h % 2):T * (h % 2) + T], bank(("og", h)),
                                     ACT.Square).then_inc(sem("gla_squares"), 1)
            mod(14)
            for h in range(GLA_H):
                root_of(("ssg", h), DV, T)

            for m in range(8):
                copy_out(("ya", m), YO[:, m, :])
            for m in range(8):
                wait_drained(act, ("ya", m))
            squares(YO, SQY, 0, T)
            mod(15)
            root_of(("ss", 1), D, T)

            def x_ready(base):
                return lambda j: act.wait_ge(sem("x_ready"), base + 2 * j + 2)

            squares(X, SQY, 0, T, x_ready(0))
            mod(16, 17)
            k0 = STAGE_PIECES[1][0]
            split(k0)
            root_of(("ss", 2), D, T)
            modulate(0, 2, 1, (0, 1))
            split(k0 + 1)
            split(k0 + 2)
            mod(18)
            for n in range(FT // 2):
                for m in (2 * n, 2 * n + 1):
                    wait_written(act, ("g", m))
                    drained_by(nc.scalar.activation(FF[:, m, :], bank(("g", m)), ACT.Silu), ("g", m))
                for k in (2 * n + 3, 2 * n + 4):
                    if k < FT:
                        split(k0 + k)
            wait_written(act, ("u", FT - 1))
            k0 = STAGE_PIECES[2][0]
            split(k0)
            wait_drained(act, ("u", FT_SPLIT - 1))
            for a, b, hi in FF_HIGH:
                nc.scalar.activation(hi, A_[:, 8192 + T * a:8192 + T * b], ACT.Copy).then_inc(sem("ff_high"), 1)
            split(k0 + 1)
            for m in range(8):
                copy_out(("yf", m), YO[:, m, :])
                if m + 2 < 8:
                    split(k0 + m + 2)
            for m in range(8):
                wait_drained(act, ("yf", m))
            squares(YO, SQY, 0, T)
            mod(19)
            act.wait_ge(sem("lam_logits"), 1)
            act_do("lam_exp", SMALL[:, 8:10], SMALL[:, 8:10], ACT.Exp)
            root_of(("ss", 3), D, T)
            k0 = STAGE_PIECES[3][0]
            split(k0)
            squares(X, SQY, 0, T, x_ready(8))
            mod(20)
            root_of(("ss", 4), D, T)
            modulate(1, 0, 2, (0, 1))
            split(k0 + 1)
            split(k0 + 2)
            mod(21)
            for i, n in enumerate(QK_ORDER):
                for m in (2 * n, 2 * n + 1):
                    if m < 8:
                        copy_out(("qk", m), Q1[:, m, :], bank(("qk", m))[:, 0:256])
                    else:
                        copy_out(("qk", m), K1[:, m - 8, :])
                split(k0 + i + 3)
            split(k0 + 11)
            attend(diff_steps())
            mod(23)
            for h in range(DIFF_H):
                root_of(("ssd", h), 2 * DIFF_D, 256)
            for m in range(8):
                copy_out(("yc", m), YO1[:, m, :], bank(("yc", m))[:, 0:256])
            for m in range(8):
                wait_drained(act, ("yc", m))
            squares(YO1, SQ1, 0, 256)
            root_of(("ss", 5), D, 256)
            squares(X, SQ1, T_CTX, T, x_ready(16))
            root_of(("ss", 6), D, 256)
            modulate(1, 2, 3, (1,))
            for t in range(2):
                for n in range(2):
                    copy_out(("ht", t, n), HTOK[:, t, 512 * n:512 * n + 512])
            act.wait_ge(sem("gate_logits"), 1)
            act_do("gate_exp", RT[:, 40:42], RT[:, 40:42], ACT.Exp)

            def expert_high(e, q):
                n = n_pre + q
                act.wait_ge(loaded[n % SLOTS], 16 * (PER_EXPERT // SLOTS * e + (n // SLOTS + 1)))
                if q >= SPLITS:
                    act.wait_ge(sem("piece_used"), PER_EXPERT * e + (q - SPLITS + 1))
                nc.scalar.activation(HI[:, q % SPLITS * PIECE:(q % SPLITS + 1) * PIECE], slot(n),
                                     ACT.Copy).then_inc(sem("hi_made"), 1)

            def tokens_high(n, e, narrow=False):
                act.wait_ge(sem(f"gathered_{n}"), e + 1)
                if narrow:
                    nc.scalar.activation(halves(XH, 1024, 0), narrow_tokens(), ACT.Copy).then_inc(sem("x_hi_1"), 1)
                    return
                nc.scalar.activation(XH[:, 1024 * n:1024 * n + 1024], banks(2 * n, 2),
                                     ACT.Copy).then_inc(sem(f"x_hi_{n}"), 1)

            def expert(e, blocks, narrow=False, last=False):
                if not narrow:
                    nc.scalar.activation(TMP[:, 2:3], SMALL[:, 5:6], ACT.Copy).then_inc(sem("low_rows"), EC)
                if blocks == 2:
                    tokens_high(1, e, narrow)
                else:
                    nc.scalar.activation(TMP[:, 0:1], SMALL[:, 5:6], ACT.Copy).then_inc(sem("x_hi_1"), 1)
                for kind, c in vector_order(blocks):
                    if kind == "split" and c > 1:
                        expert_high(e, c)
                    elif kind == "scatter_matrix":
                        act.wait_ge(sem("gt_written"), e + 1)
                        nc.scalar.activation(GT[:, 0:blocks, :].rearrange("p n t -> p (n t)"),
                                             PS[:, 7, 0:256 * blocks], ACT.Copy).then_inc(sem("gt_copied"), 1)
                    elif kind == "hidden":
                        act.wait_ge(sem("piece_used"), PER_EXPERT * e + piece_of("u", c) + 2)
                        if narrow:
                            nc.scalar.activation(MERGE, PS[64:128, 1:4:2, :], ACT.Copy).then_inc(sem("low_rows"), 1)
                            act.wait_ge(sem("merged"), EC * e + c + 1)
                        b = turn(blocks, c)
                        nc.scalar.activation(by_block(HS, blocks), PS[:, b:b + blocks, :],
                                             ACT.Silu).then_inc(sem("silu"), 1)
                    elif kind == "transposed":
                        act.wait_ge(sem("hidden_T"), EC * e + c + 1)
                        b = hidden_bank(blocks)
                        if narrow:
                            nc.scalar.activation(HTH[:, 0:512], PS[:, b, :], ACT.Copy)
                            nc.scalar.activation(halves(HTH, 512, 0), narrow_hidden(b + 1),
                                                 ACT.Copy).then_inc(sem("ht_hi"), 1)
                        else:
                            nc.scalar.activation(by_block(HTH, blocks), PS[:, b:b + blocks, :],
                                                 ACT.Copy).then_inc(sem("ht_hi"), 1)
                if not last:
                    tokens_high(0, e + 1)
                    for q in range(2):
                        act.wait_ge(sem("piece_used"), PER_EXPERT * e + (PER_EXPERT - SPLITS + q + 1))
                        expert_high(e + 1, q)
                act.wait_ge(sem("piece_used"), PER_EXPERT * e + PER_EXPERT)
                nc.scalar.activation(YS[:, 0:1024 * blocks], banks(4, 2 * blocks), ACT.Copy).then_inc(sem("y_copied"), 1)

            act.wait_ge(sem("flags_ready"), 1)
            for q in range(2):
                expert_high(0, q)
            tokens_high(0, 0)
            with act.Fori(0, E - 1) as e:
                kind = act.value_load(FLAGS[0:1, bass.ds(e, 1)], min_val=0, max_val=2)
                with act.If(kind < 1):
                    expert(e, 1)
                with act.If(kind == 1):
                    expert(e, 2, narrow=True)
                with act.If(kind > 1):
                    expert(e, 2)
            kind = act.value_load(FLAGS[0:1, E - 1:E], min_val=0, max_val=2)
            with act.If(kind < 1):
                expert(E - 1, 1, last=True)
            with act.If(kind == 1):
                expert(E - 1, 2, narrow=True, last=True)
            with act.If(kind > 1):
                expert(E - 1, 2, last=True)
            act.wait_ge(sem("moe_sum"), 1)
            root(PS[:, 0, 0:256], D)

        @block.vector
        def _(dve):
            count = {}
            V_ = nc.vector

            def do(ins, name="dve_step"):
                count[name] = count.get(name, 0) + 1
                ins.then_inc(sem(name), 1)
                dve.wait_ge(sem(name), count[name])

            def drain(ins, name):
                drained_by(ins, name)
                wait_drained(dve, name)

            def mod(*chunks):
                for g in chunks:
                    wait_written(dve, ("modT", g))
                    b = bank(("modT", g))[:, 0:8].rearrange("p (m s) -> p m s", s=2)
                    bias = param("b_mod", 4 * g, 4 * g + 4).unsqueeze(2)
                    drain(V_.tensor_tensor(MOD[:, 4 * g:4 * g + 4, :], b, bias.to_broadcast([128, 4, 2]), ALU.add),
                          ("modT", g))

            def coefs(layer, *which):
                for w in which:
                    seg, gain, one = ((1, "g_pre_mix", 1.0), (2, "g_post_mix", 0.0),
                                      (4, "g_pre_ffn", 1.0), (5, "g_post_ffn", 0.0))[w]
                    c = COEF[:, 4 * layer + w, :, :]
                    m = MOD[:, 48 * layer + 8 * seg:48 * layer + 8 * seg + 8, :]
                    g = param(gain, 8 * layer, 8 * layer + 8).unsqueeze(2).to_broadcast([128, 8, 2])
                    do(V_.tensor_scalar(c, m, one, math.sqrt(D), ALU.add, ALU.mult))
                    do(V_.tensor_tensor(c, c, g, ALU.mult), "coefs" if w == which[-1] else "dve_step")

            def rstd(name, out, n, width):
                count["rooted"] = count.get("rooted", 0) + 1
                dve.wait_ge(sem("rooted"), count["rooted"])
                drain(V_.reciprocal(out, bank(name)[:, 0:width]), name)

            def scaled(i, src, lo, hi, stage=None):
                w = hi - lo
                rstd(("ss", i), RST[:, 0:w], D, w)
                for j in range(4):
                    if stage is not None and j >= 2:
                        input_low(stage, 2 * j - 4)
                        input_low(stage, 2 * j - 3)
                    V_.tensor_tensor(H[:, 2 * j:2 * j + 2, lo:hi], src[:, 2 * j:2 * j + 2, lo:hi],
                                     RST[:, 0:w].unsqueeze(1).to_broadcast([128, 2, w]),
                                     ALU.mult).then_inc(sem("x_scaled"), 1)
                if stage is not None:
                    for kt in range(4, KT):
                        input_low(stage, kt)

            def input_low(stage, kt):
                dve.wait_ge(sem("h_hi"), KT * stage + kt + 1)
                V_.tensor_tensor(HL[:, kt, :], H[:, kt, :], HH[stage][:, kt, :].bitcast(f32),
                                 ALU.subtract).then_inc(sem("h_lo"), 1)

            def split(k):
                dve.wait_ge(sem("high_made"), k + 1)
                w = piece_width(k)
                V_.tensor_tensor(low(k)[:, 0:w], slot(split_pieces[k])[:, 0:w], high(k)[:, 0:w].bitcast(f32),
                                 ALU.subtract).then_inc(sem("low_made"), 1)

            def residual(i, y, layer, which, streams, ready="x_ready"):
                w = 256 * len(streams)
                if i is not None:
                    rstd(("ss", i), RST[:, 0:w], D, w)
                for j in range(4):
                    do(V_.tensor_tensor(y[:, 2 * j:2 * j + 2, 0:w], y[:, 2 * j:2 * j + 2, 0:w],
                                        RST[:, 0:w].unsqueeze(1).to_broadcast([128, 2, w]), ALU.mult))
                for kt in range(KT):
                    for n, s in enumerate(streams):
                        x = X[:, kt, 256 * s:256 * s + 256]
                        ins = V_.scalar_tensor_tensor(x, y[:, kt, 256 * n:256 * n + 256],
                                                      COEF[:, 4 * layer + which, kt, s:s + 1], x, ALU.mult, ALU.add)
                    ins.then_inc(sem(ready), 1)
                    count[ready] = count.get(ready, 0) + 1
                dve.wait_ge(sem(ready), count[ready])

            for j, n in enumerate((D, Q_RANK, 2 * DIFF_D)):
                do(V_.memset(SMALL[:, 5 + j:6 + j], n * EPS), "eps_ready")
            dve.wait_ge(sem("param_loaded"), 16)
            for a, b, name, f in ((0, 2, "g_q", math.sqrt(Q_RANK)), (2, 3, "g_kv", math.sqrt(KV_RANK)),
                                  (3, 4, "g_gla", math.sqrt(DV)), (4, 5, "g_diff", math.sqrt(2 * DIFF_D) * (1.0 - LAM_INIT))):
                do(V_.tensor_scalar(SMALL[:, a:b], param(name), f, None, ALU.mult))
            for j, (a, b) in enumerate((("lq1", "lk1"), ("lq2", "lk2"))):
                do(V_.tensor_tensor(TMP[:, 0:64], param(a), param(b), ALU.mult))
                do(V_.reduce_sum(SMALL[:, 8 + j:9 + j], TMP[:, 0:64], axis=AX.X), ("dve_step", "lam_logits")[j])
            mod(0, 1, 2, 3)
            coefs(0, 0)
            split(0)
            scaled(0, X, 0, T, 0)
            for k in range(1, 6):
                split(k)

            for name, parts in (("ssq", ((CQ[:, 0, :], 0), (CQ[:, 1, :], 1))), ("sskv", ((CKV, 2),))):
                rstd(name, RST[:], Q_RANK if name == "ssq" else KV_RANK, T)
                dve.wait_ge(sem("mla_squares"), 3)
                for part, g in parts:
                    do(V_.scalar_tensor_tensor(part, part, SMALL[:, g:g + 1], RST[:], ALU.mult, ALU.mult), "lora_normed")
            for k in (6, 7, 8):
                split(k)
            for d, name in enumerate(("af", "ab")):
                wait_written(dve, name)
                drain(V_.tensor_copy(AF[0:16, d, :], bank(name)[0:16, :]), name)
            for p in range(2):
                wait_written(dve, ("qr", p))
                drain(V_.tensor_copy(QR[:, p, :], bank(("qr", p))), ("qr", p))
            for t in range(TT):
                wait_written(dve, ("v", t))
                drain(V_.tensor_copy(V[:, t, :], bank(("v", t))), ("v", t))
            for name, x in ((("rotq", 0), QR[:, 0, T_CTX:T]), (("rotq", 1), QR[:, 1, T_CTX:T]), ("rotk", KR[:, T_CTX:T])):
                wait_written(dve, name)
                drain(V_.tensor_tensor(TMP[:, 0:256], bank(name)[:, 0:256], const("sin"), ALU.mult), name)
                do(V_.tensor_tensor(x, x, const("cos"), ALU.mult))
                do(V_.tensor_tensor(x, x, TMP[:, 0:256], ALU.add), "mla_roped")
            for t in range(TT):
                wait_written(dve, ("gx", t))
                drain(V_.tensor_tensor(LX[:, t, :], bank(("gx", t)), param("b_gate"), ALU.add), ("gx", t))

            def attend(steps):
                for kind, u in steps:
                    if kind == "s":
                        keys = (2 if u % TT < 2 else 4) * 128
                        wait_written(dve, ("s", u))
                        do(V_.reduce_max(STAT[:, u:u + 1], bank(("s", u))[:, 0:keys], axis=AX.X))
                        do(V_.tensor_scalar(STAT[:, u:u + 1], STAT[:, u:u + 1], -MLA_SCALE, None, ALU.mult), "mla_max")
                    elif kind == "pT":
                        keys = (2 if u % TT < 2 else 4) * 128
                        wait_drained(dve, ("s", u))
                        do(V_.reciprocal(STAT[:, 32 + u:33 + u], STAT[:, 32 + u:33 + u]))
                        do(V_.tensor_scalar(PB[:, u % 3, 0:keys], PB[:, u % 3, 0:keys], STAT[:, 32 + u:33 + u], None,
                                            ALU.mult), "probs")
                    elif kind == "o":
                        wait_written(dve, ("o", u))
                        drain(V_.tensor_copy(H[:, u // 2, 256 * (u % 2):256 * (u % 2) + 256], bank(("o", u))[:, 0:256]),
                              ("o", u))
                    elif kind in ("s1", "s2"):
                        j = kind == "s2"
                        c = 16 * j + u
                        wait_written(dve, (kind, u))
                        do(V_.reduce_max(STAT[:, c:c + 1], bank((kind, u)), axis=AX.X))
                        do(V_.tensor_scalar(STAT[:, c:c + 1], STAT[:, c:c + 1], -DIFF_SCALE, None, ALU.mult), "diff_max")
                    elif kind == "dT":
                        wait_drained(dve, ("s1", u))
                        wait_drained(dve, ("s2", u))
                        do(V_.reciprocal(STAT[:, 32 + u:33 + u], STAT[:, 32 + u:33 + u]))
                        do(V_.reciprocal(STAT[:, 48 + u:49 + u], STAT[:, 48 + u:49 + u]))
                        do(V_.tensor_scalar(E2[:, u % 3, :], E2[:, u % 3, :], STAT[:, 48 + u:49 + u], SMALL[:, 10:11],
                                            ALU.mult, ALU.mult))
                        do(V_.scalar_tensor_tensor(E1[:, u % 3, :], E1[:, u % 3, :], STAT[:, 32 + u:33 + u],
                                                   E2[:, u % 3, :], ALU.mult, ALU.subtract), "diff_probs")
                        if u == 0:
                            mod(21)
                    elif kind == "do":
                        dve.wait_ge(sem("diff_squares"), u + 1)
                        drain(V_.tensor_copy(OD[:, u, :], bank(("do", u))[:, 0:256]), ("do", u))

            do(V_.scalar_tensor_tensor(LE, LX, -1.0, LX, ALU.mult, ALU.min), "gate_abs")
            dve.wait_ge(sem("act_gate"), 1)
            do(V_.tensor_scalar(LE, LE, 1.0, None, ALU.add), "gate_plus")
            dve.wait_ge(sem("act_gate"), 2)
            do(V_.scalar_tensor_tensor(LX, LX, 0.0, LE, ALU.min, ALU.subtract), "log_decays")
            mod(4)
            attend(vector_steps(mla_steps()))

            def cum_of(d, k):
                return CUM[:, 2 * d + k, :].rearrange("p (c i) -> p c i", i=CHUNK)

            for h in range(GLA_H):
                wait_written(dve, ("att", "diag", h))
                a = ATT[:, h, :].rearrange("p (c t) -> p c t", t=128)
                drained_by(V_.tensor_tensor(a, bank(("att", "diag", h)).rearrange("p (c t) -> p c t", t=128),
                                            const("diag2").unsqueeze(1).to_broadcast([128, TT, 128]), ALU.mult),
                           ("att", "diag", h))
            for h in range(GLA_H):
                wait_drained(dve, ("att", "diag", h))
            for d in range(2):
                for k in range(2):
                    wait_drained(dve, ("cum", d, k))
                    edge = 63 if d == 0 else 0
                    last = cum_of(d, k)[:, :, edge:edge + 1].to_broadcast([128, 8, CHUNK])
                    do(V_.tensor_tensor(EX[:, d, T * k:T * k + T].rearrange("p (c i) -> p c i", i=CHUNK), last,
                                        cum_of(d, k), ALU.subtract), ("dve_step", "key_exponents")[k])
                dve.wait_ge(sem("decay_exp"), d + 1)
                do(V_.tensor_tensor(QH[:, 2 * d:2 * d + 2, :], QH[:, 2 * d:2 * d + 2, :], GQ, ALU.mult), "decayed_queries")
                dve.wait_ge(sem("key_exp"), d + 1)
                do(V_.tensor_tensor(AA[:, d, :], EX[:, d, :], A_[:, 1024:2048], ALU.mult), "decayed_keys")

            def exponents(n):
                d, m = n // 6, LEVELS[n % 6]
                cum = A_[:, m0 + 1024 * d:m0 + 1024 * d + 1024].rearrange("p (b u m) -> p b u m", u=2, m=m)
                ex = EX[:, n % 2, :].rearrange("p (b u m) -> p b u m", u=2, m=m)
                nb = 2 * T // (2 * m)
                ref = (cum[:, :, 0, m - 1:m] if d == 0 else cum[:, :, 1, 0:1]).to_broadcast([128, nb, m])
                qh = 1 - d
                V_.tensor_tensor(ex[:, :, qh, :], cum[:, :, qh, :], ref, ALU.subtract)
                do(V_.tensor_tensor(ex[:, :, 1 - qh, :], ref, cum[:, :, 1 - qh, :], ALU.subtract), "level_exponents")

            def decayed(n):
                d, m = n // 6, LEVELS[n % 6]
                qh = 1 - d
                blocks = lambda a: a.rearrange("p (b u m) -> p b u m", u=2, m=m)
                dve.wait_ge(sem("level_exp"), n + 1)
                if n < 2:
                    for t in range(TT):
                        wait_written(dve, ("kT", n, t))
                else:
                    wait_written(dve, ("att", ((n - 2) // 6, (n - 2) % 6), 3))
                V_.tensor_tensor(blocks(AA[:, n % 2, :])[:, :, qh, :], blocks(EX[:, n % 2, :])[:, :, qh, :],
                                 blocks(A_[:, 0:1024])[:, :, qh, :], ALU.mult)
                do(V_.tensor_tensor(blocks(AA[:, n % 2, :])[:, :, 1 - qh, :], blocks(EX[:, n % 2, :])[:, :, 1 - qh, :],
                                    blocks(A_[:, 1024:2048])[:, :, 1 - qh, :], ALU.mult), "level_ready")

            def add_scores(n):
                mask = C[:, CONST["masks"][0] + 128 * n:CONST["masks"][0] + 128 * n + 128].bitcast(u32)
                for h in range(GLA_H):
                    name = ("att", (n // 6, n % 6), h)
                    wait_written(dve, name)
                    drained_by(V_.copy_predicated(ATT[:, h, :].rearrange("p (c t) -> p c t", t=128),
                                                  mask.unsqueeze(1).to_broadcast([128, TT, 128]),
                                                  bank(name).rearrange("p (c t) -> p c t", t=128)), name)
                for h in range(GLA_H):
                    wait_drained(dve, ("att", (n // 6, n % 6), h))

            exponents(0)
            mod(5)
            exponents(1)
            mod(6)
            decayed(0)
            for n in range(12):
                if n + 1 < 12:
                    decayed(n + 1)
                if n + 2 < 12:
                    exponents(n + 2)
                add_scores(n)
                if n in MOD_LEVELS:
                    mod(MOD_LEVELS[n] - 1)
            coefs(0, 1, 2, 3)
            for d in range(2):
                dve.wait_ge(sem("chunk_decay"), d + 1)
            for d in range(2):
                for p in range(2):
                    left = [c for c in chunk_order[d]][:-1]
                    lasts = {r: [c for c in left if c % 2 == r][-1] for r in range(2)}
                    for r in range(2):
                        wait_written(dve, ("U", d, p, r))
                    for j, c in enumerate(left):
                        nxt = chunk_order[d][j + 1]
                        name = ("U", d, p, c % 2)
                        u = bank(name)[:, 128 * (c // 2):128 * (c // 2) + 128]
                        if j == 0:
                            ins = V_.tensor_copy(state(d, p, nxt), u)
                        else:
                            k = 64 + 16 * d + 8 * p + c
                            ins = V_.scalar_tensor_tensor(state(d, p, nxt), state(d, p, c), STAT[:, k:k + 1], u,
                                                          ALU.mult, ALU.add)
                        if lasts[c % 2] == c:
                            drain(ins, name)
                        else:
                            do(ins, "states_step")
            mod(12)
            for h in range(GLA_H):
                dve.wait_ge(sem("gla_squares"), h + 1)
                drain(V_.tensor_copy(AA[:, h // 2, T * (h % 2):T * (h % 2) + T], bank(("og", h))), ("og", h))
            mod(13)
            for h in range(GLA_H):
                rstd(("ssg", h), RST[:], DV, T)
                y = H[:, 4 + h, :]
                do(V_.scalar_tensor_tensor(y, AA[:, h // 2, T * (h % 2):T * (h % 2) + T], SMALL[:, 3:4], RST[:],
                                           ALU.mult, ALU.mult))
                do(V_.tensor_tensor(y, y, GR[:, h, :], ALU.mult), "gla_out")

            def after_drained(names):
                for x in names:
                    wait_drained(dve, x)

            mod(14)
            after_drained([("ya", m) for m in range(8)])
            residual(1, YO, 0, 1, (0, 1))
            mod(15, 16)
            coefs(1, 0)
            k0 = STAGE_PIECES[1][0]
            split(k0)
            scaled(2, X, 0, T, 1)
            split(k0 + 1)
            split(k0 + 2)
            mod(17)
            coefs(1, 1)
            for n in range(FT // 2):
                if 2 * n + 3 < FT:
                    split(k0 + 2 * n + 3)
                for m in (2 * n, 2 * n + 1):
                    wait_written(dve, ("u", m))
                    wait_drained(dve, ("g", m))
                    drain(V_.tensor_tensor(FF[:, m, :], FF[:, m, :], bank(("u", m)), ALU.mult), ("u", m))
                if 2 * n + 4 < FT:
                    split(k0 + 2 * n + 4)
            k0 = STAGE_PIECES[2][0]
            split(k0)
            for i, (a, b, hi) in enumerate(FF_HIGH):
                dve.wait_ge(sem("ff_high"), i + 1)
                V_.tensor_tensor(FF_LOW[:, T * a:T * b], A_[:, 8192 + T * a:8192 + T * b], hi.bitcast(f32),
                                 ALU.subtract).then_inc(sem("ff_low"), 1)
            for k in range(1, 8):
                split(k0 + k)
            mod(18)
            after_drained([("yf", m) for m in range(8)])
            residual(3, YO, 0, 3, (0, 1))
            k0 = STAGE_PIECES[3][0]
            mod(19)
            split(k0)
            scaled(4, X, 0, T, 2)
            for k in range(1, 11):
                split(k0 + k)
                if k == 2:
                    mod(20)
            dve.wait_ge(sem("lam_exp"), 1)
            do(V_.tensor_tensor(SMALL[:, 10:11], SMALL[:, 8:9], SMALL[:, 9:10], ALU.subtract))
            do(V_.tensor_scalar(SMALL[:, 10:11], SMALL[:, 10:11], LAM_INIT, None, ALU.add))
            for n in range(2):
                for t in range(TT):
                    wait_written(dve, ("v1", t, n))
                    drained_by(V_.tensor_copy(V1[:, t, 512 * n:512 * n + 512], bank(("v1", t, n))), ("v1", t, n))
                if n == 0:
                    split(k0 + 11)
            for m in range(8):
                wait_written(dve, ("rot", m))
                s2 = const("sin").unsqueeze(1).to_broadcast([128, 2, 256])
                drain(V_.tensor_tensor(TMP[:].rearrange("p (a b) -> p a b", b=256),
                                       bank(("rot", m)).rearrange("p (a b) -> p a b", b=256), s2, ALU.mult), ("rot", m))
                for j, x in enumerate((Q1[:, m, :], K1[:, m, T_CTX:T])):
                    do(V_.tensor_tensor(x, x, const("cos"), ALU.mult))
                    do(V_.tensor_tensor(x, x, TMP[:, 256 * j:256 * j + 256], ALU.add), ("dve_step", "diff_roped")[j])
            attend(vector_steps(diff_steps()))
            mod(22, 23)
            coefs(1, 2, 3)
            for h in range(DIFF_H):
                rstd(("ssd", h), RST[:, 0:256], 2 * DIFF_D, 256)
                do(V_.scalar_tensor_tensor(H[:, h, T_CTX:T], OD[:, h, :], SMALL[:, 4:5], RST[:, 0:256], ALU.mult,
                                           ALU.mult), "diff_out")
            after_drained([("yc", m) for m in range(8)])
            residual(5, YO1, 1, 1, (1,))
            scaled(6, X, T_CTX, T)

            LG, RK, SEL = view(RT, 0, 2, E), view(RT, 48, 2, E), view(RT, 64, 2, E)
            GATE, SPOS, CMP = view(RT, 80, 2, E), view(RT, 96, 2, E), view(RT, 128, 8, 8)
            CMQ = view(RT, 192, 8, 8)
            for t in range(2):
                wait_written(dve, ("lg", t))
                drain(V_.tensor_copy(LG[:, t, :], bank(("lg", t))[:, 0:E]), ("lg", t))
                do(V_.max(RT[:, 16 + 8 * t:24 + 8 * t], LG[:, t, :]))
                do(V_.tensor_tensor(RT[:, 40 + t:41 + t], RT[:, 17 + 8 * t:18 + 8 * t], RT[:, 16 + 8 * t:17 + 8 * t],
                                    ALU.subtract), ("dve_step", "gate_logits")[t])
            for t in range(2):
                other = LG[:, t, :].unsqueeze(1).to_broadcast([128, 8, 8])
                own = LG[:, t, :].unsqueeze(2).to_broadcast([128, 8, 8])
                do(V_.tensor_tensor(CMP, other, own, ALU.is_gt))
                do(V_.tensor_tensor(CMQ, other, own, ALU.is_equal))
                do(V_.tensor_tensor(CMQ, CMQ, const("lower8").rearrange("p (a b) -> p a b", b=8), ALU.mult))
                do(V_.tensor_tensor(CMP, CMP, CMQ, ALU.add))
                do(V_.reduce_sum(RK[:, t, :], CMP, axis=AX.X))
            do(V_.tensor_scalar(SEL, RK, 2.0, None, ALU.is_lt), "selected")
            dve.wait_ge(sem("gate_exp"), 1)
            do(V_.tensor_scalar(RT[:, 42:44], RT[:, 40:42], 1.0, None, ALU.add))
            do(V_.reciprocal(RT[:, 42:44], RT[:, 42:44]))
            do(V_.tensor_tensor(RT[:, 44:46], RT[:, 42:44], RT[:, 40:42], ALU.mult))
            for t in range(2):
                do(V_.tensor_scalar(GATE[:, t, :], RK[:, t, :], 0.0, RT[:, 42 + t:43 + t], ALU.is_equal, ALU.mult))
                do(V_.tensor_scalar(CMQ[:, 0, :], RK[:, t, :], 1.0, RT[:, 44 + t:45 + t], ALU.is_equal, ALU.mult))
                do(V_.tensor_tensor(GATE[:, t, :], GATE[:, t, :], CMQ[:, 0, :], ALU.add))
            for t in range(2):
                wait_written(dve, ("pos", t))
                drain(V_.scalar_tensor_tensor(SPOS[:, t, :], bank(("pos", t))[:, 0:E], 1000.0, SEL[:, t, :], ALU.add,
                                              ALU.mult), ("pos", t))
            do(V_.tensor_scalar(SPOS, SPOS, -1000.0, None, ALU.add))
            wait_written(dve, "cnt")
            do(V_.tensor_scalar(CMP[:, 0, :], bank("cnt")[:, 0:E], 192.0, None, ALU.is_gt))
            drain(V_.scalar_tensor_tensor(FLAGS[:], bank("cnt")[:, 0:E], 128.0, CMP[:, 0, :], ALU.is_gt, ALU.add), "cnt")
            do(V_.memset(RT[:, 120:121], 0.0), "flags_ready")
            for t in range(2):
                for n in range(2):
                    wait_written(dve, ("ht", t, n))
            do(V_.memset(ACC, 0.0), "acc_done")

            def selection(e, weighted, narrow=False):
                for t in range(2):
                    if weighted and narrow:
                        for at, iota in ((0, const("iota")[:, 0:192]), (192, const("iota")[:, 128:192])):
                            ins = V_.tensor_scalar(PG[:, t, at:at + iota.shape[-1]], iota, SPOS[:, t, bass.ds(e, 1)],
                                                   GATE[:, t, bass.ds(e, 1)], ALU.is_equal, ALU.mult)
                    elif weighted:
                        ins = V_.tensor_scalar(PG[:, t, :], const("iota"), SPOS[:, t, bass.ds(e, 1)], GATE[:, t, bass.ds(e, 1)],
                                               ALU.is_equal, ALU.mult)
                    else:
                        ins = V_.tensor_scalar(PSEL[:, t, :], const("iota"), SPOS[:, t, bass.ds(e, 1)], None, ALU.is_equal)
                ins.then_inc(sem("onehots" if weighted else "selection"), 1)

            def expert_low(e, q):
                n = n_pre + q
                dve.wait_ge(sem("hi_made"), PER_EXPERT * e + q + 1)
                l0 = n % SLOTS * PIECE
                V_.tensor_tensor(LO[:, l0:l0 + PIECE], slot(n),
                                 HI[:, q % SPLITS * PIECE:(q % SPLITS + 1) * PIECE].bitcast(f32),
                                 ALU.subtract).then_inc(sem("lo_made"), 1)

            def tokens_low(n, e, narrow=False):
                dve.wait_ge(sem(f"x_hi_{n}"), e + 1)
                if narrow:
                    V_.tensor_tensor(halves(XH, 1024, 1), narrow_tokens(), halves(XH, 1024, 0).bitcast(f32), ALU.subtract).then_inc(sem("x_lo_1"), 1)
                    return
                w = slice(1024 * n, 1024 * n + 1024)
                V_.tensor_tensor(XL[:, w], banks(2 * n, 2), XH[:, w].bitcast(f32),
                                 ALU.subtract).then_inc(sem(f"x_lo_{n}"), 1)

            def expert(e, blocks, narrow=False, last=False):
                if not narrow:
                    V_.memset(TMP[:, 3:4], 0.0).then_inc(sem("merged"), EC)
                if blocks == 2:
                    tokens_low(1, e, narrow)
                else:
                    V_.memset(TMP[:, 1:2], 0.0).then_inc(sem("x_lo_1"), 1)
                selection(e, True, narrow)
                if not last:
                    selection(e + 1, False)
                for kind, c in vector_order(blocks):
                    if kind == "split" and c > 1:
                        expert_low(e, c)
                    elif kind == "hidden":
                        if narrow:
                            dve.wait_ge(sem("low_rows"), EC * e + c + 1)
                            V_.tensor_tensor(PS[0:64, 1:4:2, :], PS[0:64, 1:4:2, :], MERGE,
                                             ALU.add).then_inc(sem("merged"), 1)
                        dve.wait_ge(sem("silu"), EC * e + c + 1)
                        h, b = by_block(HS, blocks), 2 + turn(blocks, c)
                        V_.tensor_tensor(h, h, PS[:, b:b + blocks, :], ALU.mult).then_inc(sem("hidden"), 1)
                    elif kind == "transposed":
                        dve.wait_ge(sem("ht_hi"), EC * e + c + 1)
                        b = hidden_bank(blocks)
                        if narrow:
                            V_.tensor_tensor(HTL[:, 0:512], PS[:, b, :], HTH[:, 0:512].bitcast(f32), ALU.subtract)
                            V_.tensor_tensor(halves(HTH, 512, 1), narrow_hidden(b + 1), halves(HTH, 512, 0).bitcast(f32),
                                             ALU.subtract).then_inc(sem("ht_lo"), 1)
                            continue
                        V_.tensor_tensor(by_block(HTL, blocks), PS[:, b:b + blocks, :],
                                         by_block(HTH, blocks).bitcast(f32), ALU.subtract).then_inc(sem("ht_lo"), 1)
                if not last:
                    tokens_low(0, e + 1)
                    for q in range(2):
                        expert_low(e + 1, q)
                for j in range(4):
                    dve.wait_ge(sem("scattered"), 4 * e + j + 1)
                    a = ACC[:, 2 * j:2 * j + 2, :].rearrange("p a b -> p (a b)")
                    V_.tensor_tensor(a, a, PS[:, 4 + j, :], ALU.add).then_inc(sem("acc_done"), 1)

            selection(0, False)
            for q in range(2):
                expert_low(0, q)
            tokens_low(0, 0)
            with dve.Fori(0, E - 1) as e:
                kind = dve.value_load(FLAGS[0:1, bass.ds(e, 1)], min_val=0, max_val=2)
                with dve.If(kind < 1):
                    expert(e, 1)
                with dve.If(kind == 1):
                    expert(e, 2, narrow=True)
                with dve.If(kind > 1):
                    expert(e, 2)
            kind = dve.value_load(FLAGS[0:1, E - 1:E], min_val=0, max_val=2)
            with dve.If(kind < 1):
                expert(E - 1, 1, last=True)
            with dve.If(kind == 1):
                expert(E - 1, 2, narrow=True, last=True)
            with dve.If(kind > 1):
                expert(E - 1, 2, last=True)
            dve.wait_ge(sem("acc_done"), 4 * E + 1)
            do(V_.tensor_tensor(SQ7, ACC, ACC, ALU.mult), "moe_squares")
            dve.wait_ge(sem("rooted"), count["rooted"] + 1)
            do(V_.reciprocal(RST[:, 0:256], PS[:, 0, 0:256]))
            residual(None, ACC, 1, 3, (1,), ready="out_ready")


def constants():
    out = np.zeros((128, CONST_W), np.float32)

    def put(name, a):
        out[:, CONST[name][0]:CONST[name][1]] = a

    i, j = np.arange(128)[:, None], np.arange(128)[None, :]
    same = i // CHUNK == j // CHUNK
    put("ident", i == j)
    put("ones", 1.0)
    put("tri_f", (same & (i <= j)) / TAU)
    put("tri_b", (same & (i >= j)) / TAU)
    put("before", i < j)
    rot = np.zeros((128, 128), np.float32)
    for m in range(128):
        if m % 64 < 32:
            rot[m + 32, m] = -1.0
        else:
            rot[m - 32, m] = 1.0
    put("rot", rot)
    n_freq = ROPE // 4
    tok = np.arange(T_LAT)
    freq = (np.float32(ROPE_BASE) ** (-np.arange(n_freq, dtype=np.float32) / np.float32(n_freq))).astype(np.float32)
    row, col = (tok // GRID_W).astype(np.float32), (tok % GRID_W).astype(np.float32)
    ang = np.concatenate([row[:, None] * freq, col[:, None] * freq], axis=-1).T
    put("cos", np.tile(np.cos(ang), (4, 1)))
    put("sin", np.tile(np.sin(ang), (4, 1)))
    masks = []
    for d in range(2):
        for m in LEVELS:
            lo, hi = i % (2 * m) < m, j % (2 * m) >= m
            up, dn = i % (2 * m) >= m, j % (2 * m) < m
            block = i // (2 * m) == j // (2 * m)
            masks.append(block & (lo & hi if d == 0 else up & dn))
    put("masks", np.concatenate(masks, 1))
    put("diag2", 2.0 * (i == j))
    put("iota", np.broadcast_to(np.arange(256)[None, :], (128, 256)))
    put("lower8", np.broadcast_to((np.arange(8)[None, :] < np.arange(8)[:, None]).reshape(1, 64), (128, 64)))
    return out


def kernel(**inputs):
    import concourse.bacc as _bacc
    from concourse import mybir as _mybir
    from concourse.bass_utils import run_bass_kernel_spmd as _run

    a = {k: np.asarray(v) for k, v in inputs.items()}
    uq = a["mla_w_uq"].reshape(1, Q_RANK, MLA_H, NOPE + ROPE)
    a["mla_w_uq"] = np.concatenate([uq[..., :NOPE].reshape(1, Q_RANK, -1), uq[..., NOPE:].reshape(1, Q_RANK, -1)], 2)
    by_tile = lambda v: v.reshape(-1, 128).T

    pieces = list(plan()[0])
    for e in range(E):
        for kind, c, _ in expert_order():
            for half in range(2):
                if kind == "d":
                    pieces.append(("moe_w_down", (0, e), 4 * c + 2 * half, 4 * c + 2 * half + 2, 0, D, None))
                else:
                    pieces.append((("moe_w_gate" if kind == "g" else "moe_w_up"), (0, e), 4 * half, 4 * half + 4,
                                   512 * c, 512 * c + 512, None))
    stream = np.zeros((len(pieces), 128, PIECE), np.float32)
    for n, (src, index, k0, k1, c0, c1, _) in enumerate(pieces):
        w = a[src][index][128 * k0:128 * k1, c0:c1].reshape(k1 - k0, 128, c1 - c0)
        stream[n, :, 0:(k1 - k0) * (c1 - c0)] = w.transpose(1, 0, 2).reshape(128, -1)

    param = np.zeros((128, PARAM_W), np.float32)

    def put(name, v, rows=128):
        param[0:rows, PARAM[name][0]:PARAM[name][1]] = v

    put("c", np.stack([by_tile(a["c_ctx"]), by_tile(a["c"][0])], 2).reshape(128, 16))
    for name in ("g_pre_mix", "g_post_mix", "g_pre_ffn", "g_post_ffn", "b_mod"):
        put(name, np.concatenate([by_tile(a[name][i]) for i in range(2)], 1))
    put("g_q", by_tile(a["mla_g_q"][0]))
    put("g_kv", by_tile(a["mla_g_kv"][0]))
    put("g_gla", by_tile(a["gla_g_out"][0]))
    put("g_diff", by_tile(a["diff_g_out"][0]))
    for name in ("lq1", "lk1", "lq2", "lk2"):
        put(name, np.broadcast_to(a["diff_" + name][0], (128, DIFF_D)))
    put("router", a["moe_w_router"][0].reshape(KT, 128, E).transpose(1, 0, 2).reshape(128, KT * E))
    put("w_gate", np.concatenate([a["gla_w_gate_f"][0], a["gla_w_gate_b"][0]], 1), rows=RANK)
    put("b_gate", np.broadcast_to(np.concatenate([a["gla_b_gate_f"][0], a["gla_b_gate_b"][0]]), (128, 512)))

    arrays = {"stream_dram": stream, "const_dram": constants(), "param_dram": param,
              "x_dram": np.ascontiguousarray(np.concatenate([a["ctx"][0].T, a["x"][0].T], 1))}
    nc = _bacc.Bacc("TRN2", target_bir_lowering=False, num_devices=1)
    args = [nc.dram_tensor(n, v.shape, _mybir.dt.float32, kind="ExternalInput").ap() for n, v in arrays.items()]
    args.append(nc.dram_tensor("out_dram", (D, T_LAT), _mybir.dt.float32, kind="ExternalOutput").ap())
    build(nc, *args)
    r = _run(nc, [arrays], core_ids=[0])
    return np.ascontiguousarray(r.results[0]["out_dram"].T)[None]
```
